# Optimizing a Trainium2 kernel written in Bass

```python
import math
import jax, jax.numpy as jnp
from jax import lax
import numpy as np

D_MODEL = 2048
BATCH = 1
SEQ = 256
DEPTH = 1

CHUNK = 64
Q_BLOCK = 128
SB_HEADS = 8
SB_HEAD_DIM = 128
SB_WIDTH = SB_HEADS * SB_HEAD_DIM
DA_HEADS = 8
DA_HEAD_DIM = 64
DA_V_DIM = 2 * DA_HEAD_DIM
DA_QK_WIDTH = DA_HEADS * 2 * DA_HEAD_DIM
DA_WIDTH = DA_HEADS * DA_V_DIM
N_BRANCHES = 2
IN_COLS = 3 * SB_WIDTH + 2 * DA_QK_WIDTH + DA_WIDTH + N_BRANCHES * D_MODEL
ROPE_THETA = 10000.0
N_GROUPS = 4
EXPERTS_PER_GROUP = 8
N_EXPERTS = N_GROUPS * EXPERTS_PER_GROUP
TOP_K_IN_GROUP = 2
D_EXPERT = D_MODEL // 4
MOE_BLOCK = 128
EPS = 1e-6

kernel_name = "hybrid_stickbreak_diffattn_hiermoe"

def rmsnorm(x, g):
    xf = x.astype(jnp.float32)
    y = xf * lax.rsqrt(jnp.mean(xf * xf, axis=-1, keepdims=True) + EPS)
    return (y * g.astype(jnp.float32)).astype(x.dtype)

def to_heads(t, n_heads, head_dim):
    b, s, _ = t.shape
    return t.reshape(b, s, n_heads, head_dim).transpose(0, 2, 1, 3)

def rope(x, pos):
    d = x.shape[-1]
    half = d // 2
    inv_freq = ROPE_THETA ** (-(jnp.arange(half, dtype=jnp.float32) * 2.0 / d))
    ang = pos.astype(jnp.float32)[:, None] * inv_freq[None, :]
    cos, sin = jnp.cos(ang), jnp.sin(ang)
    xf = x.astype(jnp.float32)
    x1, x2 = xf[..., :half], xf[..., half:]
    return jnp.concatenate([x1 * cos - x2 * sin, x2 * cos + x1 * sin], axis=-1).astype(x.dtype)

def stick_breaking_block(q, k, v, t0):
    qb, L, d = q.shape[2], k.shape[2], q.shape[3]
    z = jnp.einsum('bhqd,bhkd->bhqk', q, k).astype(jnp.float32) / math.sqrt(d)
    t = t0 + jnp.arange(qb)
    s = jnp.arange(L)
    mask = s[None, :] < t[:, None]
    log_1m = jnp.where(mask, jax.nn.log_sigmoid(-z), 0.0)
    suffix = lax.cumsum(log_1m, axis=3, reverse=True) - log_1m
    a = jnp.where(mask, jnp.exp(jax.nn.log_sigmoid(z) + suffix), 0.0)
    return jnp.einsum('bhqk,bhkd->bhqd', a.astype(v.dtype), v)

def diff_attn_block(q1, q2, k1, k2, v, t0, lam):
    qb, L, d = q1.shape[2], k1.shape[2], q1.shape[3]
    t = t0 + jnp.arange(qb)
    s = jnp.arange(L)
    mask = (s // CHUNK)[None, :] <= (t // CHUNK)[:, None]

    def probs(q, k):
        sc = jnp.einsum('bhqd,bhkd->bhqk', q, k).astype(jnp.float32) / math.sqrt(d)
        return jax.nn.softmax(jnp.where(mask, sc, -jnp.inf), axis=-1)

    attn = probs(q1, k1) - lam * probs(q2, k2)
    return jnp.einsum('bhqk,bhkd->bhqd', attn.astype(v.dtype), v)

def hierarchical_moe(h, w_group_router, w_expert_router, w_gate, w_up, w_down):
    b, s, d = h.shape
    n = b * s
    hf = h.reshape(n, d)
    g_logits = (hf @ w_group_router).astype(jnp.float32)
    g_prob = jax.nn.softmax(g_logits, axis=-1)
    grp = jnp.argmax(g_logits, axis=-1)
    p_grp = jnp.take_along_axis(g_prob, grp[:, None], axis=1)
    e_logits = (hf @ w_expert_router).astype(jnp.float32).reshape(n, N_GROUPS, EXPERTS_PER_GROUP)
    idx = jnp.broadcast_to(grp[:, None, None], (n, 1, EXPERTS_PER_GROUP))
    e_sel = jnp.take_along_axis(e_logits, idx, axis=1)[:, 0]
    top_val, top_idx = lax.top_k(e_sel, TOP_K_IN_GROUP)
    gate = p_grp * jax.nn.softmax(top_val, axis=-1)
    expert = grp[:, None] * EXPERTS_PER_GROUP + top_idx

    a_total = n * TOP_K_IN_GROUP
    e_flat = expert.reshape(a_total)
    tok_flat = jnp.repeat(jnp.arange(n, dtype=jnp.int32), TOP_K_IN_GROUP)
    w_flat = gate.reshape(a_total)
    order = jnp.argsort(e_flat)
    e_sorted, tok_sorted, w_sorted = e_flat[order], tok_flat[order], w_flat[order]
    counts = jnp.zeros((N_EXPERTS,), jnp.int32).at[e_flat].add(1)
    padded = (counts + MOE_BLOCK - 1) // MOE_BLOCK * MOE_BLOCK
    starts = jnp.cumsum(counts) - counts
    pad_ends = jnp.cumsum(padded)
    pad_starts = pad_ends - padded
    dest = pad_starts[e_sorted] + jnp.arange(a_total, dtype=jnp.int32) - starts[e_sorted]
    n_blocks = -(-a_total // MOE_BLOCK) + N_EXPERTS
    p_rows = n_blocks * MOE_BLOCK
    buf_tok = jnp.full((p_rows,), n, jnp.int32).at[dest].set(tok_sorted)
    buf_w = jnp.zeros((p_rows,), jnp.float32).at[dest].set(w_sorted)
    block_expert = jnp.minimum(
        jnp.searchsorted(pad_ends, jnp.arange(n_blocks, dtype=jnp.int32) * MOE_BLOCK, side='right'),
        N_EXPERTS - 1)
    h_pad = jnp.concatenate([hf, jnp.zeros((1, d), hf.dtype)], axis=0)
    xb = h_pad[buf_tok].reshape(n_blocks, MOE_BLOCK, d)

    def expert_block(args):
        xblk, e = args
        return (jax.nn.silu(xblk @ w_gate[e]) * (xblk @ w_up[e])) @ w_down[e]

    yb = lax.map(expert_block, (xb, block_expert)).reshape(p_rows, d)
    y = jnp.zeros((n + 1, d), h.dtype).at[buf_tok].add(yb * buf_w[:, None].astype(h.dtype))
    return y[:n].reshape(b, s, d)

def setup_inputs(seed: int = 0) -> dict:
    key = jax.random.key(seed)
    ks = jax.random.split(key, 20)
    f32 = jnp.float32

    def nrm(k, shape, scale):
        return jax.random.normal(k, shape, f32) * scale

    def gain(k, shape):
        return 1.0 + 0.02 * jax.random.normal(k, shape, f32)

    return {
        "x": nrm(ks[0], (BATCH, SEQ, D_MODEL), 1.0),
        "mix_norm_g": gain(ks[1], (DEPTH, D_MODEL)),
        "w_in": nrm(ks[2], (DEPTH, D_MODEL, IN_COLS), D_MODEL ** -0.5),
        "lambda_q1": nrm(ks[3], (DEPTH, DA_HEAD_DIM), 0.1),
        "lambda_k1": nrm(ks[4], (DEPTH, DA_HEAD_DIM), 0.1),
        "lambda_q2": nrm(ks[5], (DEPTH, DA_HEAD_DIM), 0.1),
        "lambda_k2": nrm(ks[6], (DEPTH, DA_HEAD_DIM), 0.1),
        "diff_subnorm_g": gain(ks[7], (DEPTH, DA_V_DIM)),
        "w_branch_sb": nrm(ks[8], (DEPTH, SB_WIDTH, D_MODEL), SB_WIDTH ** -0.5),
        "w_branch_diff": nrm(ks[9], (DEPTH, DA_WIDTH, D_MODEL), DA_WIDTH ** -0.5),
        "w_out": nrm(ks[10], (DEPTH, D_MODEL, D_MODEL), D_MODEL ** -0.5),
        "ffn_norm_g": gain(ks[11], (DEPTH, D_MODEL)),
        "w_group_router": nrm(ks[12], (DEPTH, D_MODEL, N_GROUPS), D_MODEL ** -0.5),
        "w_expert_router": nrm(ks[13], (DEPTH, D_MODEL, N_EXPERTS), D_MODEL ** -0.5),
        "w_gate": nrm(ks[14], (DEPTH, N_EXPERTS, D_MODEL, D_EXPERT), D_MODEL ** -0.5),
        "w_up": nrm(ks[15], (DEPTH, N_EXPERTS, D_MODEL, D_EXPERT), D_MODEL ** -0.5),
        "w_down": nrm(ks[16], (DEPTH, N_EXPERTS, D_EXPERT, D_MODEL), D_EXPERT ** -0.5),
        "final_norm_g": gain(ks[17], (D_MODEL,)),
    }

def reference(x, mix_norm_g, w_in, lambda_q1, lambda_k1, lambda_q2, lambda_k2, diff_subnorm_g,
              w_branch_sb, w_branch_diff, w_out, ffn_norm_g, w_group_router, w_expert_router,
              w_gate, w_up, w_down, final_norm_g):
    b, s, _ = x.shape
    pos = jnp.arange(s, dtype=jnp.int32)
    split_at = list(np.cumsum([SB_WIDTH, SB_WIDTH, SB_WIDTH, DA_QK_WIDTH, DA_QK_WIDTH, DA_WIDTH, D_MODEL]))
    for l in range(DEPTH):
        h = rmsnorm(x, mix_norm_g[l])
        proj = h @ w_in[l]
        q_sb, k_sb, v_sb, q_da, k_da, v_da, g_sb, g_da = jnp.split(proj, split_at, axis=-1)
        q_sb = to_heads(q_sb, SB_HEADS, SB_HEAD_DIM)
        k_sb = to_heads(k_sb, SB_HEADS, SB_HEAD_DIM)
        v_sb = to_heads(v_sb, SB_HEADS, SB_HEAD_DIM)
        q_da = to_heads(q_da, DA_HEADS, 2 * DA_HEAD_DIM)
        k_da = to_heads(k_da, DA_HEADS, 2 * DA_HEAD_DIM)
        v_da = to_heads(v_da, DA_HEADS, DA_V_DIM)
        q1 = rope(q_da[..., :DA_HEAD_DIM], pos)
        q2 = rope(q_da[..., DA_HEAD_DIM:], pos)
        k1 = rope(k_da[..., :DA_HEAD_DIM], pos)
        k2 = rope(k_da[..., DA_HEAD_DIM:], pos)
        lam_init = 0.8 - 0.6 * math.exp(-0.3 * l)
        lam = (jnp.exp(jnp.sum(lambda_q1[l].astype(jnp.float32) * lambda_k1[l].astype(jnp.float32)))
               - jnp.exp(jnp.sum(lambda_q2[l].astype(jnp.float32) * lambda_k2[l].astype(jnp.float32)))
               + lam_init)

        sb_blocks, da_blocks = [], []
        for i in range(s // Q_BLOCK):
            t0, t1 = i * Q_BLOCK, (i + 1) * Q_BLOCK
            sb_blocks.append(stick_breaking_block(q_sb[:, :, t0:t1], k_sb[:, :, :t1], v_sb[:, :, :t1], t0))
            da_blocks.append(diff_attn_block(q1[:, :, t0:t1], q2[:, :, t0:t1], k1[:, :, :t1], k2[:, :, :t1],
                                             v_da[:, :, :t1], t0, lam))
        o_sb = jnp.concatenate(sb_blocks, axis=2).transpose(0, 2, 1, 3).reshape(b, s, SB_WIDTH)
        o_da = rmsnorm(jnp.concatenate(da_blocks, axis=2), diff_subnorm_g[l]) * (1.0 - lam_init)
        o_da = o_da.transpose(0, 2, 1, 3).reshape(b, s, DA_WIDTH)

        merged = (jax.nn.sigmoid(g_sb) * (o_sb @ w_branch_sb[l])
                  + jax.nn.sigmoid(g_da) * (o_da @ w_branch_diff[l]))
        x = x + merged @ w_out[l]

        h2 = rmsnorm(x, ffn_norm_g[l])
        x = x + hierarchical_moe(h2, w_group_router[l], w_expert_router[l], w_gate[l], w_up[l], w_down[l])
    return rmsnorm(x, final_norm_g)


_drawn_inputs = setup_inputs


def setup_inputs(seed=0):
    import zlib

    import numpy as np

    out = dict(_drawn_inputs(seed))
    spreads = {}
    factors = {'lambda_q1': 2.746, 'lambda_q2': 8.0, 'ffn_norm_g': 3.644, 'final_norm_g': 2.828}
    for name, (base, spread) in spreads.items():
        noise = np.random.default_rng([zlib.crc32(name.encode()), seed]).standard_normal(out[name].shape)
        drawn = base * np.exp(spread * noise) if base else spread * noise
        out[name] = __import__('jax').numpy.asarray(drawn.astype(out[name].dtype))
    for name, factor in factors.items():
        out[name] = (out[name] * factor).astype(out[name].dtype)
    return out
```

```python
from contextlib import ExitStack

import numpy as np

import concourse.bass as bass
from concourse import mybir

F32 = mybir.dt.float32
BF16 = mybir.dt.bfloat16
U32 = mybir.dt.uint32
I32 = mybir.dt.int32
ALU = mybir.AluOpType
ACT = mybir.ActivationFunctionType
AX = mybir.AxisListType

P = 128
D = 2048
T = 256
TB = T // P
KC = D // P
H = 8
W = H * P
HD = 64
CHUNK = 64
G = 4
EPG = 8
E = G * EPG
F = D // 4
SLOTS = 32
QUAD = P // SLOTS
NQ = E // QUAD
EPS = 1e-6
LAM_INIT = 0.2
NEG = -1e30
SLOT = 4096
DRING = 4
MRING = 6
TILES_A = 6
PROJ_CHUNKS = 4 * TILES_A
GATE_CHUNKS = 2 * H
BRANCH_CHUNKS = 8
OUT_CHUNKS = 8
DENSE = PROJ_CHUNKS + GATE_CHUNKS + BRANCH_CHUNKS + OUT_CHUNKS
QCH = 24
R_QSB, R_KSB, R_VSB, R_QDA, R_KDA, R_VDA = range(6)

C_ID, C_TRI, C_ONE, C_PREV, C_MSB, C_MDA, C_COS, C_SIN, C_IOTA, C_THR = (
    0, 128, 256, 384, 512, 640, 768, 896, 1024, 1056)
C_N = 1064


def shape_constants():
    c = np.zeros((P, C_N), np.float32)
    i = np.arange(P)
    c[:, C_ID:C_ID + P] = i[:, None] == i[None, :]
    c[:, C_TRI:C_TRI + P] = i[:, None] >= i[None, :]
    c[:, C_ONE:C_ONE + P] = 1.0
    c[:, C_PREV:C_PREV + P] = i[:, None] < i[None, :]
    c[:, C_MSB:C_MSB + P] = np.where(i[:, None] >= i[None, :], NEG, 0.0)
    c[:, C_MDA:C_MDA + P] = np.where(i[None, :] // CHUNK > i[:, None] // CHUNK, NEG, 0.0)
    half = HD // 2
    inv = np.float32(10000.0) ** (-(np.arange(half, dtype=np.float32) * np.float32(2.0) / np.float32(HD)))
    ang = (np.arange(T, dtype=np.float32)[:, None] * inv.astype(np.float32)[None, :]).astype(np.float64)
    for m in range(TB):
        for mp in range(2):
            at = (m * 2 + mp) * half
            c[:, C_COS + at:C_COS + at + half] = np.cos(ang[m * P:(m + 1) * P])
            c[:, C_SIN + at:C_SIN + at + half] = np.sin(ang[m * P:(m + 1) * P])
    c[:, C_IOTA:C_IOTA + E] = np.arange(E)
    c[:, C_THR:C_THR + 8] = np.arange(1, 9) * SLOTS
    return c


class Chain:

    def __init__(self, eng, sem):
        self.eng, self.sem, self.n, self.off = eng, sem, 0, 0

    def link(self, ins):
        self.n += 1
        ins.then_inc(self.sem, 1)
        self.eng.wait_ge(self.sem, self.off + self.n)


def build(nc, x, mix_g, w_in, lq1, lk1, lq2, lk2, sub_g, w_sb, w_da, w_out, ffn_g, w_gr, w_er,
          w_gate, w_up, w_down, fin_g, consts, out):
    ctx = ExitStack()

    def sb(name, shape, dt=F32):
        return ctx.enter_context(nc.sbuf_tensor(name, shape, dt))

    def sem(name):
        return ctx.enter_context(nc.semaphore(name))

    cst = sb("cst", [P, C_N])
    gain = sb("gain", [P, D])
    wr = sb("wr", [P, KC, G + E])
    wr_raw = sb("wr_raw", [P, KC * G])
    ident16 = sb("ident16", [P, P], BF16)
    mask16 = sb("mask16", [P, 2, P], BF16)
    cell = sb("cell", [P, 64])
    arena = sb("arena", [P, 6 * SLOT + SLOT + 6 * 2048 + 6400])
    ps = ctx.enter_context(nc.psum_tensor("ps", [P, 8, 512], F32))

    ident, tri, ones, prev = (cst[:, a:a + P] for a in (C_ID, C_TRI, C_ONE, C_PREV))
    cosH = cst[:, C_COS:C_COS + P].rearrange("p (s f) -> p s f", s=4)
    sinH = cst[:, C_SIN:C_SIN + P].rearrange("p (s f) -> p s f", s=4)

    def at(base, n):
        return arena[:, base:base + n]

    ring = [at(s * SLOT, SLOT) for s in range(MRING)]
    B_GATE = 4 * SLOT
    gates = at(B_GATE, 2 * SLOT).rearrange("p (g m n) -> p g m n", g=8, m=TB)
    x0 = at(B_GATE, SLOT).rearrange("p (m d) -> p m d", m=TB)
    h0 = at(B_GATE + SLOT, SLOT).rearrange("p (m d) -> p m d", m=TB)
    rope_u = at(B_GATE, SLOT).rearrange("p (b s f) -> p b s f", b=16, s=4)
    rope_v = at(B_GATE + SLOT, SLOT).rearrange("p (b s f) -> p b s f", b=16, s=4)
    B_T = 6 * SLOT
    hT = at(B_T, SLOT).rearrange("p (c t) -> p c t", c=KC)
    yS = at(B_T, D)
    B_P = 7 * SLOT
    proj = at(B_P, 6 * 2048).rearrange("p (r h m d) -> p r h m d", r=6, h=H, m=TB)
    merged = at(B_P + 2048, SLOT).rearrange("p (m n) -> p m n", m=TB)
    h2 = at(B_P + 2048, SLOT).rearrange("p (m c d) -> p m c d", m=TB, c=KC)
    xr = at(B_P + 4 * 2048, SLOT).rearrange("p (m d) -> p m d", m=TB)
    oT_sb = at(B_P, 2048).rearrange("p (h t) -> p h t", h=H)
    oT_da = at(B_P + 3 * 2048, 2048).rearrange("p (h t) -> p h t", h=H)
    h2T = [at(B_P + b, 2048).rearrange("p (c t) -> p c t", c=8) for b in (0, 3 * 2048)]
    xgT = at(B_P, 2048).rearrange("p (c s) -> p c s", c=KC)
    B_X = B_P + 6 * 2048
    used = [B_X]

    def temp(n):
        used[0] += n
        assert used[0] <= B_X + 6400
        return at(used[0] - n, n)

    lamv = temp(256).rearrange("p (v d) -> p v d", v=4)
    gsub = temp(P)
    qk_sb = temp(512).rearrange("p (w m d) -> p w m d", w=2, m=TB)
    qk_da = temp(512).rearrange("p (w m d) -> p w m d", w=2, m=TB)
    v_sb = temp(256).rearrange("p (m d) -> p m d", m=TB)
    qkT_sb = temp(512).rearrange("p (w t) -> p w t", w=2)
    qkT_da = temp(512).rearrange("p (w t) -> p w t", w=2)
    zS, eS, lS, aT, attn, attnT = (temp(384) for _ in range(6))
    pS = temp(768).rearrange("p (a k) -> p a k", a=2)
    oS = temp(256).rearrange("p (m d) -> p m d", m=TB)
    oN = temp(256).rearrange("p (m d) -> p m d", m=TB)
    sq = temp(P)
    used[0] = B_X
    part = temp(1024)
    used[0] = B_X
    lg = temp(TB * (G + 4 + E)).rearrange("p (m e) -> p m e", m=TB)
    gm8, gi8f, ev8, ei8f = (temp(16).rearrange("p (m e) -> p m e", m=TB) for _ in range(4))
    gi8, ei8 = (temp(16).bitcast(U32).rearrange("p (m e) -> p m e", m=TB) for _ in range(2))
    goh = temp(8).rearrange("p (m g) -> p m g", m=TB)
    gexp = temp(8).rearrange("p (m g) -> p m g", m=TB)
    picked = temp(TB * E).rearrange("p (m e) -> p m e", m=TB)
    esel = temp(16).rearrange("p (m e) -> p m e", m=TB)
    oh1, oh2, took, share, rank = (temp(TB * E).rearrange("p (m e) -> p m e", m=TB) for _ in range(5))
    rt = temp(64)
    count8 = temp(8)
    steps_i = temp(2).bitcast(I32)
    selE = temp(TB * P).rearrange("p (m e s) -> p m e s", m=TB, e=QUAD)
    selW = temp(TB * P).rearrange("p (m e s) -> p m e s", m=TB, e=QUAD)
    selWT = temp(T)
    gE, hS, hT4 = (temp(512) for _ in range(3))
    outS = at(B_T, SLOT).rearrange("p (m d) -> p m d", m=TB)

    one_c = cell[:, 0:1]
    ss, rs = cell[:, 2:4], cell[:, 4:6]
    neglam = cell[:, 6:7]
    lam4 = cell[:, 8:10]
    lamE = cell[:, 10:12]
    mx, nmx, sm, rsm = cell[:, 12:16], cell[:, 16:20], cell[:, 20:24], cell[:, 24:28]
    oss, ors = cell[:, 28:30], cell[:, 30:32]
    rsn = cell[:, 32:34]
    rv, ry, rq = cell[:, 34:36], cell[:, 36:38], cell[:, 38:40]

    s_x, s_cst, s_gain, s_small, s_xr, s_store = (sem(n) for n in (
        "x_landed", "consts_landed", "gain_landed", "small_landed", "xr_landed", "stored"))
    landed = [sem(f"slot{s}_landed") for s in range(MRING)]
    s_used = sem("chunks_used")
    s_dve, s_act = sem("dve_chain"), sem("act_chain")
    s_set = sem("cells_set")
    s_ssq = sem("squares_summed")
    s_h = sem("h_ready")
    s_turned = sem("h_turned")
    s_fd, s_fa = sem("half_free_dve"), sem("half_free_act")
    s_roped = sem("roped")
    s_v, s_y0 = sem("mean_square_ready"), sem("root_estimated")
    s_hsb, s_hda, s_hv = sem("head_sb_copied"), sem("head_da_copied"), sem("head_v_copied")
    s_tsb, s_tda = sem("sb_qk_turned"), sem("da_qk_turned")
    s_kd, s_ka = sem("qkT_by_dve"), sem("qkT_by_act")
    s_z, s_sc = sem("z_done"), sem("da_scores_done")
    s_l, s_L = sem("log_part_ready"), sem("softplus_ready")
    s_zc, s_c, s_a = sem("z_less_sum_ready"), sem("sums_done"), sem("a_ready")
    s_mx, s_p = sem("row_max_ready"), sem("probs_ready")
    s_at, s_att, s_atT = sem("attn_ready"), sem("attn_turned"), sem("attnT_ready")
    s_osb, s_oda = sem("sb_o_done"), sem("da_o_done")
    s_ost, s_oS, s_oN, s_oT, s_odt = (sem(n) for n in (
        "oT_sb_stored", "da_o_copied", "da_o_normed", "da_o_turned", "oT_da_stored"))
    s_ge, s_sig, s_gd = sem("gate_tile_copied"), sem("gates_squashed"), sem("gates_read")
    s_lam = sem("lambda_sums")
    s_lamE = sem("lambda_exps")
    s_At, s_Bt = sem("branch_a_read"), sem("branch_b_read")
    s_mT, s_md, s_ma = sem("merged_turned"), sem("mT_by_dve"), sem("mT_by_act")
    s_x2, s_sq2, s_h2 = sem("x2_ready"), sem("x2_squares"), sem("h2_ready")
    s_h2t, s_2d, s_2a = sem("h2_turned"), sem("h2T_by_dve"), sem("h2T_by_act")
    s_log, s_gm, s_gx = sem("logits_done"), sem("group_max_ready"), sem("group_exp_ready")
    s_ex = sem("pair_exp_ready")
    s_dd = sem("pair_gap_ready")
    s_took, s_rank, s_steps = sem("took_ready"), sem("ranks_done"), sem("steps_ready")
    s_sel, s_gath, s_xd, s_xa = sem("sel_ready"), sem("gathered"), sem("xgT_by_dve"), sem("xgT_by_act")
    s_swt, s_sw = sem("shares_turned"), sem("sharesT_ready")
    s_gu, s_e, s_hS = sem("gate_up_done"), sem("silu_ready"), sem("hidden_ready")
    s_ht, s_hT = sem("hidden_turned"), sem("hiddenT_ready")
    s_yd, s_ya = sem("y_by_dve"), sem("y_by_act")
    s_comb, s_add = sem("combined"), sem("added")
    s_fss, s_out = sem("final_squares"), sem("out_rows_ready")

    w_in_c = w_in[0].rearrange("(c k p) n -> c p k n", c=4, p=P)
    w_gt_c = w_in[0].rearrange("(c k p) n -> c p k n", c=2, p=P)
    w_br_c = [w[0].rearrange("(c k p) n -> c p k n", c=2, p=P) for w in (w_sb, w_da)]
    w_out_c = w_out[0].rearrange("(c k p) n -> c p k n", c=4, p=P)
    w_gate_q = w_gate[0].rearrange("(q e) (p c) f -> q p e c f", e=QUAD, c=KC)
    w_up_q = w_up[0].rearrange("(q e) (p c) f -> q p e c f", e=QUAD, c=KC)
    w_down_q = w_down[0].rearrange("(q e) (c p) n -> q p e c n", e=QUAD, p=P)
    x_rows = x[0].rearrange("(m p) d -> p m d", p=P)
    out_rows = out[0].rearrange("(m p) d -> p m d", p=P)

    def mslot(j):
        return (j + DRING) % MRING

    def mlanded(eng, j, it):
        s = mslot(j)
        base = 16 * (DENSE // DRING) if s < DRING else 0
        eng.wait_ge(landed[s], it * (16 * QCH // MRING) + base + 16 * (j // MRING + 1))

    block = ctx.enter_context(nc.Block())

    @block.sync
    def _(sp):
        sp.dma_start(x0, x_rows).then_inc(s_x, 16)
        sp.dma_start(cst[:], consts).then_inc(s_cst, 16)
        for c in range(4):
            sp.dma_start(ring[c].rearrange("p (k n) -> p k n", k=4),
                         w_in_c[c, :, :, 0:1024]).then_inc(landed[c], 16)
        with sp.Fori(1, TILES_A) as t:
            for c in range(4):
                sp.wait_ge(s_used, 4 * t + (c - 3))
                sp.dma_start(ring[c].rearrange("p (k n) -> p k n", k=4),
                             w_in_c[c, :, :, bass.ds(t * 1024, 1024)]).then_inc(landed[c], 16)
        with sp.Fori(0, H // 2) as i:
            for c in range(4):
                sp.wait_ge(s_used, 4 * i + (PROJ_CHUNKS + c - 3))
                sp.dma_start(ring[c].rearrange("p (k n) -> p k n", k=8),
                             w_gt_c[c % 2, :, :, bass.ds(i * 1024 + (6 * 1024 + 512 * (c // 2)), 512)]
                             ).then_inc(landed[c], 16)
        with sp.Fori(0, 2) as t:
            for c in range(4):
                sp.wait_ge(s_used, 4 * t + (PROJ_CHUNKS + GATE_CHUNKS + c - 3))
                sp.dma_start(ring[c].rearrange("p (k n) -> p k n", k=4),
                             w_br_c[c // 2][c % 2, :, :, bass.ds(t * 1024, 1024)]).then_inc(landed[c], 16)
        with sp.Fori(0, 2) as t:
            for c in range(4):
                sp.wait_ge(s_used, 4 * t + (DENSE - OUT_CHUNKS + c - 3))
                sp.dma_start(ring[c].rearrange("p (k n) -> p k n", k=4),
                             w_out_c[c, :, :, bass.ds(t * 1024, 1024)]).then_inc(landed[c], 16)
        sp.wait_ge(s_gd, 1)

        def load_quad(it, q):
            for j in range(QCH):
                sp.wait_ge(s_used, it * QCH + (DENSE + j - MRING + 1))
                dst = ring[mslot(j)].rearrange("p (e n) -> p e n", e=QUAD)
                if j < 16:
                    w, kp = (w_gate_q, w_up_q)[j % 2], j // 2
                    src = w[bass.ds(q, 1), :, :, 2 * kp:2 * kp + 2, :].rearrange("q p e c f -> p (q e) (c f)")
                else:
                    nh, c = (j - 16) // 4, (j - 16) % 4
                    src = w_down_q[bass.ds(q, 1), :, :, c, nh * 1024:nh * 1024 + 1024].rearrange(
                        "q p e n -> p (q e) n")
                sp.dma_start(dst, src).then_inc(landed[mslot(j)], 16)

        with sp.Fori(0, NQ - 1) as it:
            load_quad(it, it)
        sp.wait_ge(s_steps, 1)
        n = sp.value_load(steps_i[0:1, 0:1], min_val=NQ, max_val=NQ * (T // SLOTS))
        with sp.Fori(NQ - 1, n) as it:
            load_quad(it, it % NQ)
        for m in range(TB):
            sp.wait_ge(s_out, m + 1)
            sp.dma_start(out_rows[:, m, :], outS[:, m, :]).then_inc(s_store, 16)
        sp.wait_ge(s_store, 16 * TB)

    @block.gpsimd
    def _(pool):
        pool.dma_start(gain[:], mix_g[0:1, :].to_broadcast([P, D])).then_inc(s_gain, 16)
        for v, lv in enumerate((lq1, lk1, lq2, lk2)):
            pool.dma_start(lamv[:, v, :], lv[0:1, :].to_broadcast([P, HD])).then_inc(s_small, 16)
        pool.dma_start(gsub, sub_g[0:1, :].to_broadcast([P, P])).then_inc(s_small, 16)
        pool.dma_start(wr_raw[:], w_gr[0].rearrange("(p c) g -> p (c g)", c=KC)).then_inc(s_small, 16)
        pool.dma_start(wr[:, :, G:], w_er[0].rearrange("(p c) g -> p c g", c=KC)).then_inc(s_small, 16)
        pool.wait_ge(s_small, 16 * 7)
        pool.tensor_copy(wr[:, :, 0:G], wr_raw[:].rearrange("p (c g) -> p c g", g=G)).then_inc(s_set, 1)
        pool.wait_ge(s_fd, 2 + TILES_A)
        pool.wait_ge(s_fa, 2 + TILES_A)
        pool.wait_ge(s_roped, 1)
        with pool.Fori(0, H) as h:
            pool.wait_ge(s_tsb, h + 1)
            pool.tensor_copy(qk_sb.rearrange("p w m d -> p w (m d)"),
                             proj[:, R_QSB:R_QSB + 2, bass.ds(h, 1), :, :].rearrange(
                                 "p w h m d -> p w (h m d)")).then_inc(s_hsb, 1)
            pool.wait_ge(s_tda, h + 1)
            pool.tensor_copy(qk_da.rearrange("p w m d -> p w (m d)"),
                             proj[:, R_QDA:R_QDA + 2, bass.ds(h, 1), :, :].rearrange(
                                 "p w h m d -> p w (h m d)")).then_inc(s_hda, 1)
            pool.wait_ge(s_osb, h + 1)
            pool.tensor_copy(v_sb.rearrange("p m d -> p (m d)"),
                             proj[:, R_VSB, bass.ds(h, 1), :, :].rearrange(
                                 "p h m d -> p (h m d)")).then_inc(s_hv, 1)
        pool.wait_ge(s_oda, H)
        pool.wait_ge(s_hda, H)
        pool.dma_start(xr, x_rows).then_inc(s_xr, 16)
        pool.wait_ge(s_h, 2)
        pool.dma_start(gain[:], ffn_g[0:1, :].to_broadcast([P, D])).then_inc(s_gain, 16)
        pool.wait_ge(s_h2, 2)
        pool.dma_start(gain[:], fin_g.rearrange("(a d) -> a d", a=1).to_broadcast([P, D])).then_inc(s_gain, 16)

    @block.tensor
    def _(pe):
        for s in (s_tsb, s_tda, s_osb):
            pe.sem_inc(s, 1)
        pe.wait_ge(s_cst, 16)
        pe.wait_ge(s_h, 2)
        for half in range(2):
            for j in range(4 * half, 4 * half + 4):
                for k in range(2):
                    for m in range(TB):
                        c = 2 * j + k
                        mm = pe.transpose(ps[:, j, (2 * k + m) * P:(2 * k + m + 1) * P],
                                          h0[:, m, c * P:(c + 1) * P], ident)
            mm.then_inc(s_turned, 1)
        pe.wait_ge(s_fd, 2)
        pe.wait_ge(s_fa, 2)

        def wide_tile(bank, lhs, turn):
            for c in range(4):
                pe.wait_ge(landed[c], turn)
                for k in range(4):
                    for m in range(TB):
                        for n in range(2):
                            mm = pe.matmul(ps[:, bank + 2 * m + n, :], lhs[:, 4 * c + k, m * P:(m + 1) * P],
                                           ring[c][:, k * 1024 + n * 512:k * 1024 + n * 512 + 512],
                                           start=(c == 0 and k == 0), stop=(c == 3 and k == 3))
                mm.then_inc(s_used, 1)
            return mm

        with pe.Fori(0, TILES_A // 2) as i:
            for par in range(2):
                pe.wait_ge(s_fd, 2 * i + (par + 1))
                pe.wait_ge(s_fa, 2 * i + (par + 1))
                wide_tile(4 * par, hT, i * 32 + 16 * (par + 1))
        pe.wait_ge(s_fd, 2 + TILES_A)
        pe.wait_ge(s_fa, 2 + TILES_A)
        pe.wait_ge(s_set, 2)

        def head(h, slots, turn):
            def gate_part(g):
                if g % 2 == 0:
                    pe.wait_ge(landed[slots[g // 2]], turn)
                for k in range(4):
                    for m in range(TB):
                        kc = 4 * g + k
                        a = (kc % 8) * 512
                        mm = pe.matmul(ps[:, m, :], hT[:, kc, m * P:(m + 1) * P],
                                       ring[slots[g // 2]][:, a:a + 512], start=(kc == 0), stop=(kc == KC - 1))
                if g % 2 == 1:
                    mm.then_inc(s_used, 1)

            pe.wait_ge(s_hsb, h + 1)
            pe.wait_ge(s_ost, h + 1)
            for w in range(2):
                for m in range(TB):
                    mm = pe.transpose(ps[:, 2, (2 * w + m) * P:(2 * w + m + 1) * P], qk_sb[:, w, m, :], ident)
            mm.then_inc(s_tsb, 1)
            pe.wait_ge(s_hda, h + 1)
            pe.wait_ge(s_odt, h + 1)
            for w in range(2):
                for m in range(TB):
                    mm = pe.transpose(ps[:, 3, (2 * w + m) * P:(2 * w + m + 1) * P], qk_da[:, w, m, :], ident)
            mm.then_inc(s_tda, 1)
            pe.wait_ge(s_ge, h + 1)
            gate_part(0)
            pe.wait_ge(s_kd, h + 1)
            pe.wait_ge(s_ka, h + 1)
            pe.matmul(ps[:, 4, 0:256], qkT_sb[:, 1, 0:P], qkT_sb[:, 0, :], start=True, stop=True)
            pe.matmul(ps[:, 4, 0:128], ident16[:], mask16[:, 0, :], start=False, stop=True,
                      skip_group_check=True)
            pe.matmul(ps[:, 4, 256:384], qkT_sb[:, 1, P:T], qkT_sb[:, 0, P:T], start=True, stop=True,
                      skip_group_check=True)
            pe.matmul(ps[:, 4, 256:384], ident16[:], mask16[:, 0, :], start=False, stop=True,
                      skip_group_check=True).then_inc(s_z, 1)
            for mp in range(2):
                r = slice(HD * mp, HD * mp + HD)
                pe.matmul(ps[:, 5 + mp, 0:128], qkT_da[r, 0, 0:P], qkT_da[r, 1, 0:P], start=True, stop=True)
                pe.matmul(ps[:, 5 + mp, 0:128], ident16[:], mask16[:, 1, :], start=False, stop=True,
                          skip_group_check=True)
                pe.matmul(ps[:, 5 + mp, 128:384], qkT_da[r, 0, P:T], qkT_da[r, 1, :], start=True, stop=True,
                          skip_group_check=True)
                mm = pe.matmul(ps[:, 5 + mp, 256:384], ident16[:], mask16[:, 1, :], start=False, stop=True,
                               skip_group_check=True)
            mm.then_inc(s_sc, 1)
            gate_part(1)
            pe.wait_ge(s_L, h + 1)
            pe.matmul(ps[:, 7, 0:256], tri, eS[:, 0:256], start=True, stop=True)
            pe.matmul(ps[:, 7, 128:256], ones, eS[:, 256:384], start=False, stop=True, skip_group_check=True)
            pe.matmul(ps[:, 7, 256:384], tri, eS[:, 256:384], start=True, stop=True,
                      skip_group_check=True).then_inc(s_c, 1)
            pe.wait_ge(s_at, h + 1)
            for b in range(3):
                mm = pe.transpose(ps[:, 3, b * P:(b + 1) * P], attn[:, b * P:(b + 1) * P], ident)
            mm.then_inc(s_att, 1)
            gate_part(2)
            pe.wait_ge(s_hv, h + 1)
            pe.wait_ge(s_a, h + 1)
            pe.matmul(ps[:, 2, 0:256], v_sb[:, 0, :], aT[:, 0:256], start=True, stop=True)
            pe.matmul(ps[:, 2, 128:256], v_sb[:, 1, :], aT[:, 256:384], start=False, stop=True,
                      skip_group_check=True).then_inc(s_osb, 1)
            pe.wait_ge(s_atT, h + 1)

            def v_da(m):
                return proj[:, R_VDA, bass.ds(h, 1), m, :].rearrange("p h d -> p (h d)")

            pe.matmul(ps[:, 3, 0:128], attnT[:, 0:P], v_da(0), start=True, stop=True)
            pe.matmul(ps[:, 3, 128:256], attnT[:, P:2 * P], v_da(0), start=True, stop=True,
                      skip_group_check=True)
            pe.matmul(ps[:, 3, 128:256], attnT[:, 2 * P:3 * P], v_da(1), start=False, stop=True,
                      skip_group_check=True).then_inc(s_oda, 1)
            gate_part(3)
            pe.wait_ge(s_oN, h + 1)
            for m in range(TB):
                mm = pe.transpose(ps[:, 3, (2 + m) * P:(3 + m) * P], oN[:, m, :], ident)
            mm.then_inc(s_oT, 1)

        with pe.Fori(0, H // 2) as i:
            head(2 * i, (0, 1), i * 16 + 16 * (TILES_A + 1))
            head(2 * i + 1, (2, 3), i * 16 + 16 * (TILES_A + 1))
        pe.wait_ge(s_ge, H + 1)
        pe.wait_ge(s_ost, H + 1)
        pe.wait_ge(s_odt, H + 1)
        with pe.Fori(0, 2) as t:
            for br, (lhs, taken) in enumerate(((oT_sb, s_At), (oT_da, s_Bt))):
                pe.wait_ge(taken, t + 1)
                for c in range(2):
                    slot = 2 * br + c
                    pe.wait_ge(landed[slot], t * 16 + 16 * (TILES_A + H // 2 + 1))
                    for k in range(4):
                        for m in range(TB):
                            for n in range(2):
                                a = k * 1024 + n * 512
                                mm = pe.matmul(ps[:, 4 * br + 2 * m + n, :],
                                               lhs[:, 4 * c + k, m * P:(m + 1) * P], ring[slot][:, a:a + 512],
                                               start=(c == 0 and k == 0), stop=(c == 1 and k == 3))
                    mm.then_inc(s_used, 1)
        pe.wait_ge(s_At, 2 + 1)
        pe.wait_ge(s_Bt, 2 + 1)
        for j in range(8):
            for k in range(2):
                for m in range(TB):
                    c = 2 * j + k
                    mm = pe.transpose(ps[:, j, (2 * k + m) * P:(2 * k + m + 1) * P],
                                      merged[:, m, c * P:(c + 1) * P], ident)
            if j % 4 == 3:
                mm.then_inc(s_mT, 1)
        pe.wait_ge(s_md, 2)
        pe.wait_ge(s_ma, 2)
        for t in range(2):
            wide_tile(4 * t, hT, 16 * (TILES_A + H // 2 + 2 + t + 1))
        pe.wait_ge(s_x2, 2)
        pe.wait_ge(s_h2, 2)
        for j in range(8):
            for k in range(2):
                for m in range(TB):
                    mm = pe.transpose(ps[:, j, (2 * k + m) * P:(2 * k + m + 1) * P], h2[:, m, 2 * j + k, :], ident)
            if j % 4 == 3:
                mm.then_inc(s_h2t, 1)
        pe.wait_ge(s_2d, 2)
        pe.wait_ge(s_2a, 2)
        for m in range(TB):
            for c in range(KC):
                mm = pe.matmul(ps[:, m, 0:G + E], h2T[c // 8][:, c % 8, m * P:(m + 1) * P], wr[:, c, :],
                               start=(c == 0), stop=(c == KC - 1))
        mm.then_inc(s_log, 1)
        pe.wait_ge(s_took, 1)
        pe.matmul(ps[:, 2, 0:E], prev, took[:, 0, :], start=True, stop=True)
        pe.matmul(ps[:, 2, E:2 * E], prev, took[:, 1, :], start=True, stop=True, skip_group_check=True)
        pe.matmul(ps[:, 2, E:2 * E], ones, took[:, 0, :], start=False, stop=True, skip_group_check=True)
        pe.matmul(ps[:, 2, 2 * E:3 * E], ones, took[:, 0, :], start=True, stop=True, skip_group_check=True)
        pe.matmul(ps[:, 2, 2 * E:3 * E], ones, took[:, 1, :], start=False, stop=True,
                  skip_group_check=True).then_inc(s_rank, 1)
        pe.wait_ge(s_steps, 1)
        n_steps = pe.value_load(steps_i[0:1, 0:1], min_val=NQ, max_val=NQ * (T // SLOTS))
        with pe.Fori(0, n_steps) as it:
            pe.wait_ge(s_sel, it + 1)
            pe.wait_ge(s_yd, 2 * it + 1)
            pe.wait_ge(s_ya, 2 * it + 1)
            for j in range(4):
                for k in range(4):
                    for m in range(TB):
                        mm = pe.matmul(ps[:, 4 + j, k * P:(k + 1) * P], h2[:, m, 4 * j + k, :],
                                       selE[:, m, :, :].rearrange("p e s -> p (e s)"),
                                       start=(m == 0), stop=(m == 1), skip_group_check=True)
            mm.then_inc(s_gath, 1)
            pe.wait_ge(s_add, 8 * it + 1)
            for m in range(TB):
                mm = pe.transpose(ps[:, 2, m * P:(m + 1) * P], selW[:, m, :, :].rearrange("p e s -> p (e s)"),
                                  ident)
            mm.then_inc(s_swt, 1)
            pe.wait_ge(s_xd, it + 1)
            pe.wait_ge(s_xa, it + 1)
            for j in range(16):
                mlanded(pe, j, it)
                for c in range(2):
                    kc = 2 * (j // 2) + c
                    for e in range(QUAD):
                        mm = pe.matmul(ps[SLOTS * e:SLOTS * e + SLOTS, j % 2, :],
                                       xgT[:, kc, SLOTS * e:SLOTS * e + SLOTS],
                                       ring[mslot(j)][:, e * 1024 + c * 512:e * 1024 + c * 512 + 512],
                                       start=(kc == 0), stop=(kc == KC - 1))
                mm.then_inc(s_used, 1)
            pe.wait_ge(s_hS, it + 1)
            for f in range(4):
                mm = pe.transpose(ps[:, 0, f * P:(f + 1) * P], hS[:, f * P:(f + 1) * P], ident)
            mm.then_inc(s_ht, 1)
            pe.wait_ge(s_hT, it + 1)
            for nh in range(2):
                for c in range(4):
                    j = 16 + 4 * nh + c
                    mlanded(pe, j, it)
                    for n in range(2):
                        for e in range(QUAD):
                            a = e * 1024 + n * 512
                            mm = pe.matmul(ps[SLOTS * e:SLOTS * e + SLOTS, 4 + 2 * nh + n, :],
                                           hT4[:, c * P + SLOTS * e:c * P + SLOTS * e + SLOTS],
                                           ring[mslot(j)][:, a:a + 512], start=(c == 0), stop=(c == 3))
                    mm.then_inc(s_used, 1)
            pe.wait_ge(s_sw, it + 1)
            for nh in range(2):
                pe.wait_ge(s_yd, 2 * it + (nh + 2))
                pe.wait_ge(s_ya, 2 * it + (nh + 2))
                for n in range(2):
                    for m in range(TB):
                        k = 4 * nh + 2 * n + m
                        if k >= 2:
                            pe.wait_ge(s_add, 8 * it + k)
                        pe.matmul(ps[:, 2 + m, :], selWT[:, m * P:(m + 1) * P],
                                  yS[:, (2 * nh + n) * 512:(2 * nh + n + 1) * 512],
                                  start=True, stop=True).then_inc(s_comb, 1)

    def rsqrt_dve(dve, link, dst, src, scale, n):
        dve.tensor_scalar(rv, src, scale, EPS, ALU.mult, ALU.add).then_inc(s_v, 1)
        dve.wait_ge(s_v, n)
        dve.wait_ge(s_y0, n)
        link(dve.tensor_tensor(rq, rv, ry, ALU.mult))
        link(dve.tensor_tensor(rq, rq, ry, ALU.mult))
        link(dve.tensor_scalar(rq, rq, -0.5, 1.5, ALU.mult, ALU.add))
        link(dve.tensor_tensor(dst, rq, ry, ALU.mult))

    def rsqrt_act(act, link, n):
        act.wait_ge(s_v, n)
        link(act.activation(ry, rv, ACT.Ln))
        act.activation(ry, ry, ACT.Exp, scale=-0.5).then_inc(s_y0, 1)

    @block.vector
    def _(dve):
        ch = Chain(dve, s_dve)
        link = ch.link
        for s in (s_ost, s_At, s_Bt, s_yd, s_add):
            dve.sem_inc(s, 1)
        dve.memset(one_c, 1.0).then_inc(s_set, 1)
        dve.wait_ge(s_x, 16)
        link(dve.tensor_tensor_reduce(h0[:, 1, :], x0[:, 1, :], x0[:, 1, :], 1.0, 0.0, ALU.mult, ALU.add,
                                      ss[:, 1:2]))
        dve.wait_ge(s_ssq, 1)
        rsqrt_dve(dve, link, rs, ss, 1.0 / D, 1)
        dve.wait_ge(s_gain, 16)
        for m in range(TB):
            dve.scalar_tensor_tensor(h0[:, m, :], x0[:, m, :], rs[:, m:m + 1], gain[:], ALU.mult,
                                     ALU.mult).then_inc(s_h, 1)
        dve.wait_ge(s_cst, 16)
        link(dve.tensor_copy(ident16[:], ident))
        dve.tensor_copy(mask16[:], cst[:, C_MSB:C_MSB + 2 * P].rearrange("p (a b) -> p a b", a=2)).then_inc(s_dve, 1)
        ch.n += 1
        dve.wait_ge(s_small, 16 * 7)
        for v in range(2):
            link(dve.tensor_tensor_reduce(lamv[:, 2 * v, :], lamv[:, 2 * v, :], lamv[:, 2 * v + 1, :], 1.0, 0.0,
                                          ALU.mult, ALU.add, lam4[:, v:v + 1]))
        link(dve.tensor_copy(lamE, lam4))
        dve.tensor_copy(lam4, lamE).then_inc(s_lam, 1)

        def hT_half(half):
            b = 4 * half
            return (hT[:, 8 * half:8 * half + 4, :].rearrange("p c t -> p (c t)"),
                    ps[:, b:b + 2, :].rearrange("p b n -> p (b n)"))

        for half in range(2):
            dve.wait_ge(s_turned, half + 1)
            d, s = hT_half(half)
            dve.tensor_copy(d, s).then_inc(s_fd, 1)

        def take_tile(t, par):
            dve.wait_ge(s_used, 4 * t + 4)
            dve.tensor_copy(proj[:, bass.ds(t, 1), :, 0, :].rearrange("p r h d -> p (r h) d"),
                            ps[:, 4 * par:4 * par + 2, :].rearrange("p b (h d) -> p (b h) d", d=P)
                            ).then_inc(s_fd, 1)

        with dve.Fori(0, 2) as i:
            take_tile(2 * i, 0)
            take_tile(2 * i + 1, 1)
        take_tile(4, 0)
        dve.wait_ge(s_fa, 2 + 5)
        dve.wait_ge(s_fd, 2 + 5)
        qk = at(B_P + R_QDA * 2048, SLOT).rearrange("p (b s a f) -> p b s a f", b=16, s=4, a=2)
        lo, hi = qk[:, :, :, 0, :], qk[:, :, :, 1, :]
        half_u = at(B_GATE, 2048).rearrange("p (b s f) -> p b s f", b=16, s=4)
        half_v = at(B_GATE + 2048, 2048).rearrange("p (b s f) -> p b s f", b=16, s=4)
        cosB = cosH.unsqueeze(1).to_broadcast([P, 16, 4, HD // 2])
        sinB = sinH.unsqueeze(1).to_broadcast([P, 16, 4, HD // 2])
        link(dve.tensor_tensor(half_u, hi, sinB, ALU.mult))
        link(dve.tensor_tensor(half_v, lo, sinB, ALU.mult))
        link(dve.tensor_tensor(lo, lo, cosB, ALU.mult))
        link(dve.tensor_tensor(hi, hi, cosB, ALU.mult))
        link(dve.tensor_tensor(lo, lo, half_u, ALU.subtract))
        dve.tensor_tensor(hi, hi, half_v, ALU.add).then_inc(s_roped, 1)
        take_tile(5, 1)
        dve.wait_ge(s_lamE, 1)
        link(dve.tensor_tensor(neglam, lamE[:, 1:2], lamE[:, 0:1], ALU.subtract))
        link(dve.tensor_scalar(neglam, neglam, -LAM_INIT, None, ALU.add))
        dve.wait_ge(s_roped, 1)

        n0 = ch.n
        with dve.Fori(0, H) as h:
            ch.off = h * 16
            dve.wait_ge(s_tsb, h + 2)
            link(dve.tensor_scalar(qkT_sb[:, 0, :], ps[:, 2, 0:256], float(P) ** -0.5, None, ALU.mult))
            dve.tensor_copy(qkT_sb[:, 1, :], ps[:, 2, 256:512]).then_inc(s_kd, 1)
            dve.wait_ge(s_sc, h + 1)
            link(dve.tensor_reduce(mx[:, 0:2], ps[:, 5:7, 0:128], AX.X, ALU.max))
            link(dve.tensor_reduce(mx[:, 2:4], ps[:, 5:7, 128:384], AX.X, ALU.max))
            dve.tensor_scalar(nmx, mx, -1.0, None, ALU.mult).then_inc(s_mx, 1)
            dve.wait_ge(s_l, h + 1)
            dve.scalar_tensor_tensor(eS, zS, 0.0, lS, ALU.max, ALU.add).then_inc(s_L, 1)
            dve.wait_ge(s_p, h + 1)
            link(dve.reciprocal(rsm, sm))
            rsm2 = rsm.rearrange("p (q a) -> p q a", a=2)
            link(dve.tensor_scalar(rsn.rearrange("p (q a) -> p q a", a=1), rsm2[:, :, 1:2], neglam, None,
                                   ALU.mult))
            for q, cols in enumerate((slice(0, 128), slice(128, 384))):
                link(dve.tensor_scalar(attn[:, cols], pS[:, 0, cols], rsm[:, 2 * q:2 * q + 1], None, ALU.mult))
            link(dve.scalar_tensor_tensor(attn[:, 0:128], pS[:, 1, 0:128], rsn[:, 0:1], attn[:, 0:128],
                                          ALU.mult, ALU.add))
            dve.scalar_tensor_tensor(attn[:, 128:384], pS[:, 1, 128:384], rsn[:, 1:2], attn[:, 128:384],
                                     ALU.mult, ALU.add).then_inc(s_at, 1)
            dve.wait_ge(s_c, h + 1)
            dve.tensor_tensor(zS, zS, ps[:, 7, 0:384], ALU.subtract).then_inc(s_zc, 1)
            dve.wait_ge(s_att, h + 1)
            dve.tensor_copy(attnT, ps[:, 3, 0:384]).then_inc(s_atT, 1)
            dve.wait_ge(s_osb, h + 2)
            dve.tensor_copy(oT_sb[:, bass.ds(h, 1), :].rearrange("p h t -> p (h t)"),
                            ps[:, 2, 0:256]).then_inc(s_ost, 1)
            dve.wait_ge(s_oS, h + 1)
            for m in range(TB):
                link(dve.tensor_tensor_reduce(sq, oS[:, m, :], oS[:, m, :], 1.0, 0.0, ALU.mult, ALU.add,
                                              oss[:, m:m + 1]))
            rsqrt_dve(dve, link, ors, oss, 1.0 / P, h + 2)
            link(dve.tensor_scalar(ors, ors, 1.0 - LAM_INIT, None, ALU.mult))
            link(dve.scalar_tensor_tensor(oN[:, 0, :], oS[:, 0, :], ors[:, 0:1], gsub, ALU.mult, ALU.mult))
            dve.scalar_tensor_tensor(oN[:, 1, :], oS[:, 1, :], ors[:, 1:2], gsub, ALU.mult,
                                     ALU.mult).then_inc(s_oN, 1)
        per = ch.n - n0
        assert per == 16, per
        ch.n, ch.off = n0 + per * H, 0

        n0 = ch.n
        with dve.Fori(0, 2) as t:
            ch.off = t * 4
            dve.wait_ge(s_used, 4 * t + (PROJ_CHUNKS + GATE_CHUNKS + 2))
            dve.wait_ge(s_sig, 2 * t + 1)
            for m in range(TB):
                ins = dve.tensor_tensor(
                    merged[:, m, bass.ds(t * 1024, 1024)].rearrange("p (b n) -> p b n", b=2),
                    ps[:, 2 * m:2 * m + 2, :], gates[:, bass.ds(2 * t, 2), m, :], ALU.mult)
                if m == 0:
                    link(ins)
            ins.then_inc(s_At, 1)
            dve.wait_ge(s_used, 4 * t + (PROJ_CHUNKS + GATE_CHUNKS + 4))
            dve.wait_ge(s_sig, 2 * t + 2)
            dve.wait_ge(s_At, t + 2)
            for m in range(TB):
                link(dve.tensor_tensor(part.rearrange("p (b n) -> p b n", b=2), ps[:, 4 + 2 * m:6 + 2 * m, :],
                                       gates[:, bass.ds(2 * t + 4, 2), m, :], ALU.mult))
                mg = merged[:, m, bass.ds(t * 1024, 1024)]
                ins = dve.tensor_tensor(mg, mg, part, ALU.add)
                if m == 0:
                    link(ins)
            ins.then_inc(s_Bt, 1)
        assert ch.n - n0 == 4
        ch.n, ch.off = n0 + 8, 0
        dve.wait_ge(s_Bt, 2 + 1)
        dve.memset(cell[:, 40:41], 0.0).then_inc(s_gd, 1)
        for half in range(2):
            dve.wait_ge(s_mT, half + 1)
            d, s = hT_half(half)
            dve.tensor_copy(d, s).then_inc(s_md, 1)

        dve.wait_ge(s_xr, 16)
        for t in range(2):
            dve.wait_ge(s_used, DENSE - 4 + 4 * t)
            for m in range(TB):
                xs = xr[:, m, t * 1024:(t + 1) * 1024]
                ins = dve.tensor_tensor(xs, xs, ps[:, 4 * t + 2 * m:4 * t + 2 * m + 2, :].rearrange(
                    "p b n -> p (b n)"), ALU.add)
                if t == 1:
                    ins.then_inc(s_x2, 1)
                else:
                    link(ins)
        dve.wait_ge(s_x2, 2)
        dve.wait_ge(s_h, 2)
        link(dve.tensor_tensor_reduce(outS[:, 1, :], xr[:, 1, :], xr[:, 1, :], 1.0, 0.0, ALU.mult, ALU.add,
                                      ss[:, 1:2]))
        dve.wait_ge(s_sq2, 1)
        rsqrt_dve(dve, link, rs, ss, 1.0 / D, H + 2)
        dve.wait_ge(s_gain, 32)
        for m in range(TB):
            dve.scalar_tensor_tensor(h2[:, m].rearrange("q c p -> q p c"),
                                     xr[:, m, :].rearrange("q (p c) -> q p c", c=KC), rs[:, m:m + 1],
                                     gain[:].rearrange("q (p c) -> q p c", c=KC), ALU.mult,
                                     ALU.mult).then_inc(s_h2, 1)
        link(dve.memset(lg[:, :, G:8], -3.0e38))
        for half in range(2):
            dve.wait_ge(s_h2t, half + 1)
            dve.tensor_copy(h2T[half][:, 0:4, :].rearrange("p c t -> p (c t)"),
                            ps[:, 4 * half:4 * half + 2, :].rearrange("p b n -> p (b n)")).then_inc(s_2d, 1)
        dve.wait_ge(s_log, 1)
        link(dve.tensor_copy(lg[:, :, 0:G], ps[:, 0:2, 0:G]))
        link(dve.tensor_copy(lg[:, :, 8:8 + E], ps[:, 0:2, G:G + E]))
        for m in range(TB):
            link(dve.max(gm8[:, m, :], lg[:, m, 0:8]))
            link(dve.max_index(gi8[:, m, :], gm8[:, m, :], lg[:, m, 0:8]))
        rt4 = rt.rearrange("p (a m) -> p a m", m=TB)
        neg_gm, gsum, pg = rt4[:, 0, :], rt4[:, 1, :], rt4[:, 2, :]
        gap, dexp, base, w1, w2, e1, e2 = (rt4[:, 3 + i, :] for i in range(7))
        dve.tensor_scalar(neg_gm.unsqueeze(2), gm8[:, :, 0:1], -1.0, None, ALU.mult).then_inc(s_gm, 1)
        link(dve.tensor_copy(gi8f, gi8))
        iota_g = cst[:, C_IOTA:C_IOTA + G]
        iota_e = cst[:, C_IOTA:C_IOTA + E]
        for m in range(TB):
            link(dve.tensor_scalar(goh[:, m, :], iota_g, gi8f[:, m, 0:1], None, ALU.is_equal))
            link(dve.tensor_tensor(picked[:, m, :].rearrange("p (g j) -> p g j", g=G),
                                   lg[:, m, 8:8 + E].rearrange("p (g j) -> p g j", g=G),
                                   goh[:, m, :].unsqueeze(2).to_broadcast([P, G, EPG]), ALU.mult))
            link(dve.tensor_reduce(esel[:, m, :], picked[:, m, :].rearrange("p (g j) -> p j g", g=G), AX.X, ALU.add))
            link(dve.max(ev8[:, m, :], esel[:, m, :]))
            link(dve.max_index(ei8[:, m, :], ev8[:, m, :], esel[:, m, :]))
        dve.tensor_tensor(gap.unsqueeze(2), ev8[:, :, 1:2], ev8[:, :, 0:1], ALU.subtract).then_inc(s_dd, 1)
        link(dve.tensor_copy(ei8f, ei8))
        link(dve.tensor_scalar(base.unsqueeze(2), gi8f[:, :, 0:1], float(EPG), None, ALU.mult))
        link(dve.tensor_tensor(e1.unsqueeze(2), base.unsqueeze(2), ei8f[:, :, 0:1], ALU.add))
        link(dve.tensor_tensor(e2.unsqueeze(2), base.unsqueeze(2), ei8f[:, :, 1:2], ALU.add))
        for m in range(TB):
            link(dve.tensor_scalar(oh1[:, m, :], iota_e, e1[:, m:m + 1], None, ALU.is_equal))
            link(dve.tensor_scalar(oh2[:, m, :], iota_e, e2[:, m:m + 1], None, ALU.is_equal))
        dve.tensor_tensor(took, oh1, oh2, ALU.add).then_inc(s_took, 1)
        dve.wait_ge(s_gx, 1)
        link(dve.reciprocal(pg, gsum))
        dve.wait_ge(s_ex, 1)
        link(dve.tensor_scalar(w1, dexp, 1.0, None, ALU.add))
        link(dve.reciprocal(w1, w1))
        link(dve.tensor_tensor(w1, w1, pg, ALU.mult))
        link(dve.tensor_tensor(w2, w1, dexp, ALU.mult))
        for m in range(TB):
            link(dve.tensor_scalar(share[:, m, :], oh2[:, m, :], w2[:, m:m + 1], None, ALU.mult))
            link(dve.scalar_tensor_tensor(share[:, m, :], oh1[:, m, :], w1[:, m:m + 1], share[:, m, :],
                                          ALU.mult, ALU.add))
        dve.wait_ge(s_rank, 1)
        link(dve.tensor_scalar(rank, ps[:, 2, 0:2 * E].rearrange("p (m e) -> p m e", m=TB), 4096.0, None, ALU.add))
        dve.wait_ge(s_took, 1)
        link(dve.tensor_tensor(rank, rank, took, ALU.mult))
        link(dve.tensor_scalar(rank, rank, -4096.0, None, ALU.add))
        link(dve.tensor_reduce(w1[:, 0:1], ps[:, 2, 2 * E:3 * E], AX.X, ALU.max))
        link(dve.tensor_scalar(count8, cst[:, C_THR:C_THR + 8], w1[:, 0:1], None, ALU.is_lt))
        link(dve.tensor_reduce(w1[:, 0:1], count8, AX.X, ALU.add))
        dve.tensor_scalar(steps_i[:, 0:1], w1[:, 0:1], float(NQ), float(NQ), ALU.mult, ALU.add).then_inc(s_steps, 1)
        dve.wait_ge(s_steps, 1)
        n_steps = dve.value_load(steps_i[0:1, 0:1], min_val=NQ, max_val=NQ * (T // SLOTS))

        n0 = ch.n
        per_step = 3
        with dve.Fori(0, n_steps) as it:
            ch.off = it * per_step
            q = it % NQ
            rk = rank[:, :, bass.ds(q * QUAD, QUAD)]
            for m in range(TB):
                ins = dve.tensor_tensor(selE[:, m], iota_e.unsqueeze(1).to_broadcast([P, QUAD, SLOTS]),
                                        rk[:, m, :].unsqueeze(2).to_broadcast([P, QUAD, SLOTS]), ALU.is_equal)
                link(ins)
                ins = dve.tensor_tensor(selW[:, m], selE[:, m],
                                        share[:, m, bass.ds(q * QUAD, QUAD)].unsqueeze(2).to_broadcast(
                                            [P, QUAD, SLOTS]), ALU.mult)
                if m == 1:
                    ins.then_inc(s_sel, 1)
            link(dve.tensor_scalar(rk, rk, -float(SLOTS), None, ALU.add))
            dve.wait_ge(s_gath, it + 1)
            dve.tensor_copy(xgT[:, 0:8, :].rearrange("p c s -> p (c s)"),
                            ps[:, 4:6, :].rearrange("p b n -> p (b n)")).then_inc(s_xd, 1)
            dve.wait_ge(s_swt, it + 1)
            dve.tensor_copy(selWT, ps[:, 2, 0:T]).then_inc(s_sw, 1)
            dve.wait_ge(s_e, it + 1)
            dve.tensor_tensor(hS, gE, ps[:, 1, :], ALU.mult).then_inc(s_hS, 1)
            for nh in range(2):
                dve.wait_ge(s_used, it * QCH + (DENSE + 20 + 4 * nh))
                dve.tensor_copy(yS[:, nh * 1024:nh * 1024 + 512], ps[:, 4 + 2 * nh, :]).then_inc(s_yd, 1)
            for nh in range(2):
                for n in range(2):
                    for m in range(TB):
                        k = 4 * nh + 2 * n + m
                        dve.wait_ge(s_comb, it * 8 + (k + 1))
                        cols = slice((2 * nh + n) * 512, (2 * nh + n + 1) * 512)
                        dve.tensor_tensor(xr[:, m, cols], xr[:, m, cols], ps[:, 2 + m, :],
                                          ALU.add).then_inc(s_add, 1)
        assert ch.n - n0 == per_step, ch.n - n0
        ch.n, ch.off = n0, n_steps * per_step

        dve.wait_ge(s_add, n_steps * 8 + 1)
        link(dve.tensor_tensor_reduce(outS[:, 1, :], xr[:, 1, :], xr[:, 1, :], 1.0, 0.0, ALU.mult, ALU.add,
                                      ss[:, 1:2]))
        dve.wait_ge(s_fss, 1)
        rsqrt_dve(dve, link, rs, ss, 1.0 / D, H + 3)
        dve.wait_ge(s_gain, 48)
        for m in range(TB):
            dve.scalar_tensor_tensor(outS[:, m, :], xr[:, m, :], rs[:, m:m + 1], gain[:], ALU.mult,
                                     ALU.mult).then_inc(s_out, 1)

    @block.scalar
    def _(act):
        ch = Chain(act, s_act)
        link = ch.link
        for s in (s_odt, s_ge, s_ya):
            act.sem_inc(s, 1)
        act.wait_ge(s_x, 16)
        act.activation(h0[:, 0, :], x0[:, 0, :], ACT.Square, accum_out=ss[:, 0:1]).then_inc(s_ssq, 1)
        rsqrt_act(act, link, 1)

        def hT_half(half):
            b = 4 * half + 2
            return (hT[:, 8 * half + 4:8 * half + 8, :].rearrange("p c t -> p (c t)"),
                    ps[:, b:b + 2, :].rearrange("p b n -> p (b n)"))

        for half in range(2):
            act.wait_ge(s_turned, half + 1)
            d, s = hT_half(half)
            act.copy(d, s).then_inc(s_fa, 1)
        act.wait_ge(s_lam, 1)
        act.activation(lamE, lam4, ACT.Exp).then_inc(s_lamE, 1)

        with act.Fori(0, TILES_A // 2) as i:
            for par in range(2):
                act.wait_ge(s_used, 8 * i + 4 * (par + 1))
                act.copy(proj[:, bass.ds(2 * i + par, 1), :, 1, :].rearrange("p r h d -> p (r h) d"),
                         ps[:, 4 * par + 2:4 * par + 4, :].rearrange("p b (h d) -> p (b h) d", d=P)
                         ).then_inc(s_fa, 1)
        act.wait_ge(s_set, 2)
        n0 = ch.n
        with act.Fori(0, H) as h:
            ch.off = h * 5
            act.wait_ge(s_tda, h + 2)
            link(act.activation(qkT_da[:, 0, :], ps[:, 3, 0:256], ACT.Copy, scale=float(HD) ** -0.5))
            act.copy(qkT_da[:, 1, :], ps[:, 3, 256:512]).then_inc(s_ka, 1)
            act.wait_ge(s_z, h + 1)
            link(act.copy(zS, ps[:, 4, 0:384]))
            link(act.activation(lS, ps[:, 4, 0:384], ACT.Abs))
            link(act.activation(lS, lS, ACT.Exp, scale=-1.0))
            act.activation(lS, lS, ACT.Ln, bias=one_c).then_inc(s_l, 1)
            act.wait_ge(s_mx, h + 1)
            for q, cols in enumerate((slice(0, 128), slice(128, 384))):
                for mp in range(2):
                    i = 2 * q + mp
                    ins = act.activation(pS[:, mp, cols], ps[:, 5 + mp, cols], ACT.Exp, bias=nmx[:, i:i + 1],
                                         accum_out=sm[:, i:i + 1])
            ins.then_inc(s_p, 1)
            act.wait_ge(s_zc, h + 1)
            act.activation(aT, zS, ACT.Exp).then_inc(s_a, 1)
            act.wait_ge(s_oda, h + 1)
            act.copy(oS.rearrange("p m d -> p (m d)"), ps[:, 3, 0:256]).then_inc(s_oS, 1)
            rsqrt_act(act, link, h + 2)
            act.wait_ge(s_used, 2 * h + (PROJ_CHUNKS + 2))
            act.copy(gates[:, bass.ds(h, 1), :, :].rearrange("p h m n -> p (h m n)"),
                     ps[:, 0:2, :].rearrange("p b n -> p (b n)")).then_inc(s_ge, 1)
            act.wait_ge(s_oT, h + 1)
            act.copy(oT_da[:, bass.ds(h, 1), :].rearrange("p h t -> p (h t)"),
                     ps[:, 3, 256:512]).then_inc(s_odt, 1)
        assert ch.n - n0 == 5, ch.n - n0
        ch.n, ch.off = n0 + (ch.n - n0) * H, 0
        act.wait_ge(s_ge, H + 1)
        for t in range(2):
            for br in range(2):
                gt = gates[:, 4 * br + 2 * t:4 * br + 2 * t + 2, :, :].rearrange("p h m n -> p (h m n)")
                act.activation(gt, gt, ACT.Sigmoid).then_inc(s_sig, 1)
        for half in range(2):
            act.wait_ge(s_mT, half + 1)
            d, s = hT_half(half)
            act.copy(d, s).then_inc(s_ma, 1)
        act.wait_ge(s_x2, 2)
        act.activation(outS[:, 0, :], xr[:, 0, :], ACT.Square, accum_out=ss[:, 0:1]).then_inc(s_sq2, 1)
        rsqrt_act(act, link, H + 2)
        for half in range(2):
            act.wait_ge(s_h2t, half + 1)
            act.copy(h2T[half][:, 4:8, :].rearrange("p c t -> p (c t)"),
                     ps[:, 4 * half + 2:4 * half + 4, :].rearrange("p b n -> p (b n)")).then_inc(s_2a, 1)
        rt4 = rt.rearrange("p (a m) -> p a m", m=TB)
        act.wait_ge(s_gm, 1)
        for m in range(TB):
            ins = act.activation(gexp[:, m, :], lg[:, m, 0:G], ACT.Exp, bias=rt4[:, 0, m:m + 1],
                                 accum_out=rt4[:, 1, m:m + 1])
        ins.then_inc(s_gx, 1)
        act.wait_ge(s_dd, 1)
        act.activation(rt4[:, 4, :], rt4[:, 3, :], ACT.Exp).then_inc(s_ex, 1)
        act.wait_ge(s_steps, 1)
        n_steps = act.value_load(steps_i[0:1, 0:1], min_val=NQ, max_val=NQ * (T // SLOTS))
        with act.Fori(0, n_steps) as it:
            act.wait_ge(s_gath, it + 1)
            act.copy(xgT[:, 8:16, :].rearrange("p c s -> p (c s)"),
                     ps[:, 6:8, :].rearrange("p b n -> p (b n)")).then_inc(s_xa, 1)
            act.wait_ge(s_used, it * QCH + (DENSE + 16))
            act.activation(gE, ps[:, 0, :], ACT.Silu).then_inc(s_e, 1)
            act.wait_ge(s_ht, it + 1)
            act.copy(hT4, ps[:, 0, :]).then_inc(s_hT, 1)
            for nh in range(2):
                act.wait_ge(s_used, it * QCH + (DENSE + 20 + 4 * nh))
                act.copy(yS[:, nh * 1024 + 512:nh * 1024 + 1024], ps[:, 5 + 2 * nh, :]).then_inc(s_ya, 1)
        act.wait_ge(s_add, n_steps * 8 + 1)
        act.activation(outS[:, 0, :], xr[:, 0, :], ACT.Square, accum_out=ss[:, 0:1]).then_inc(s_fss, 1)
        rsqrt_act(act, link, H + 3)

    ctx.close()


_INS = ["x", "mix_norm_g", "w_in", "lambda_q1", "lambda_k1", "lambda_q2", "lambda_k2", "diff_subnorm_g",
        "w_branch_sb", "w_branch_diff", "w_out", "ffn_norm_g", "w_group_router", "w_expert_router",
        "w_gate", "w_up", "w_down", "final_norm_g"]


def kernel(**inputs):
    import concourse.bacc as bacc
    from concourse.bass_utils import run_bass_kernel_spmd

    nc = bacc.Bacc("TRN2", target_bir_lowering=False, num_devices=1)
    arrays, args = {}, []
    for name in _INS:
        a = np.ascontiguousarray(inputs[name])
        arrays[f"in_{name}"] = a
        args.append(nc.dram_tensor(f"in_{name}", a.shape, mybir.dt.from_np(a.dtype), kind="ExternalInput").ap())
    c = shape_constants()
    arrays["shape_constants"] = c
    args.append(nc.dram_tensor("shape_constants", c.shape, F32, kind="ExternalInput").ap())
    out = nc.dram_tensor("out", inputs["x"].shape, F32, kind="ExternalOutput").ap()
    build(nc, *args, out)
    r = run_bass_kernel_spmd(nc, [arrays], core_ids=[0])
    return r.results[0]["out"]
```

```python
from contextlib import ExitStack

import numpy as np

import concourse.bass as bass
from concourse import mybir

F32 = mybir.dt.float32
F32R = mybir.dt.float32r
BF16 = mybir.dt.bfloat16
U32 = mybir.dt.uint32
I32 = mybir.dt.int32
ALU = mybir.AluOpType
ACT = mybir.ActivationFunctionType
AX = mybir.AxisListType

P = 128
D = 2048
T = 256
TB = T // P
KC = D // P
H = 8
W = H * P
HD = 64
CHUNK = 64
G = 4
EPG = 8
E = G * EPG
F = D // 4
SLOTS = 32
QUAD = P // SLOTS
NQ = E // QUAD
EPS = 1e-6
LN_EXP = "natural_log_exp_and_others"
LAM_INIT = 0.2
NEG = -1e30
SLOT = 4096
DRING = 4
MRING = 8
MORDER = (4, 5, 0, 1, 2, 3, 6, 7)
TEMPS = 7168
RC = 64
TILES_A = 6
PROJ_CHUNKS = 4 * TILES_A
GATE_CHUNKS = 2 * H
BRANCH_CHUNKS = 8
OUT_CHUNKS = 8
DENSE = PROJ_CHUNKS + GATE_CHUNKS + BRANCH_CHUNKS + OUT_CHUNKS
QCH = 24
R_QSB, R_QDA, R_KSB, R_VSB, R_KDA, R_VDA = range(6)
PIECE = 512
AHEAD = 4
PT = 32
G_B = TILES_A * PT
G_C = G_B + H * KC
G_D = G_C + 2 * PT
OUT_ORDER = ((0, 0), (0, 1), (1, 0), (1, 1))

C_ID, C_TRI, C_ONE, C_PREV, C_MSB, C_MDA, C_COS, C_SIN, C_IOTA, C_THR = (
    0, 128, 256, 384, 512, 640, 768, 896, 1024, 1056)
C_ST = 1064
C_N = 1064 + G + E


def shape_constants():
    c = np.zeros((P, C_N), np.float32)
    i = np.arange(P)
    c[:, C_ID:C_ID + P] = i[:, None] == i[None, :]
    c[:, C_TRI:C_TRI + P] = i[:, None] >= i[None, :]
    c[:, C_ONE:C_ONE + P] = 1.0
    c[:, C_PREV:C_PREV + P] = i[:, None] < i[None, :]
    c[:, C_MSB:C_MSB + P] = np.where(i[:, None] >= i[None, :], NEG, 0.0)
    c[:, C_MDA:C_MDA + P] = np.where(i[None, :] // CHUNK > i[:, None] // CHUNK, NEG, 0.0)
    half = HD // 2
    inv = np.float32(10000.0) ** (-(np.arange(half, dtype=np.float32) * np.float32(2.0) / np.float32(HD)))
    ang = (np.arange(T, dtype=np.float32)[:, None] * inv.astype(np.float32)[None, :]).astype(np.float64)
    for m in range(TB):
        for mp in range(2):
            at = (m * 2 + mp) * half
            c[:, C_COS + at:C_COS + at + half] = np.cos(ang[m * P:(m + 1) * P])
            c[:, C_SIN + at:C_SIN + at + half] = np.sin(ang[m * P:(m + 1) * P])
    c[:, C_IOTA:C_IOTA + E] = np.arange(E)
    c[:, C_THR:C_THR + 8] = np.arange(1, 9) * SLOTS
    for half in range(2):
        c[half * RC:half * RC + G + E, C_ST:] = np.eye(G + E)
    return c


class Chain:

    def __init__(self, eng, sem):
        self.eng, self.sem, self.n, self.off = eng, sem, 0, 0

    def link(self, ins):
        self.n += 1
        ins.then_inc(self.sem, 1)
        self.eng.wait_ge(self.sem, self.off + self.n)


def build(nc, x, mix_g, w_in, lq1, lk1, lq2, lk2, sub_g, w_sb, w_da, w_out, ffn_g, w_gr, w_er,
          w_gate, w_up, w_down, fin_g, consts, out):
    ctx = ExitStack()

    def sb(name, shape, dt=F32):
        return ctx.enter_context(nc.sbuf_tensor(name, shape, dt))

    def sem(name):
        return ctx.enter_context(nc.semaphore(name))

    cst = sb("cst", [P, C_N])
    gain = sb("gain", [P, D])
    wr = sb("wr", [P, KC, RC])
    g16 = sb("g16", [KC, P])
    gT = sb("gT", [P, KC])
    ident16 = sb("ident16", [P, P], BF16)
    mask16 = sb("mask16", [P, 2, P], BF16)
    cell = sb("cell", [P, 64])
    arena = sb("arena", [P, DRING * SLOT + 6 * 2048 + TEMPS])
    n_split = 2 * SLOT + AHEAD * 2 * PIECE
    with nc.sbuf_tensor("split", [P, n_split], F32R) as split:
        pass
    late = sb("late", [P, n_split])
    ps = ctx.enter_context(nc.psum_tensor("ps", [P, 8, 512], F32))

    ident, tri, ones, prev = (cst[:, a:a + P] for a in (C_ID, C_TRI, C_ONE, C_PREV))
    cosH = cst[:, C_COS:C_COS + P].rearrange("p (s f) -> p s f", s=4)
    sinH = cst[:, C_SIN:C_SIN + P].rearrange("p (s f) -> p s f", s=4)

    xH = split[:, 0:SLOT].rearrange("p (c t) -> p c t", c=KC)
    xL = split[:, SLOT:2 * SLOT].rearrange("p (c t) -> p c t", c=KC)
    wH = [split[:, 2 * SLOT + b * 2 * PIECE:2 * SLOT + (2 * b + 1) * PIECE] for b in range(AHEAD)]
    wL = [split[:, 2 * SLOT + (2 * b + 1) * PIECE:2 * SLOT + (2 * b + 2) * PIECE] for b in range(AHEAD)]

    def at(base, n):
        return arena[:, base:base + n]

    B_P = DRING * SLOT
    proj = at(B_P, 6 * 2048).rearrange("p (r h m d) -> p r h m d", r=6, h=H, m=TB)
    gates = proj[:, 2:6]
    x0 = at(B_P + 2 * 2048, SLOT).rearrange("p (m d) -> p m d", m=TB)
    h0 = at(B_P + 4 * 2048, SLOT).rearrange("p (m d) -> p m d", m=TB)
    oT = at(B_P, SLOT).rearrange("p (c t) -> p c t", c=KC)
    xr = at(B_P, SLOT).rearrange("p (m d) -> p m d", m=TB)
    h2 = late[:, 0:SLOT].rearrange("p (m c d) -> p m c d", m=TB, c=KC)
    xgT = late[:, SLOT:SLOT + 2048].rearrange("p (c s) -> p c s", c=KC)
    yS = late[:, SLOT + 2048:2 * SLOT]
    outS = late[:, SLOT:2 * SLOT].rearrange("p (m d) -> p m d", m=TB)
    ring = ([at(s * SLOT, SLOT) for s in range(DRING)]
            + [at(B_P + (2 + 2 * s) * 2048, SLOT) for s in range(2)]
            + [late[:, 2 * SLOT:3 * SLOT],
               at(B_P + 6 * 2048, SLOT)])
    B_X = B_P + 6 * 2048
    used = [B_X]

    def temp(n):
        used[0] += n
        assert used[0] <= B_X + TEMPS
        return at(used[0] - n, n)

    squares = at(B_X, SLOT).rearrange("p (m d) -> p m d", m=TB)
    gsub = at(B_X + TEMPS - P, P)
    lamv = at(B_X + SLOT, 256).rearrange("p (v d) -> p v d", v=4)
    rope_u, rope_v = (temp(1024).rearrange("p (b s f) -> p b s f", b=H, s=4) for _ in range(2))
    used[0] = B_X
    qk_sb = temp(512).rearrange("p (w m d) -> p w m d", w=2, m=TB)
    qk_da = temp(512).rearrange("p (w m d) -> p w m d", w=2, m=TB)
    v_sb = temp(256).rearrange("p (m d) -> p m d", m=TB)
    qkT_sb = temp(512).rearrange("p (w t) -> p w t", w=2)
    qkT_da = temp(512).rearrange("p (w t) -> p w t", w=2)
    zS, eS, lS, aT, attn, attnT = (temp(384) for _ in range(6))
    pS = temp(768).rearrange("p (a k) -> p a k", a=2)
    oS = temp(256).rearrange("p (m d) -> p m d", m=TB)
    oN = temp(256).rearrange("p (m d) -> p m d", m=TB)
    sq = temp(P)
    used[0] = B_X
    merged = temp(SLOT).rearrange("p (m n) -> p m n", m=TB)
    part = temp(1024)
    used[0] = B_X
    x2T = temp(SLOT).rearrange("p (c t) -> p c t", c=KC)
    accS = temp(T)
    lg = temp(TB * (G + 4 + E)).rearrange("p (m e) -> p m e", m=TB)
    gm8, gi8f, ev8, ei8f = (temp(16).rearrange("p (m e) -> p m e", m=TB) for _ in range(4))
    gi8, ei8 = (temp(16).bitcast(U32).rearrange("p (m e) -> p m e", m=TB) for _ in range(2))
    goh = temp(8).rearrange("p (m g) -> p m g", m=TB)
    gexp = temp(8).rearrange("p (m g) -> p m g", m=TB)
    picked = temp(TB * E).rearrange("p (m e) -> p m e", m=TB)
    esel = temp(16).rearrange("p (m e) -> p m e", m=TB)
    oh1, oh2, took, share, rank = (temp(TB * E).rearrange("p (m e) -> p m e", m=TB) for _ in range(5))
    rt = temp(64)
    count8 = temp(8)
    steps_i = temp(2).bitcast(I32)
    selE = temp(TB * P).rearrange("p (m e s) -> p m e s", m=TB, e=QUAD)
    selW = temp(TB * P).rearrange("p (m e s) -> p m e s", m=TB, e=QUAD)
    selG = temp(TB * P).rearrange("p (m n) -> p m n", m=TB)
    selWT = temp(T)
    hidden, hT4 = (temp(512) for _ in range(2))
    outJ = at(B_X + TEMPS - 2048, 2048).rearrange("p (m d) -> p m d", m=TB)

    one_c = cell[:, 0:1]
    ss, rs = cell[:, 2:4], cell[:, 4:6]
    neglam = cell[:, 6:7]
    lam4 = cell[:, 8:10]
    lamE = cell[:, 10:12]
    mx, nmx, sm, rsm = cell[:, 12:16], cell[:, 16:20], cell[:, 20:24], cell[:, 24:28]
    oss, ors = cell[:, 28:30], cell[:, 30:32]
    rsn = cell[:, 32:34]
    ssA, ssB = cell[:, 42:44], cell[:, 44:46]
    rv, ry, rq = cell[:, 34:36], cell[:, 36:38], cell[:, 38:40]

    s_cst, s_gain, s_small, s_xr, s_store = (sem(n) for n in (
        "consts_landed", "gain_landed", "small_landed", "xr_landed", "stored"))
    s_xk = [sem(f"x_half{k}_landed") for k in range(2)]
    landed = [sem(f"slot{s}_landed") for s in range(MRING)]
    s_wh, s_wl, s_pu = sem("piece_rounded"), sem("piece_rest_ready"), sem("pieces_used")
    s_used = sem("expert_chunks_used")
    s_dve, s_act = sem("dve_chain"), sem("act_chain")
    s_set = sem("cells_set")
    s_ssq = sem("squares_summed")
    s_h = sem("h_ready")
    s_turned, s_xh, s_xl = sem("operand_turned"), sem("operand_rounded"), sem("operand_rest_ready")
    s_fd, s_fa = sem("half_free_dve"), sem("half_free_act")
    s_roped = sem("roped")
    s_v, s_y0, s_rs = sem("mean_square_ready"), sem("root_estimated"), sem("root_ready")
    s_gt, s_wr = sem("gain_turned"), sem("router_weights_ready")
    s_hsb, s_hda, s_hv = sem("head_sb_copied"), sem("head_da_copied"), sem("head_v_copied")
    s_tsb, s_tda = sem("sb_qk_turned"), sem("da_qk_turned")
    s_kd, s_ka = sem("qkT_by_dve"), sem("qkT_by_act")
    s_z, s_sc = sem("z_done"), sem("da_scores_done")
    s_l, s_L = sem("log_part_ready"), sem("softplus_ready")
    s_zc, s_c, s_a = sem("z_less_sum_ready"), sem("sums_done"), sem("a_ready")
    s_mx, s_p = sem("row_max_ready"), sem("probs_ready")
    s_at, s_att, s_atT = sem("attn_ready"), sem("attn_turned"), sem("attnT_ready")
    s_osb, s_oda = sem("sb_o_done"), sem("da_o_done")
    s_ost, s_oS, s_oN, s_oT, s_odt = (sem(n) for n in (
        "oT_sb_stored", "da_o_copied", "da_o_normed", "da_o_turned", "oT_da_stored"))
    s_ge, s_sig, s_gd = sem("gate_tile_copied"), sem("gates_squashed"), sem("gates_read")
    s_lam = sem("lambda_sums")
    s_lamE = sem("lambda_exps")
    s_At, s_Bt = sem("branch_a_read"), sem("branch_b_read")
    s_x2, s_sq2, s_h2 = sem("x2_ready"), sem("x2_squares"), sem("h2_ready")
    s_x2t, s_2d, s_2a = sem("x2_turned"), sem("x2T_by_dve"), sem("x2T_by_act")
    s_acc, s_accS = sem("logits_summed"), sem("logit_sums_copied")
    s_log, s_gm, s_gx = sem("logits_done"), sem("group_max_ready"), sem("group_exp_ready")
    s_ex = sem("pair_exp_ready")
    s_dd = sem("pair_gap_ready")
    s_took, s_rank, s_steps = sem("took_ready"), sem("ranks_done"), sem("steps_ready")
    s_shr = sem("shares_ready")
    s_sel, s_gath, s_xd, s_xa = sem("sel_ready"), sem("gathered"), sem("xgT_by_dve"), sem("xgT_by_act")
    s_swt, s_sw = sem("shares_turned"), sem("sharesT_ready")
    s_e, s_hS = sem("silu_ready"), sem("hidden_ready")
    s_ht, s_hT = sem("hidden_turned"), sem("hiddenT_ready")
    s_yd, s_ya = sem("y_by_dve"), sem("y_by_act")
    s_comb, s_add = sem("combined"), sem("added")
    s_fss, s_out = sem("final_squares"), sem("out_rows_ready")

    w_in_c = w_in[0].rearrange("(c k p) n -> c p k n", c=4, p=P)
    w_gt_c = w_in[0].rearrange("(c k p) n -> c p k n", c=2, p=P)
    w_br_c = [w[0].rearrange("(c k p) n -> c p k n", c=2, p=P) for w in (w_sb, w_da)]
    w_out_c = w_out[0].rearrange("(c k p) n -> c p k n", c=4, p=P)
    w_gate_q = w_gate[0].rearrange("(q e) (p c) f -> q p e c f", e=QUAD, c=KC)
    w_up_q = w_up[0].rearrange("(q e) (p c) f -> q p e c f", e=QUAD, c=KC)
    w_down_q = w_down[0].rearrange("(q e) (c p) n -> q p e c n", e=QUAD, p=P)
    x_rows = x[0].rearrange("(m p) d -> p m d", p=P)
    out_rows = out[0].rearrange("(m p) d -> p m d", p=P)

    def mslot(j):
        return MORDER[j % MRING]

    def mlanded(eng, j, it):
        s = mslot(j)
        base = 16 * (DENSE // DRING) if s < DRING else 0
        eng.wait_ge(landed[s], it * (16 * QCH // MRING) + base + 16 * (j // MRING + 1))

    def piece_of_ring(c):
        return ring[(c // 8) % DRING][:, (c % 8) * PIECE:(c % 8 + 1) * PIECE]

    block = ctx.enter_context(nc.Block())

    @block.sync
    def _(sp):
        def load_dense(c, n, src, k):
            if n is not None:
                sp.wait_ge(s_wl, n)
            sp.dma_start(ring[c].rearrange("p (k n) -> p k n", k=k), src).then_inc(landed[c], 16)

        sp.dma_start(cst[:], consts).then_inc(s_cst, 16)
        for k in range(2):
            cols = slice(k * 1024, (k + 1) * 1024)
            sp.dma_start(x0[:, :, cols], x_rows[:, :, cols]).then_inc(s_xk[k], 16)
        for c in range(4):
            load_dense(c, None, w_in_c[c, :, :, 0:1024], 4)
        for c in range(4):
            load_dense(c, 8 * (c + 1), w_in_c[c, :, :, 3 * 1024:4 * 1024], 4)
        with sp.Fori(1, TILES_A // 2) as i:
            for par in range(2):
                for c in range(4):
                    load_dense(c, 64 * i + (32 * (par - 1) + 8 * (c + 1)),
                               w_in_c[c, :, :, bass.ds(i * 3072 + (1024 * par - 2048), 1024)], 4)
        with sp.Fori(0, H // 2) as i:
            for c in range(4):
                load_dense(c, 32 * i + (G_B - PT + 8 * (c + 1)),
                           w_gt_c[c % 2, :, :, bass.ds(i * 1024 + (6 * 1024 + 512 * (c // 2)), 512)], 8)
        for t in range(2):
            for c in range(4):
                load_dense(c, 32 * t + (G_C - PT + 8 * (c + 1)),
                           w_br_c[c // 2][c % 2, :, :, t * 1024:(t + 1) * 1024], 4)
        for t in range(2):
            for c in range(4):
                load_dense(c, 32 * t + (G_D - PT + 8 * (c + 1)),
                           w_out_c[c, :, :, t * 1024:(t + 1) * 1024], 4)

        def load_quad(it, q, first=False):
            for j in range(QCH):
                if not first or j >= MRING:
                    sp.wait_ge(s_used, it * QCH + (j + 1))
                elif j < 2:
                    sp.wait_ge(s_gd, 1)
                elif j < 6:
                    sp.wait_ge(s_wl, G_D + PT + 8 * (j - 1))
                elif j == 6:
                    sp.wait_ge(s_pu, G_D + 2 * PT + AHEAD)
                else:
                    sp.wait_ge(s_acc, 2)
                dst = ring[mslot(j)].rearrange("p (e n) -> p e n", e=QUAD)
                if j < 16:
                    w, kp = (w_gate_q, w_up_q)[j % 2], j // 2
                    src = w[bass.ds(q, 1), :, :, 2 * kp:2 * kp + 2, :].rearrange("q p e c f -> p (q e) (c f)")
                else:
                    nh, c = (j - 16) // 4, (j - 16) % 4
                    src = w_down_q[bass.ds(q, 1), :, :, c, nh * 1024:nh * 1024 + 1024].rearrange(
                        "q p e n -> p (q e) n")
                sp.dma_start(dst, src).then_inc(landed[mslot(j)], 16)

        load_quad(0, 0, first=True)
        with sp.Fori(1, NQ - 1) as it:
            load_quad(it, it)
        sp.wait_ge(s_steps, 1)
        n = sp.value_load(steps_i[0:1, 0:1], min_val=NQ, max_val=NQ * (T // SLOTS))
        with sp.Fori(NQ - 1, n) as it:
            load_quad(it, it % NQ)
        for n, (m, k) in enumerate(OUT_ORDER):
            sp.wait_ge(s_out, n + 1)
            cols = slice(k * 1024, (k + 1) * 1024)
            sp.dma_start(out_rows[:, m, cols], outS[:, m, cols]).then_inc(s_store, 16)
        sp.wait_ge(s_store, 16 * len(OUT_ORDER))

    @block.gpsimd
    def _(pool):
        pool.dma_start(gain[:], mix_g[0:1, :].to_broadcast([P, D])).then_inc(s_gain, 16)
        for v, lv in enumerate((lq1, lk1, lq2, lk2)):
            pool.dma_start(lamv[:, v, :], lv[0:1, :].to_broadcast([P, HD])).then_inc(s_small, 16)
        pool.dma_start(gsub, sub_g[0:1, :].to_broadcast([P, P])).then_inc(s_small, 16)
        pool.dma_start(g16[:], ffn_g[0].rearrange("(c p) -> c p", p=P)).then_inc(s_small, 16)
        pool.dma_start(wr[:, :, 0:G], w_gr[0].rearrange("(c p) g -> p c g", p=P)).then_inc(s_small, 16)
        pool.dma_start(wr[:, :, G:G + E], w_er[0].rearrange("(c p) g -> p c g", p=P)).then_inc(s_small, 16)
        pool.memset(wr[:, :, G + E:], 0.0).then_inc(s_set, 1)
        pool.wait_ge(s_h, 4)
        pool.dma_start(gain[:], ffn_g[0:1, :].to_broadcast([P, D])).then_inc(s_gain, 16)
        pool.wait_ge(s_fd, 2 + TILES_A - 1)
        pool.wait_ge(s_fa, 2 + TILES_A - 1)
        pool.wait_ge(s_roped, 2)
        with pool.Fori(0, H) as h:
            pool.wait_ge(s_tsb, h + 1)
            for w, r in enumerate((R_QSB, R_KSB)):
                ins = pool.tensor_copy(qk_sb[:, w].rearrange("p m d -> p (m d)"),
                                       proj[:, r, bass.ds(h, 1), :, :].rearrange("p h m d -> p (h m d)"))
                ins.then_inc(s_hsb, 1)
            pool.wait_ge(s_tda, h + 1)
            for w, r in enumerate((R_QDA, R_KDA)):
                ins = pool.tensor_copy(qk_da[:, w].rearrange("p m d -> p (m d)"),
                                       proj[:, r, bass.ds(h, 1), :, :].rearrange("p h m d -> p (h m d)"))
                ins.then_inc(s_hda, 1)
            pool.wait_ge(s_osb, h + 1)
            pool.tensor_copy(v_sb.rearrange("p m d -> p (m d)"),
                             proj[:, R_VSB, bass.ds(h, 1), :, :].rearrange(
                                 "p h m d -> p (h m d)")).then_inc(s_hv, 1)
        pool.wait_ge(s_xl, 16)
        pool.dma_start(xr, x_rows).then_inc(s_xr, 16)
        pool.wait_ge(s_gain, 32)
        pool.wait_ge(s_pu, G_D + 2 * PT + AHEAD)
        for k in range(2):
            pool.wait_ge(s_x2, 4 * k + 4)
            for m in range(TB):
                cols = slice(k * 1024, (k + 1) * 1024)
                pool.tensor_tensor(h2[:, m, :, k * HD:(k + 1) * HD].rearrange("q c p -> q p c"),
                                   xr[:, m, cols].rearrange("q (p c) -> q p c", c=KC),
                                   gain[:, cols].rearrange("q (p c) -> q p c", c=KC), ALU.mult).then_inc(s_h2, 1)
        pool.wait_ge(s_h2, 4)
        pool.dma_start(gain[:], fin_g.rearrange("(a d) -> a d", a=1).to_broadcast([P, D])).then_inc(s_gain, 16)

    @block.tensor
    def _(pe):
        for s in (s_tsb, s_tda, s_osb):
            pe.sem_inc(s, 1)
        pe.sem_inc(s_pu, AHEAD)
        pe.sem_inc(s_used, MRING)

        def turn_rows(src, j, bank):
            for k in range(2):
                for m in range(TB):
                    c = 2 * j + k
                    mm = pe.transpose(ps[:, bank, (2 * k + m) * P:(2 * k + m + 1) * P],
                                      src[:, m, c * P:(c + 1) * P], ident)
            mm.then_inc(s_turned, 1)

        def piece(i, c, kc, banks, start, stop):
            pe.wait_ge(s_wl, i * PT + (c + 1))
            b = c % AHEAD
            for m in range(TB):
                o, cols = ps[:, banks[m], :], slice(m * P, (m + 1) * P)
                pe.matmul(o, xH[:, kc, cols], wH[b], start=start, stop=False)
                pe.matmul(o, xL[:, kc, cols], wH[b], start=False, stop=False)
                mm = pe.matmul(o, xH[:, kc, cols], wL[b], start=False, stop=stop)
            mm.then_inc(s_pu, 1)

        pe.wait_ge(s_cst, 16)
        for j in range(4):
            if j % 2 == 0:
                pe.wait_ge(s_h, j // 2 + 1)
            turn_rows(h0, j, 4 + j)
        for c in range(PT):
            if c % 4 == 0:
                pe.wait_ge(s_xl, c // 4 + 1)
            if c in (4, 6, 8, 10):
                j = 4 + (c - 4) // 2
                pe.wait_ge(s_h, j // 2 + 1)
                pe.wait_ge(s_xl, j - 3)
                turn_rows(h0, j, j)
            if c == 20:
                pe.wait_ge(s_small, 16 * 8)
                pe.wait_ge(s_xl, 8)
                pe.transpose(ps[:, 7, 0:KC], g16[:], ident[0:KC, 0:KC]).then_inc(s_gt, 1)
            piece(0, c, c // 2, (c % 2, c % 2 + 2), c < 2, c >= PT - 2)
        pe.wait_ge(s_wr, 1)

        def a_tile(t, par):
            for c in range(PT):
                bank = 4 * par + c % 2
                piece(t, c, c // 2, (bank, bank + 2), c < 2, c >= PT - 2)

        a_tile(1, 1)
        with pe.Fori(1, TILES_A // 2) as i:
            for par in range(2):
                pe.wait_ge(s_fd, 2 * i + (par + 1))
                pe.wait_ge(s_fa, 2 * i + (par + 1))
                a_tile(2 * i + par, par)

        def turn_sb(h):
            pe.wait_ge(s_hsb, 2 * h + 2)
            pe.wait_ge(s_ost, h + 1)
            for w in range(2):
                for m in range(TB):
                    mm = pe.transpose(ps[:, 4, (2 * w + m) * P:(2 * w + m + 1) * P], qk_sb[:, w, m, :], ident)
            mm.then_inc(s_tsb, 1)

        def turn_da(h):
            pe.wait_ge(s_hda, 2 * h + 2)
            pe.wait_ge(s_oS, h + 1)
            for w in range(2):
                for m in range(TB):
                    mm = pe.transpose(ps[:, 7, (2 * w + m) * P:(2 * w + m + 1) * P], qk_da[:, w, m, :], ident)
            mm.then_inc(s_tda, 1)

        def head(i, par, last=False):
            h = 2 * i + par

            def gate_piece(p, par=par, i=i):
                piece(i + TILES_A, 16 * par + p, p % 16, (2 * (par % 2), 2 * (par % 2) + 1),
                      p == 0, p == KC - 1)

            gate_piece(2)
            pe.wait_ge(s_kd, h + 1)
            pe.matmul(ps[:, 4, 0:256], qkT_sb[:, 1, 0:P], qkT_sb[:, 0, :], start=True, stop=True)
            pe.matmul(ps[:, 4, 0:128], ident16[:], mask16[:, 0, :], start=False, stop=True,
                      skip_group_check=True)
            pe.matmul(ps[:, 4, 256:384], qkT_sb[:, 1, P:T], qkT_sb[:, 0, P:T], start=True, stop=True,
                      skip_group_check=True)
            pe.matmul(ps[:, 4, 256:384], ident16[:], mask16[:, 0, :], start=False, stop=True,
                      skip_group_check=True).then_inc(s_z, 1)
            gate_piece(3)
            pe.wait_ge(s_ka, h + 1)
            pe.wait_ge(s_odt, h + 1)
            for mp in range(2):
                r = slice(HD * mp, HD * mp + HD)
                pe.matmul(ps[:, 5 + mp, 0:128], qkT_da[r, 0, 0:P], qkT_da[r, 1, 0:P], start=True, stop=True)
                pe.matmul(ps[:, 5 + mp, 0:128], ident16[:], mask16[:, 1, :], start=False, stop=True,
                          skip_group_check=True)
                pe.matmul(ps[:, 5 + mp, 128:384], qkT_da[r, 0, P:T], qkT_da[r, 1, :], start=True, stop=True,
                          skip_group_check=True)
                mm = pe.matmul(ps[:, 5 + mp, 256:384], ident16[:], mask16[:, 1, :], start=False, stop=True,
                               skip_group_check=True)
            mm.then_inc(s_sc, 1)
            for p in range(4, 8):
                gate_piece(p)
            pe.wait_ge(s_L, h + 1)
            pe.matmul(ps[:, 4, 0:256], tri, eS[:, 0:256], start=True, stop=True)
            pe.matmul(ps[:, 4, 128:256], ones, eS[:, 256:384], start=False, stop=True, skip_group_check=True)
            pe.matmul(ps[:, 4, 256:384], tri, eS[:, 256:384], start=True, stop=True,
                      skip_group_check=True).then_inc(s_c, 1)
            for p in range(8, 11):
                gate_piece(p)
            pe.wait_ge(s_at, h + 1)
            for b in range(3):
                mm = pe.transpose(ps[:, 7, b * P:(b + 1) * P], attn[:, b * P:(b + 1) * P], ident)
            mm.then_inc(s_att, 1)
            gate_piece(11)
            pe.wait_ge(s_hv, h + 1)
            pe.wait_ge(s_a, h + 1)
            pe.matmul(ps[:, 4, 0:256], v_sb[:, 0, :], aT[:, 0:256], start=True, stop=True)
            pe.matmul(ps[:, 4, 128:256], v_sb[:, 1, :], aT[:, 256:384], start=False, stop=True,
                      skip_group_check=True).then_inc(s_osb, 1)
            gate_piece(12)
            pe.wait_ge(s_atT, h + 1)

            def v_da(m):
                return proj[:, R_VDA, bass.ds(h, 1), m, :].rearrange("p h d -> p (h d)")

            pe.matmul(ps[:, 7, 0:128], attnT[:, 0:P], v_da(0), start=True, stop=True)
            pe.matmul(ps[:, 7, 128:256], attnT[:, P:2 * P], v_da(0), start=True, stop=True,
                      skip_group_check=True)
            pe.matmul(ps[:, 7, 128:256], attnT[:, 2 * P:3 * P], v_da(1), start=False, stop=True,
                      skip_group_check=True).then_inc(s_oda, 1)
            for p in range(13, 16):
                gate_piece(p)
            if not last:
                turn_sb(h + 1)
                pe.wait_ge(s_ge, h + 2)
                gate_piece(0, (par + 1) % 2, i + (par + 1) // 2)
                turn_da(h + 1)
                gate_piece(1, (par + 1) % 2, i + (par + 1) // 2)
            pe.wait_ge(s_oN, h + 1)
            for m in range(TB):
                mm = pe.transpose(ps[:, 5, m * P:(m + 1) * P], oN[:, m, :], ident)
            mm.then_inc(s_oT, 1)

        pe.wait_ge(s_fd, 2 + TILES_A - 1)
        pe.wait_ge(s_fa, 2 + TILES_A - 1)
        piece(TILES_A, 0, 0, (0, 1), True, False)
        piece(TILES_A, 1, 1, (0, 1), False, False)
        pe.wait_ge(s_fd, 2 + TILES_A)
        pe.wait_ge(s_fa, 2 + TILES_A)
        pe.wait_ge(s_set, 2)
        turn_sb(0)
        turn_da(0)
        with pe.Fori(0, H // 2 - 1) as i:
            head(i, 0)
            head(i, 1)
        head(H // 2 - 1, 0)
        head(H // 2 - 1, 1, last=True)

        pe.wait_ge(s_ge, H + 2)
        for t in range(2):
            for c in range(PT):
                if t == 0 and c % 4 == 0:
                    pe.wait_ge(s_xl, 8 + c // 4 + 1)
                if t == 0 and c == 16:
                    pe.wait_ge(s_odt, H + 1)
                if t == 1 and c == 0:
                    pe.wait_ge(s_At, 1)
                if t == 1 and c == 16:
                    pe.wait_ge(s_Bt, 1)
                bank = 4 * (c // 16) + c % 2
                piece(10 + t, c, c // 2, (bank, bank + 2), c % 16 < 2, c % 16 >= 14)
                if t == 1 and c == 23:
                    pe.wait_ge(s_At, 2)
                if t == 1 and 23 <= c < 31 and c % 2 == 1:
                    turn_rows(merged, (c - 23) // 2, (c - 23) // 2)
        def turn_x2(j, bank):
            for k in range(2):
                for m in range(TB):
                    c = 2 * j + k
                    mm = pe.transpose(ps[:, bank, (2 * k + m) * P:(2 * k + m + 1) * P],
                                      xr[:, m, c * P:(c + 1) * P], ident)
            mm.then_inc(s_x2t, 1)

        def logits(half, bank):
            for k in range(4):
                for g in range(2):
                    c = 8 * half + 2 * k + g
                    mm = pe.matmul(ps[RC * g:RC * g + RC, bank, 0:T], wr[:, c, :], x2T[:, c, :],
                                   start=(k == 0), stop=(k == 3), skip_group_check=True)
            mm.then_inc(s_acc, 1)

        for t in range(2):
            for c in range(PT):
                if t == 0 and c % 4 == 0:
                    pe.wait_ge(s_xl, 16 + max(c // 4 + 1, 4))
                if t == 0 and c in (4, 6, 8, 10):
                    j = 4 + (c - 4) // 2
                    if j == 4:
                        pe.wait_ge(s_Bt, 2)
                    turn_rows(merged, j, j)
                if t == 1 and c == 12:
                    pe.wait_ge(s_x2, 4)
                    for j in range(4):
                        turn_x2(j, j)
                if t == 1 and c == 22:
                    pe.wait_ge(s_2d, 2)
                    pe.wait_ge(s_2a, 2)
                    logits(0, 3)
                bank = 4 * t + c % 2
                piece(12 + t, c, c // 2, (bank, bank + 2), c < 2, c >= PT - 2)
        for n in range(2):
            pe.wait_ge(s_x2, 4 + 2 * n + 2)
            for j in range(2):
                turn_x2(4 + 2 * n + j, 2 * n + j if n == 0 else 2 + 2 * j)
        pe.wait_ge(s_2d, 4)
        pe.wait_ge(s_2a, 4)
        logits(1, 5)
        pe.wait_ge(s_accS, 1)
        for m in range(TB):
            mm = pe.matmul(ps[:, m, 0:G + E], accS[:, m * P:(m + 1) * P], cst[:, C_ST:], start=True, stop=True)
        mm.then_inc(s_log, 1)
        pe.wait_ge(s_took, 1)
        pe.matmul(ps[:, 2, 0:E], prev, took[:, 0, :], start=True, stop=True)
        pe.matmul(ps[:, 2, E:2 * E], prev, took[:, 1, :], start=True, stop=True, skip_group_check=True)
        pe.matmul(ps[:, 2, E:2 * E], ones, took[:, 0, :], start=False, stop=True, skip_group_check=True)
        pe.matmul(ps[:, 2, 2 * E:3 * E], ones, took[:, 0, :], start=True, stop=True, skip_group_check=True)
        pe.matmul(ps[:, 2, 2 * E:3 * E], ones, took[:, 1, :], start=False, stop=True,
                  skip_group_check=True).then_inc(s_rank, 1)
        pe.wait_ge(s_h2, 4)
        pe.wait_ge(s_steps, 1)
        n_steps = pe.value_load(steps_i[0:1, 0:1], min_val=NQ, max_val=NQ * (T // SLOTS))
        with pe.Fori(0, n_steps) as it:
            def gather(b):
                for k in range(4):
                    for m in range(TB):
                        mm = pe.matmul(ps[:, 4 + b, k * P:(k + 1) * P], h2[:, m, 4 * b + k, :], selG[:, m, :],
                                       start=(m == 0), stop=(m == 1), skip_group_check=True)
                mm.then_inc(s_gath, 1)

            pe.wait_ge(s_sel, it + 1)
            pe.wait_ge(s_yd, 2 * it + 1)
            pe.wait_ge(s_ya, 2 * it + 1)
            gather(0)
            gather(1)
            for j in range(16):
                if j % 4 == 0:
                    pe.wait_ge((s_xd, s_xa)[j // 4 % 2], 2 * it + (j // 8 + 1))
                if j in (4, 8):
                    gather(j // 4 + 1)
                mlanded(pe, j, it)
                for c in range(2):
                    kc = 2 * (j // 2) + c
                    for e in range(QUAD):
                        mm = pe.matmul(ps[SLOTS * e:SLOTS * e + SLOTS, j % 2, :],
                                       xgT[:, kc, SLOTS * e:SLOTS * e + SLOTS],
                                       ring[mslot(j)][:, e * 1024 + c * 512:e * 1024 + c * 512 + 512],
                                       start=(kc == 0), stop=(kc == KC - 1))
                mm.then_inc(s_used, 1)
            pe.wait_ge(s_add, 8 * it + 4)
            pe.wait_ge(s_shr, it + 1)
            for m in range(TB):
                mm = pe.transpose(ps[:, 2, m * P:(m + 1) * P], selW[:, m, :, :].rearrange("p e s -> p (e s)"),
                                  ident)
            mm.then_inc(s_swt, 1)
            pe.wait_ge(s_hS, it + 1)
            for f in range(4):
                mm = pe.transpose(ps[:, 0, f * P:(f + 1) * P], hidden[:, f * P:(f + 1) * P], ident)
            mm.then_inc(s_ht, 1)
            pe.wait_ge(s_hT, it + 1)
            for nh in range(2):
                for c in range(4):
                    j = 16 + 4 * nh + c
                    mlanded(pe, j, it)
                    for n in range(2):
                        for e in range(QUAD):
                            a = e * 1024 + n * 512
                            mm = pe.matmul(ps[SLOTS * e:SLOTS * e + SLOTS, 4 + 2 * nh + n, :],
                                           hT4[:, c * P + SLOTS * e:c * P + SLOTS * e + SLOTS],
                                           ring[mslot(j)][:, a:a + 512], start=(c == 0), stop=(c == 3))
                    mm.then_inc(s_used, 1)
            pe.wait_ge(s_sw, it + 1)
            for nh in range(2):
                pe.wait_ge(s_yd, 2 * it + (nh + 2))
                pe.wait_ge(s_ya, 2 * it + (nh + 2))
                for n in range(2):
                    for m in range(TB):
                        k = 4 * nh + 2 * n + m
                        if k >= 2:
                            pe.wait_ge(s_add, 8 * it + (k + 3))
                        pe.matmul(ps[:, 2 + m, :], selWT[:, m * P:(m + 1) * P],
                                  yS[:, (2 * nh + n) * 512:(2 * nh + n + 1) * 512],
                                  start=True, stop=True).then_inc(s_comb, 1)

    def rsqrt_dve(dve, link, dst, src, scale, n):
        dve.tensor_scalar(rv, src, scale, EPS, ALU.mult, ALU.add).then_inc(s_v, 1)
        dve.wait_ge(s_v, n)
        dve.wait_ge(s_y0, n)
        link(dve.tensor_tensor(rq, rv, ry, ALU.mult))
        link(dve.tensor_tensor(rq, rq, ry, ALU.mult))
        link(dve.tensor_scalar(rq, rq, -0.5, 1.5, ALU.mult, ALU.add))
        dve.tensor_tensor(dst, rq, ry, ALU.mult).then_inc(s_rs, 1)
        dve.wait_ge(s_rs, n)

    def rsqrt_act(act, link, n):
        act.wait_ge(s_v, n)
        link(act.activation(ry, rv, ACT.Ln))
        act.activation(ry, ry, ACT.Exp, scale=-0.5).then_inc(s_y0, 1)

    @block.vector
    def _(dve):
        ch = Chain(dve, s_dve)
        link = ch.link
        for s in (s_ost, s_yd):
            dve.sem_inc(s, 1)
        dve.sem_inc(s_add, 4)
        dve.memset(one_c, 1.0).then_inc(s_set, 1)

        def rest(i, c):
            dve.wait_ge(s_wh, i * PT + (c + 1))
            b = c % AHEAD
            dve.tensor_tensor(wL[b], piece_of_ring(c), wH[b].bitcast(F32), ALU.subtract).then_inc(s_wl, 1)

        def x_rest(n, src, j):
            dve.wait_ge(s_xh, n + 1)
            cols = slice(j * PIECE, (j + 1) * PIECE)
            return dve.tensor_tensor(split[:, SLOT + j * PIECE:SLOT + (j + 1) * PIECE], src,
                                     split[:, cols].bitcast(F32), ALU.subtract).then_inc(s_xl, 1)

        def times_gain(k):
            cols = slice(k * PIECE, (k + 1) * PIECE)
            dve.tensor_tensor(h0[:, :, cols], x0[:, :, cols],
                              gain[:, cols].unsqueeze(1).to_broadcast([P, TB, PIECE]), ALU.mult).then_inc(s_h, 1)

        dve.wait_ge(s_gain, 16)
        dve.wait_ge(s_xk[0], 16)
        times_gain(0)
        times_gain(1)
        x_rest(0, ps[:, 4, :], 0)
        x_rest(1, ps[:, 5, :], 1)
        rest(0, 0)
        rest(0, 1)
        dve.wait_ge(s_xk[1], 16)
        times_gain(2)
        x_rest(2, ps[:, 6, :], 2)
        rest(0, 2)
        rest(0, 3)
        times_gain(3)
        x_rest(3, ps[:, 7, :], 3)
        for j in range(4, 8):
            for c in (2 * j - 4, 2 * j - 3):
                rest(0, c)
            x_rest(j, ps[:, j, :], j)
        link(dve.tensor_tensor_reduce(squares[:, 1, :], x0[:, 1, :], x0[:, 1, :], 1.0, 0.0, ALU.mult, ALU.add,
                                      ss[:, 1:2]))
        dve.wait_ge(s_ssq, 1)
        rsqrt_dve(dve, link, rs, ss, 1.0 / D, 1)
        dve.sem_inc(s_fd, 2)
        dve.wait_ge(s_cst, 16)
        link(dve.tensor_copy(ident16[:], ident))
        link(dve.tensor_copy(mask16[:], cst[:, C_MSB:C_MSB + 2 * P].rearrange("p (a b) -> p a b", a=2)))

        def take_tile(t):
            dve.wait_ge(s_pu, t * PT + (PT + AHEAD))
            dve.tensor_scalar(proj[:, bass.ds(t, 1), :, 0, :].rearrange("p r h d -> p (r h) d"),
                              ps[:, bass.ds((t % 2) * 4, 2), :].rearrange("p b (h d) -> p (b h) d", d=P),
                              rs[:, 0:1], None, ALU.mult).then_inc(s_fd, 1)

        for c in range(12, PT + AHEAD):
            rest(0, c)
            if c == 26:
                dve.wait_ge(s_gt, 1)
                link(dve.tensor_copy(gT[:], ps[:, 7, 0:KC]))
                dve.tensor_tensor(wr[:, :, 0:G + E], wr[:, :, 0:G + E],
                                  gT[:].unsqueeze(2).to_broadcast([P, KC, G + E]), ALU.mult).then_inc(s_wr, 1)
        take_tile(0)
        with dve.Fori(1, TILES_A - 1) as t:
            for c in range(AHEAD, PT + AHEAD):
                rest(t, c)
            take_tile(t)
        cosB = cosH.unsqueeze(1).to_broadcast([P, H, 4, HD // 2])
        sinB = sinH.unsqueeze(1).to_broadcast([P, H, 4, HD // 2])

        def rope_steps(r):
            qk = at(B_P + r * 2048, 2048).rearrange("p (b s a f) -> p b s a f", b=H, s=4, a=2)
            lo, hi = qk[:, :, :, 0, :], qk[:, :, :, 1, :]
            return [(rope_u, hi, sinB, ALU.mult), (rope_v, lo, sinB, ALU.mult), (lo, lo, cosB, ALU.mult),
                    (hi, hi, cosB, ALU.mult), (lo, lo, rope_u, ALU.subtract), (hi, hi, rope_v, ALU.add)]

        dve.wait_ge(s_small, 16 * 8)
        for v in range(2):
            link(dve.tensor_tensor_reduce(lamv[:, 2 * v, :], lamv[:, 2 * v, :], lamv[:, 2 * v + 1, :], 1.0, 0.0,
                                          ALU.mult, ALU.add, lam4[:, v:v + 1]))
        dve.tensor_copy(lamE, lam4).then_inc(s_lam, 1)
        dve.wait_ge(s_lamE, 1)
        link(dve.tensor_tensor(neglam, lam4[:, 1:2], lam4[:, 0:1], ALU.subtract))
        link(dve.tensor_scalar(neglam, neglam, -LAM_INIT, None, ALU.add))
        dve.wait_ge(s_fa, 2 + TILES_A - 1)
        dve.wait_ge(s_fd, 2 + TILES_A - 1)
        rope = rope_steps(R_QDA) + rope_steps(R_KDA)
        for c in range(AHEAD, PT + AHEAD):
            rest(TILES_A - 1, c)
            if c % 2 == 1 and rope:
                step = rope.pop(0)
                ins = dve.tensor_tensor(*step)
                if len(rope) in (0, 6):
                    ins.then_inc(s_roped, 1)
                else:
                    link(ins)
        take_tile(TILES_A - 1)

        def head(i, par):
            h = 2 * i + par
            dve.wait_ge(s_tsb, h + 2)
            link(dve.tensor_scalar(qkT_sb[:, 0, :], ps[:, 4, 0:256], float(P) ** -0.5, None, ALU.mult))
            dve.tensor_copy(qkT_sb[:, 1, :], ps[:, 4, 256:512]).then_inc(s_kd, 1)
            for p in range(4, 20):
                rest(i + TILES_A, 16 * par + p)
                if p == 8:
                    dve.wait_ge(s_sc, h + 1)
                    link(dve.tensor_reduce(mx[:, 0:2], ps[:, 5:7, 0:128], AX.X, ALU.max))
                    link(dve.tensor_reduce(mx[:, 2:4], ps[:, 5:7, 128:384], AX.X, ALU.max))
                    dve.tensor_scalar(nmx, mx, -1.0, None, ALU.mult).then_inc(s_mx, 1)
                if p == 9:
                    dve.wait_ge(s_l, h + 1)
                    dve.scalar_tensor_tensor(eS, zS, 0.0, lS, ALU.max, ALU.add).then_inc(s_L, 1)
                if p == 11:
                    dve.wait_ge(s_p, h + 1)
                    link(dve.reciprocal(rsm, sm))
                    rsm2 = rsm.rearrange("p (q a) -> p q a", a=2)
                    link(dve.tensor_scalar(rsn.rearrange("p (q a) -> p q a", a=1), rsm2[:, :, 1:2], neglam, None,
                                           ALU.mult))
                    for q, cols in enumerate((slice(0, 128), slice(128, 384))):
                        link(dve.tensor_scalar(attn[:, cols], pS[:, 0, cols], rsm[:, 2 * q:2 * q + 1], None,
                                               ALU.mult))
                    link(dve.scalar_tensor_tensor(attn[:, 0:128], pS[:, 1, 0:128], rsn[:, 0:1], attn[:, 0:128],
                                                  ALU.mult, ALU.add))
                    dve.scalar_tensor_tensor(attn[:, 128:384], pS[:, 1, 128:384], rsn[:, 1:2],
                                             attn[:, 128:384], ALU.mult, ALU.add).then_inc(s_at, 1)
                if p == 12:
                    dve.wait_ge(s_c, h + 1)
                    dve.tensor_tensor(zS, zS, ps[:, 4, 0:384], ALU.subtract).then_inc(s_zc, 1)
                if p == 15:
                    dve.wait_ge(s_att, h + 1)
                    dve.tensor_copy(attnT, ps[:, 7, 0:384]).then_inc(s_atT, 1)
                if p == 16:
                    dve.wait_ge(s_osb, h + 2)
                    dve.tensor_copy(oT[:, bass.ds(h, 1), :].rearrange("p h t -> p (h t)"),
                                    ps[:, 4, 0:256]).then_inc(s_ost, 1)
                if p == 18:
                    dve.wait_ge(s_oS, h + 2)
                    for m in range(TB):
                        link(dve.tensor_tensor_reduce(sq, oS[:, m, :], oS[:, m, :], 1.0, 0.0, ALU.mult,
                                                      ALU.add, oss[:, m:m + 1]))
                    dve.tensor_scalar(rv, oss, 1.0 / P, EPS, ALU.mult, ALU.add).then_inc(s_v, 1)
            root(h + 2, ors)
            link(dve.tensor_scalar(ors, ors, 1.0 - LAM_INIT, None, ALU.mult))
            link(dve.scalar_tensor_tensor(oN[:, 0, :], oS[:, 0, :], ors[:, 0:1], gsub, ALU.mult, ALU.mult))
            dve.scalar_tensor_tensor(oN[:, 1, :], oS[:, 1, :], ors[:, 1:2], gsub, ALU.mult,
                                     ALU.mult).then_inc(s_oN, 1)

        def root(n, dst):
            dve.wait_ge(s_v, n)
            dve.wait_ge(s_y0, n)
            link(dve.tensor_tensor(rq, rv, ry, ALU.mult))
            link(dve.tensor_tensor(rq, rq, ry, ALU.mult))
            link(dve.tensor_scalar(rq, rq, -0.5, 1.5, ALU.mult, ALU.add))
            dve.tensor_tensor(dst, rq, ry, ALU.mult).then_inc(s_rs, 1)
            dve.wait_ge(s_rs, n)

        n0, per = ch.n, 2 * 15
        with dve.Fori(0, H // 2) as i:
            ch.off = i * per
            head(i, 0)
            head(i, 1)
        assert ch.n - n0 == per, ch.n - n0
        ch.n, ch.off = n0 + per * H // 2, 0

        def gate(t, br, m):
            g = gates[:, :, 4 * br + 2 * t:4 * br + 2 * t + 2, m, :]
            return g.rearrange("p r h d -> p h r d")

        def branch(ap):
            return ap.rearrange("p (h r d) -> p h r d", h=2, r=4)

        def take_a(t, m):
            dve.wait_ge(s_pu, G_C + t * PT + 16 + AHEAD)
            dve.wait_ge(s_sig, 2 * t + 1)
            src = ps[:, 2 * m:2 * m + 2, :].rearrange("p b (r d) -> p b r d", r=4)
            ins = dve.tensor_tensor(branch(merged[:, m, t * 1024:(t + 1) * 1024]), src, gate(t, 0, m), ALU.mult)
            if m == 0:
                link(ins)
            else:
                ins.then_inc(s_At, 1)

        def take_b(t, m, step):
            if step == 0:
                dve.wait_ge(s_pu, G_C + (t + 1) * PT + AHEAD)
                dve.wait_ge(s_sig, 2 * t + 2)
                src = ps[:, 4 + 2 * m:6 + 2 * m, :].rearrange("p b (r d) -> p b r d", r=4)
                link(dve.tensor_tensor(branch(part), src, gate(t, 1, m), ALU.mult))
            else:
                mg = merged[:, m, t * 1024:(t + 1) * 1024]
                ins = dve.tensor_tensor(mg, mg, part, ALU.add)
                if m == 0:
                    link(ins)
                else:
                    ins.then_inc(s_Bt, 1)

        for j in range(2):
            x_rest(8 + j, oT[:, 2 * j:2 * j + 2, :].rearrange("p c t -> p (c t)"), j)
        for t in range(2):
            for c in range(AHEAD, PT + AHEAD):
                rest(10 + t, c)
                if t == 0 and c % 2 == 0 and 2 <= c // 2 < 8:
                    j = c // 2
                    x_rest(8 + j, oT[:, 2 * j:2 * j + 2, :].rearrange("p c t -> p (c t)"), j)
                if c in (19, 21):
                    take_a(t, (c - 19) // 2)
                if t == 1 and 4 <= c < 12 and c % 2 == 0:
                    take_b(0, (c - 4) // 4, (c - 4) // 2 % 2)
                if t == 1 and c >= 29 and c % 2 == 1 and (c - 29) // 2 < 4:
                    j = (c - 29) // 2
                    x_rest(16 + j, ps[:, j, :], j)
        for m in range(TB):
            for step in range(2):
                take_b(1, m, step)
        dve.wait_ge(s_Bt, 2)
        dve.memset(cell[:, 40:41], 0.0).then_inc(s_gd, 1)

        def add_out(t, n, m):
            xs = xr[:, m, t * 1024 + n * 512:t * 1024 + (n + 1) * 512]
            dve.tensor_tensor(xs, xs, ps[:, 4 * t + 2 * m + n, :], ALU.add).then_inc(s_x2, 1)

        for t in range(2):
            for c in range(AHEAD, PT + (AHEAD if t == 0 else 0)):
                rest(12 + t, c)
                if t == 0 and c in (8, 10, 12, 14):
                    j = 4 + (c - 8) // 2
                    x_rest(16 + j, ps[:, j, :], j)
                if t == 1 and 4 <= c < 8:
                    dve.wait_ge(s_xr, 16)
                    dve.wait_ge(s_pu, G_D + PT + AHEAD)
                    add_out(0, (c - 4) // 2, c % 2)
                if t == 1 and c in (18, 20):
                    j = c - 18
                    dve.wait_ge(s_x2t, j + 1)
                    dve.tensor_copy(x2T[:, 2 * j:2 * j + 2, :].rearrange("p c t -> p (c t)"),
                                    ps[:, j, :]).then_inc(s_2d, 1)
        dve.wait_ge(s_pu, G_D + 2 * PT + AHEAD)
        for n in range(2):
            for m in range(TB):
                add_out(1, n, m)
        dve.wait_ge(s_acc, 1)
        link(dve.tensor_copy(accS, ps[:, 3, 0:T]))
        for j, bank in ((4, 0), (6, 2)):
            dve.wait_ge(s_x2t, j + 1)
            dve.tensor_copy(x2T[:, 2 * j:2 * j + 2, :].rearrange("p c t -> p (c t)"),
                            ps[:, bank, :]).then_inc(s_2d, 1)
        dve.wait_ge(s_acc, 2)
        dve.tensor_tensor(accS, accS, ps[:, 5, 0:T], ALU.add).then_inc(s_accS, 1)
        dve.wait_ge(s_sq2, 1)
        link(dve.tensor_tensor(ss, ssA, ssB, ALU.add))
        rsqrt_dve(dve, link, rs, ss, 1.0 / D, H + 2)
        link(dve.memset(lg[:, :, G:8], -3.0e38))
        def issue(ins):
            ch.n += 1
            ins.then_inc(s_dve, 1)

        def join():
            dve.wait_ge(s_dve, ch.n)

        rt4 = rt.rearrange("p (a m) -> p a m", m=TB)
        neg_gm, gsum, pg = rt4[:, 0, :], rt4[:, 1, :], rt4[:, 2, :]
        gap, dexp, base, w1, w2, e1, e2 = (rt4[:, 3 + i, :] for i in range(7))
        iota_g = cst[:, C_IOTA:C_IOTA + G]
        iota_e = cst[:, C_IOTA:C_IOTA + E]

        def col(a):
            return a.unsqueeze(2)

        def over(a, n):
            return a.unsqueeze(2).to_broadcast([P, TB, n])

        def both(a, n):
            return a.unsqueeze(1).to_broadcast([P, TB, n])

        dve.wait_ge(s_log, 1)
        for m in range(TB):
            issue(dve.tensor_scalar(lg[:, m, 0:G], ps[:, m, 0:G], rs[:, m:m + 1], None, ALU.mult))
            issue(dve.tensor_scalar(lg[:, m, 8:8 + E], ps[:, m, G:G + E], rs[:, m:m + 1], None, ALU.mult))
        join()
        for m in range(TB):
            issue(dve.max(gm8[:, m, :], lg[:, m, 0:8]))
        join()
        for m in range(TB):
            issue(dve.max_index(gi8[:, m, :], gm8[:, m, :], lg[:, m, 0:8]))
        dve.tensor_scalar(col(neg_gm), gm8[:, :, 0:1], -1.0, None, ALU.mult).then_inc(s_gm, 1)
        join()
        link(dve.tensor_copy(gi8f, gi8))
        issue(dve.tensor_tensor(goh, both(iota_g, G), gi8f[:, :, 0:1].to_broadcast([P, TB, G]), ALU.is_equal))
        issue(dve.tensor_scalar(col(base), gi8f[:, :, 0:1], float(EPG), None, ALU.mult))
        join()
        for m in range(TB):
            issue(dve.tensor_tensor(picked[:, m, :].rearrange("p (g j) -> p g j", g=G),
                                    lg[:, m, 8:8 + E].rearrange("p (g j) -> p g j", g=G),
                                    goh[:, m, :].unsqueeze(2).to_broadcast([P, G, EPG]), ALU.mult))
        join()
        link(dve.tensor_reduce(esel, picked.rearrange("p m (g j) -> p m j g", g=G), AX.X, ALU.add))
        for m in range(TB):
            issue(dve.max(ev8[:, m, :], esel[:, m, :]))
        join()
        for m in range(TB):
            issue(dve.max_index(ei8[:, m, :], ev8[:, m, :], esel[:, m, :]))
        dve.tensor_tensor(col(gap), ev8[:, :, 1:2], ev8[:, :, 0:1], ALU.subtract).then_inc(s_dd, 1)
        join()
        link(dve.tensor_copy(ei8f, ei8))
        issue(dve.tensor_tensor(col(e1), col(base), ei8f[:, :, 0:1], ALU.add))
        issue(dve.tensor_tensor(col(e2), col(base), ei8f[:, :, 1:2], ALU.add))
        join()
        issue(dve.tensor_tensor(oh1, both(iota_e, E), over(e1, E), ALU.is_equal))
        issue(dve.tensor_tensor(oh2, both(iota_e, E), over(e2, E), ALU.is_equal))
        join()
        dve.tensor_tensor(took, oh1, oh2, ALU.add).then_inc(s_took, 1)
        dve.wait_ge(s_gx, 1)
        issue(dve.reciprocal(pg, gsum))
        dve.wait_ge(s_ex, 1)
        link(dve.tensor_scalar(w1, dexp, 1.0, None, ALU.add))
        link(dve.reciprocal(w1, w1))
        link(dve.tensor_tensor(w1, w1, pg, ALU.mult))
        link(dve.tensor_tensor(w2, w1, dexp, ALU.mult))
        issue(dve.tensor_tensor(oh1, oh1, over(w1, E), ALU.mult))
        issue(dve.tensor_tensor(oh2, oh2, over(w2, E), ALU.mult))
        join()
        issue(dve.tensor_tensor(share, oh1, oh2, ALU.add))
        dve.wait_ge(s_rank, 1)
        issue(dve.tensor_reduce(w1[:, 0:1], ps[:, 2, 2 * E:3 * E], AX.X, ALU.max))
        issue(dve.tensor_scalar(rank, ps[:, 2, 0:2 * E].rearrange("p (m e) -> p m e", m=TB), 4096.0, None, ALU.add))
        join()
        dve.wait_ge(s_took, 1)
        issue(dve.tensor_scalar(count8, cst[:, C_THR:C_THR + 8], w1[:, 0:1], None, ALU.is_lt))
        issue(dve.tensor_tensor(rank, rank, took, ALU.mult))
        join()
        issue(dve.tensor_reduce(w1[:, 1:2], count8, AX.X, ALU.add))
        issue(dve.tensor_scalar(rank, rank, -4096.0, None, ALU.add))
        join()
        dve.tensor_scalar(steps_i[:, 0:1], w1[:, 1:2], float(NQ), float(NQ), ALU.mult, ALU.add).then_inc(s_steps, 1)
        dve.wait_ge(s_steps, 1)
        n_steps = dve.value_load(steps_i[0:1, 0:1], min_val=NQ, max_val=NQ * (T // SLOTS))

        n0 = ch.n
        per_step = 2
        with dve.Fori(0, n_steps) as it:
            ch.off = it * per_step
            q = it % NQ
            rk = rank[:, :, bass.ds(q * QUAD, QUAD)]
            for m in range(TB):
                ins = dve.tensor_tensor(selE[:, m], iota_e.unsqueeze(1).to_broadcast([P, QUAD, SLOTS]),
                                        rk[:, m, :].unsqueeze(2).to_broadcast([P, QUAD, SLOTS]), ALU.is_equal)
                if m == 1:
                    link(ins)
            for m in range(TB):
                ins = dve.tensor_scalar(selG[:, m, :], selE[:, m].rearrange("p e s -> p (e s)"), rs[:, m:m + 1],
                                        None, ALU.mult)
            ins.then_inc(s_sel, 1)
            for m in range(TB):
                ins = dve.tensor_tensor(selW[:, m], selE[:, m],
                                        share[:, m, bass.ds(q * QUAD, QUAD)].unsqueeze(2).to_broadcast(
                                            [P, QUAD, SLOTS]), ALU.mult)
            ins.then_inc(s_shr, 1)
            link(dve.tensor_scalar(rk, rk, -float(SLOTS), None, ALU.add))
            for b in (0, 2):
                dve.wait_ge(s_gath, 4 * it + (b + 1))
                dve.tensor_copy(xgT[:, 4 * b:4 * b + 4, :].rearrange("p c s -> p (c s)"),
                                ps[:, 4 + b, :]).then_inc(s_xd, 1)
            dve.wait_ge(s_swt, it + 1)
            dve.tensor_copy(selWT, ps[:, 2, 0:T]).then_inc(s_sw, 1)
            dve.wait_ge(s_e, it + 1)
            dve.tensor_tensor(hidden, hidden, ps[:, 1, :], ALU.mult).then_inc(s_hS, 1)
            for nh in range(2):
                dve.wait_ge(s_used, it * QCH + (MRING + 20 + 4 * nh))
                dve.tensor_copy(yS[:, nh * 1024:nh * 1024 + 512], ps[:, 4 + 2 * nh, :]).then_inc(s_yd, 1)
            for nh in range(2):
                for n in range(2):
                    for m in range(TB):
                        k = 4 * nh + 2 * n + m
                        dve.wait_ge(s_comb, it * 8 + (k + 1))
                        cols = slice((2 * nh + n) * 512, (2 * nh + n + 1) * 512)
                        dve.tensor_tensor(xr[:, m, cols], xr[:, m, cols], ps[:, 2 + m, :],
                                          ALU.add).then_inc(s_add, 1)
        assert ch.n - n0 == per_step, ch.n - n0
        ch.n, ch.off = n0, n_steps * per_step

        dve.wait_ge(s_add, n_steps * 8 + 4)
        for k, half in enumerate((ssA, ssB)):
            cols = slice(k * 1024, (k + 1) * 1024)
            link(dve.tensor_tensor_reduce(squares[:, 1, cols], xr[:, 1, cols], xr[:, 1, cols], 1.0, 0.0, ALU.mult,
                                          ALU.add, half[:, 1:2]))
        dve.wait_ge(s_fss, 1)
        link(dve.tensor_tensor(ss, ssA, ssB, ALU.add))
        rsqrt_dve(dve, link, rs, ss, 1.0 / D, H + 3)
        dve.wait_ge(s_gain, 48)
        for m, k in OUT_ORDER:
            cols = slice(k * 1024, (k + 1) * 1024)
            dve.scalar_tensor_tensor(outS[:, m, cols], xr[:, m, cols], rs[:, m:m + 1], gain[:, cols], ALU.mult,
                                     ALU.mult).then_inc(s_out, 1)

    @block.scalar
    def _(act):
        ch = Chain(act, s_act)
        link = ch.link
        for s in (s_odt, s_oS, s_ya):
            act.sem_inc(s, 1)
        for s in (s_ge, s_fa):
            act.sem_inc(s, 2)

        def rounded(i, c):
            if c % 8 == 0:
                act.wait_ge(landed[(c // 8) % DRING], i * 16 + 16 * (c // PT + 1))
            act.wait_ge(s_pu, i * PT + (c + 1))
            act.copy(wH[c % AHEAD], piece_of_ring(c)).then_inc(s_wh, 1)

        def x_rounded(src, j):
            act.copy(split[:, j * PIECE:(j + 1) * PIECE], src).then_inc(s_xh, 1)

        act.preload_act_table_set(LN_EXP)
        for j in range(2):
            act.wait_ge(s_turned, j + 1)
            x_rounded(ps[:, 4 + j, :], j)
        for c in range(AHEAD):
            rounded(0, c)
            if c < 2:
                act.wait_ge(s_turned, c + 3)
                x_rounded(ps[:, 6 + c, :], 2 + c)
        for j in range(4, 8):
            for c in (2 * j - 4, 2 * j - 3):
                rounded(0, c)
            act.wait_ge(s_turned, j + 1)
            x_rounded(ps[:, j, :], j)
        act.activation(squares[:, 0, :], x0[:, 0, :], ACT.Square, accum_out=ss[:, 0:1]).then_inc(s_ssq, 1)
        rsqrt_act(act, link, 1)

        def take_tile(t):
            act.wait_ge(s_pu, t * PT + (PT + AHEAD))
            act.activation(proj[:, bass.ds(t, 1), :, 1, :].rearrange("p r h d -> p (r h) d"),
                           ps[:, bass.ds((t % 2) * 4 + 2, 2), :].rearrange("p b (h d) -> p (b h) d", d=P),
                           ACT.Copy, scale=rs[:, 1:2]).then_inc(s_fa, 1)

        for c in range(12, PT + AHEAD):
            rounded(0, c)
        act.wait_ge(s_rs, 1)
        take_tile(0)
        with act.Fori(1, TILES_A - 1) as t:
            for c in range(AHEAD, PT + AHEAD):
                rounded(t, c)
            take_tile(t)
        act.wait_ge(s_lam, 1)
        act.activation(lam4, lamE, ACT.Exp).then_inc(s_lamE, 1)
        for c in range(AHEAD, PT + AHEAD):
            rounded(TILES_A - 1, c)
        take_tile(TILES_A - 1)
        act.wait_ge(s_set, 2)

        act.preload_act_table_set(LN_EXP)
        def head(i, par):
            h = 2 * i + par
            act.wait_ge(s_tda, h + 2)
            link(act.activation(qkT_da[:, 0, :], ps[:, 7, 0:256], ACT.Copy, scale=float(HD) ** -0.5))
            act.copy(qkT_da[:, 1, :], ps[:, 7, 256:512]).then_inc(s_ka, 1)
            for p in range(4, 20):
                rounded(i + TILES_A, 16 * par + p)
                if p == 7:
                    act.wait_ge(s_z, h + 1)
                    link(act.copy(zS, ps[:, 4, 0:384]))
                    link(act.activation(lS, ps[:, 4, 0:384], ACT.Abs))
                    link(act.activation(lS, lS, ACT.Exp, scale=-1.0))
                    act.activation(lS, lS, ACT.Ln, bias=one_c).then_inc(s_l, 1)
                if p == 9:
                    act.wait_ge(s_mx, h + 1)
                    for q, cols in enumerate((slice(0, 128), slice(128, 384))):
                        for mp in range(2):
                            k = 2 * q + mp
                            ins = act.activation(pS[:, mp, cols], ps[:, 5 + mp, cols], ACT.Exp,
                                                 bias=nmx[:, k:k + 1], accum_out=sm[:, k:k + 1])
                    ins.then_inc(s_p, 1)
                if p == 13:
                    act.wait_ge(s_zc, h + 1)
                    act.activation(aT, zS, ACT.Exp).then_inc(s_a, 1)
                if p == 17:
                    act.wait_ge(s_oda, h + 1)
                    act.copy(oS.rearrange("p m d -> p (m d)"), ps[:, 7, 0:256]).then_inc(s_oS, 1)
            rsqrt_act(act, link, h + 2)
            act.wait_ge(s_pu, h * KC + (G_B + KC + AHEAD))
            for m in range(TB):
                ins = act.activation(gates[:, :, bass.ds(h, 1), m, :].rearrange("p r h d -> p (r h) d"),
                                     ps[:, 2 * par + m, :].rearrange("p (r d) -> p r d", r=4), ACT.Copy,
                                     scale=rs[:, m:m + 1])
            ins.then_inc(s_ge, 1)
            act.wait_ge(s_oT, h + 1)
            act.copy(oT[:, bass.ds(h + H, 1), :].rearrange("p h t -> p (h t)"),
                     ps[:, 5, 0:256]).then_inc(s_odt, 1)

        n0, per = ch.n, 2 * 5
        with act.Fori(0, H // 2) as i:
            ch.off = i * per
            head(i, 0)
            head(i, 1)
        assert ch.n - n0 == per, ch.n - n0
        ch.n, ch.off = n0 + per * H // 2, 0

        act.preload_act_table(ACT.Sigmoid)
        act.wait_ge(s_ge, H + 2)
        act.wait_ge(s_odt, H + 1)

        def o_part(j):
            return oT[:, 2 * j:2 * j + 2, :].rearrange("p c t -> p (c t)")

        act.wait_ge(s_ost, H + 1)
        for j in range(2):
            x_rounded(o_part(j), j)
        for t in range(2):
            for c in range(AHEAD, PT + AHEAD):
                rounded(10 + t, c)
                if t == 0 and c % 2 == 0 and 2 <= c // 2 < 8:
                    x_rounded(o_part(c // 2), c // 2)
                if (t, c) in ((0, 12), (0, 24), (1, 8), (1, 20)):
                    n = ((0, 12), (0, 24), (1, 8), (1, 20)).index((t, c))
                    tt, br = n // 2, n % 2
                    gt = gates[:, :, 4 * br + 2 * tt:4 * br + 2 * tt + 2, :, :].rearrange("p r h m d -> p r (h m d)")
                    act.activation(gt, gt, ACT.Sigmoid).then_inc(s_sig, 1)
                    if n == 3:
                        act.preload_act_table_set(LN_EXP)
                if t == 1 and c >= 29 and c % 2 == 1 and (c - 29) // 2 < 4:
                    j = (c - 29) // 2
                    act.wait_ge(s_turned, 8 + j + 1)
                    act.wait_ge(s_pu, G_C + PT + 16 + AHEAD)
                    x_rounded(ps[:, j, :], j)
        def squares_of(k, half):
            for m in range(TB):
                ins = act.activation(outJ[:, m, :], xr[:, m, k * 1024:(k + 1) * 1024], ACT.Square,
                                     accum_out=half[:, m:m + 1])
            if k == 1:
                ins.then_inc(s_sq2, 1)

        for t in range(2):
            for c in range(AHEAD, PT + (AHEAD if t == 0 else 0)):
                rounded(12 + t, c)
                if t == 0 and c in (8, 10, 12, 14):
                    j = 4 + (c - 8) // 2
                    act.wait_ge(s_turned, 8 + j + 1)
                    x_rounded(ps[:, j, :], j)
                if t == 1 and c in (19, 21):
                    j = c - 18
                    act.wait_ge(s_x2t, j + 1)
                    act.copy(x2T[:, 2 * j:2 * j + 2, :].rearrange("p c t -> p (c t)"),
                             ps[:, j, :]).then_inc(s_2a, 1)
                if t == 1 and c == 26:
                    squares_of(0, ssA)
        for j, bank in ((5, 1), (7, 4)):
            act.wait_ge(s_x2t, j + 1)
            act.copy(x2T[:, 2 * j:2 * j + 2, :].rearrange("p c t -> p (c t)"), ps[:, bank, :]).then_inc(s_2a, 1)
        squares_of(1, ssB)
        rsqrt_act(act, link, H + 2)
        rt4 = rt.rearrange("p (a m) -> p a m", m=TB)
        act.wait_ge(s_gm, 1)
        for m in range(TB):
            ins = act.activation(gexp[:, m, :], lg[:, m, 0:G], ACT.Exp, bias=rt4[:, 0, m:m + 1],
                                 accum_out=rt4[:, 1, m:m + 1])
        ins.then_inc(s_gx, 1)
        act.wait_ge(s_dd, 1)
        act.activation(rt4[:, 4, :], rt4[:, 3, :], ACT.Exp).then_inc(s_ex, 1)
        act.preload_act_table(ACT.Silu)
        act.wait_ge(s_steps, 1)
        n_steps = act.value_load(steps_i[0:1, 0:1], min_val=NQ, max_val=NQ * (T // SLOTS))
        with act.Fori(0, n_steps) as it:
            for b in (1, 3):
                act.wait_ge(s_gath, 4 * it + (b + 1))
                act.copy(xgT[:, 4 * b:4 * b + 4, :].rearrange("p c s -> p (c s)"),
                         ps[:, 4 + b, :]).then_inc(s_xa, 1)
            act.wait_ge(s_used, it * QCH + (MRING + 16))
            act.activation(hidden, ps[:, 0, :], ACT.Silu).then_inc(s_e, 1)
            act.wait_ge(s_ht, it + 1)
            act.copy(hT4, ps[:, 0, :]).then_inc(s_hT, 1)
            for nh in range(2):
                act.wait_ge(s_used, it * QCH + (MRING + 20 + 4 * nh))
                act.copy(yS[:, nh * 1024 + 512:nh * 1024 + 1024], ps[:, 5 + 2 * nh, :]).then_inc(s_ya, 1)
        act.preload_act_table_set(LN_EXP)
        for k, half in enumerate((ssA, ssB)):
            act.wait_ge(s_add, n_steps * 8 + 4 * k)
            cols = slice(k * 1024, (k + 1) * 1024)
            ins = act.activation(squares[:, 0, cols], xr[:, 0, cols], ACT.Square, accum_out=half[:, 0:1])
        ins.then_inc(s_fss, 1)
        rsqrt_act(act, link, H + 3)

    ctx.close()


_INS = ["x", "mix_norm_g", "w_in", "lambda_q1", "lambda_k1", "lambda_q2", "lambda_k2", "diff_subnorm_g",
        "w_branch_sb", "w_branch_diff", "w_out", "ffn_norm_g", "w_group_router", "w_expert_router",
        "w_gate", "w_up", "w_down", "final_norm_g"]


def kernel(**inputs):
    import concourse.bacc as bacc
    from concourse.bass_utils import run_bass_kernel_spmd

    nc = bacc.Bacc("TRN2", target_bir_lowering=False, num_devices=1)
    arrays, args = {}, []
    for name in _INS:
        a = np.ascontiguousarray(inputs[name])
        arrays[f"in_{name}"] = a
        args.append(nc.dram_tensor(f"in_{name}", a.shape, mybir.dt.from_np(a.dtype), kind="ExternalInput").ap())
    c = shape_constants()
    arrays["shape_constants"] = c
    args.append(nc.dram_tensor("shape_constants", c.shape, F32, kind="ExternalInput").ap())
    out = nc.dram_tensor("out", inputs["x"].shape, F32, kind="ExternalOutput").ap()
    build(nc, *args, out)
    r = run_bass_kernel_spmd(nc, [arrays], core_ids=[0])
    return r.results[0]["out"]
```

```python
from contextlib import ExitStack

import numpy as np

import concourse.bass as bass
from concourse import mybir

F32 = mybir.dt.float32
F32R = mybir.dt.float32r
BF16 = mybir.dt.bfloat16
U32 = mybir.dt.uint32
I32 = mybir.dt.int32
ALU = mybir.AluOpType
ACT = mybir.ActivationFunctionType
AX = mybir.AxisListType

P = 128
D = 2048
T = 256
TB = T // P
KC = D // P
H = 8
HD = 64
CHUNK = 64
G = 4
EPG = 8
E = G * EPG
SLOTS = 32
QUAD = P // SLOTS
NQ = E // QUAD
EPS = 1e-6
LN_EXP = "natural_log_exp_and_others"
LAM_INIT = 0.2
NEG = -1e30
SLOT = 4096
DRING = 4
MRING = 8
MORDER = (4, 5, 0, 1, 2, 3, 6, 7)
TEMPS = 7168
RC = 64
TILES_A = 6
PROJ_CHUNKS = 4 * TILES_A
GATE_CHUNKS = 2 * H
BRANCH_CHUNKS = 8
OUT_CHUNKS = 8
DENSE = PROJ_CHUNKS + GATE_CHUNKS + BRANCH_CHUNKS + OUT_CHUNKS
QCH = 24
R_QSB, R_QDA, R_KSB, R_VSB, R_KDA, R_VDA = range(6)
PIECE = 512
AHEAD = 4
PT = 32
G_B = TILES_A * PT
G_C = G_B + H * KC
G_D = G_C + 2 * PT
KEEP_BUSY = 32
LATE = (5, 6, 7)
EXTRA = MRING

C_ID, C_TRI, C_ONE, C_PREV, C_MSB, C_MDA, C_COS, C_SIN, C_IOTA, C_THR = (
    0, 128, 256, 384, 512, 640, 768, 896, 1024, 1056)
C_ST = 1064
C_N = 1064 + G + E


def shape_constants():
    c = np.zeros((P, C_N), np.float32)
    i = np.arange(P)
    c[:, C_ID:C_ID + P] = i[:, None] == i[None, :]
    c[:, C_TRI:C_TRI + P] = i[:, None] >= i[None, :]
    c[:, C_ONE:C_ONE + P] = 1.0
    c[:, C_PREV:C_PREV + P] = i[:, None] < i[None, :]
    c[:, C_MSB:C_MSB + P] = np.where(i[:, None] >= i[None, :], NEG, 0.0)
    c[:, C_MDA:C_MDA + P] = np.where(i[None, :] // CHUNK > i[:, None] // CHUNK, NEG, 0.0)
    half = HD // 2
    inv = np.float32(10000.0) ** (-(np.arange(half, dtype=np.float32) * np.float32(2.0) / np.float32(HD)))
    ang = (np.arange(T, dtype=np.float32)[:, None] * inv.astype(np.float32)[None, :]).astype(np.float64)
    for m in range(TB):
        for mp in range(2):
            at = (m * 2 + mp) * half
            c[:, C_COS + at:C_COS + at + half] = np.cos(ang[m * P:(m + 1) * P])
            c[:, C_SIN + at:C_SIN + at + half] = np.sin(ang[m * P:(m + 1) * P])
    c[:, C_IOTA:C_IOTA + E] = np.arange(E)
    c[:, C_THR:C_THR + 8] = np.arange(1, 9) * SLOTS
    for half in range(2):
        c[half * RC:half * RC + G + E, C_ST:] = np.eye(G + E)
    return c


class Chain:

    def __init__(self, eng, sem):
        self.eng, self.sem, self.n, self.off = eng, sem, 0, 0

    def link(self, ins):
        self.n += 1
        ins.then_inc(self.sem, 1)
        self.eng.wait_ge(self.sem, self.off + self.n)


def build(nc, x, mix_g, w_in, lq1, lk1, lq2, lk2, sub_g, w_sb, w_da, w_out, ffn_g, w_gr, w_er,
          w_gate, w_up, w_down, fin_g, consts, out):
    ctx = ExitStack()

    def sb(name, shape, dt=F32):
        return ctx.enter_context(nc.sbuf_tensor(name, shape, dt))

    def sem(name):
        return ctx.enter_context(nc.semaphore(name))

    cst = sb("cst", [P, C_N])
    gain = sb("gain", [P, D])
    wr = sb("wr", [P, KC, RC])
    g16 = sb("g16", [KC, 2, P])
    gT = sb("gT", [P, 2, KC])
    ident16 = sb("ident16", [P, P], BF16)
    mask16 = sb("mask16", [P, 2, P], BF16)
    count16 = sb("count16", [P, 2, P], BF16)
    took16 = sb("took16", [P, TB, E], BF16)
    cell = sb("cell", [P, 64])
    arena = sb("arena", [P, DRING * SLOT + 6 * 2048 + TEMPS])
    n_split = 2 * SLOT + AHEAD * 2 * PIECE
    with nc.sbuf_tensor("split", [P, n_split], F32R) as split:
        pass
    late = sb("late", [P, n_split])
    ps = ctx.enter_context(nc.psum_tensor("ps", [P, 8, 512], F32))

    ident, tri, ones = (cst[:, a:a + P] for a in (C_ID, C_TRI, C_ONE))
    ones16, prev16 = count16[:, 0, :], count16[:, 1, :]
    cosH = cst[:, C_COS:C_COS + P].rearrange("p (s f) -> p s f", s=4)
    sinH = cst[:, C_SIN:C_SIN + P].rearrange("p (s f) -> p s f", s=4)

    xH = split[:, 0:SLOT].rearrange("p (c t) -> p c t", c=KC)
    xL = split[:, SLOT:2 * SLOT].rearrange("p (c t) -> p c t", c=KC)
    wH = [split[:, 2 * SLOT + b * 2 * PIECE:2 * SLOT + (2 * b + 1) * PIECE] for b in range(AHEAD)]
    wL = [split[:, 2 * SLOT + (2 * b + 1) * PIECE:2 * SLOT + (2 * b + 2) * PIECE] for b in range(AHEAD)]

    def at(base, n):
        return arena[:, base:base + n]

    B_P = DRING * SLOT
    proj = at(B_P, 6 * 2048).rearrange("p (r h m d) -> p r h m d", r=6, h=H, m=TB)
    gates = proj[:, 2:6]
    x0 = at(B_P + 2 * 2048, SLOT).rearrange("p (m d) -> p m d", m=TB)
    oT = at(B_P, SLOT).rearrange("p (c t) -> p c t", c=KC)
    xr = at(B_P, SLOT).rearrange("p (m d) -> p m d", m=TB)
    h2 = late[:, 0:SLOT].rearrange("p (m c d) -> p m c d", m=TB, c=KC)
    xgT = late[:, SLOT:SLOT + 2048].rearrange("p (c s) -> p c s", c=KC)
    yS = late[:, SLOT + 2048:2 * SLOT]
    outS = late[:, 0:SLOT].rearrange("p (m d) -> p m d", m=TB)
    xgJ = late[:, SLOT:SLOT + 2048].rearrange("p (k d) -> p k d", k=2)
    ring = ([at(s * SLOT, SLOT) for s in range(DRING)]
            + [at(B_P + (2 + 2 * s) * 2048, SLOT) for s in range(2)]
            + [late[:, 2 * SLOT:3 * SLOT],
               at(B_P + 6 * 2048, SLOT)])
    extra = (yS, gain)
    B_X = B_P + 6 * 2048
    used = [B_X]

    def temp(n):
        used[0] += n
        assert used[0] <= B_X + TEMPS
        return at(used[0] - n, n)

    squares = at(B_X, SLOT).rearrange("p (m d) -> p m d", m=TB)
    gsub = at(B_X + TEMPS - P, P)
    lamv = at(B_X + SLOT, 256).rearrange("p (v d) -> p v d", v=4)
    rope_u, rope_v = (temp(1024).rearrange("p (b s f) -> p b s f", b=H, s=4) for _ in range(2))
    used[0] = B_X
    qk_sb = temp(512).rearrange("p (w m d) -> p w m d", w=2, m=TB)
    qk_da = temp(512).rearrange("p (w m d) -> p w m d", w=2, m=TB)
    v_sb = temp(256).rearrange("p (m d) -> p m d", m=TB)
    qkT_sb = temp(512).rearrange("p (w t) -> p w t", w=2)
    qkT_da = temp(512).rearrange("p (w t) -> p w t", w=2)
    zS, eS, lS, aT, attn, attnT = (temp(384) for _ in range(6))
    pS = temp(768).rearrange("p (a k) -> p a k", a=2)
    oS = temp(256).rearrange("p (m d) -> p m d", m=TB)
    oN = temp(256).rearrange("p (m d) -> p m d", m=TB)
    sq = temp(P)
    used[0] = B_X
    merged = temp(SLOT).rearrange("p (m n) -> p m n", m=TB)
    part = temp(1024)
    used[0] = B_X
    x2T = temp(SLOT).rearrange("p (c t) -> p c t", c=KC)
    accS = temp(T)
    lg = temp(TB * (G + 4 + E)).rearrange("p (m e) -> p m e", m=TB)
    gm8, gi8f, ev8, ei8f = (temp(16).rearrange("p (m e) -> p m e", m=TB) for _ in range(4))
    gi8, ei8 = (temp(16).bitcast(U32).rearrange("p (m e) -> p m e", m=TB) for _ in range(2))
    goh = temp(8).rearrange("p (m g) -> p m g", m=TB)
    gexp = temp(8).rearrange("p (m g) -> p m g", m=TB)
    picked = temp(TB * E).rearrange("p (m e) -> p m e", m=TB)
    esel = temp(16).rearrange("p (m e) -> p m e", m=TB)
    oh1, oh2, share, rank = (temp(TB * E).rearrange("p (m e) -> p m e", m=TB) for _ in range(4))
    rt = temp(64)
    count8 = temp(8)
    steps_i = temp(2).bitcast(I32)
    selE = temp(TB * P).rearrange("p (m e s) -> p m e s", m=TB, e=QUAD)
    selW = temp(TB * P).rearrange("p (m e s) -> p m e s", m=TB, e=QUAD)
    selG = temp(TB * P).rearrange("p (m n) -> p m n", m=TB)
    selWT = temp(T)
    hidden, hT4 = (temp(512) for _ in range(2))
    outJ = at(B_X + TEMPS - 2048, 2048).rearrange("p (m d) -> p m d", m=TB)

    one_c = cell[:, 0:1]
    ss, rs = cell[:, 2:4], cell[:, 4:6]
    neglam = cell[:, 6:7]
    lam4 = cell[:, 8:10]
    lamE = cell[:, 10:12]
    mx, nmx, sm, rsm = cell[:, 12:16], cell[:, 16:20], cell[:, 20:24], cell[:, 24:28]
    oss, ors = cell[:, 28:30], cell[:, 30:32]
    rsn = cell[:, 32:34]
    ssA, ssB, ssC = cell[:, 42:44], cell[:, 44:46], cell[:, 46:48]
    rv, ry, rq = cell[:, 34:36], cell[:, 36:38], cell[:, 38:40]

    s_cst, s_gain, s_small, s_xr, s_store = (sem(n) for n in (
        "consts_landed", "gain_landed", "small_landed", "xr_landed", "stored"))
    s_xk = [sem(f"x_quarter{k}_landed") for k in range(4)]
    landed = [sem(f"slot{s}_landed") for s in range(MRING)]
    s_wh, s_wl, s_pu = sem("piece_rounded"), sem("piece_rest_ready"), sem("pieces_used")
    s_used = sem("expert_chunks_used")
    s_dve, s_act = sem("dve_chain"), sem("act_chain")
    s_set = sem("cells_set")
    s_ssq = sem("squares_summed")
    s_turned, s_xh, s_xl = sem("operand_turned"), sem("operand_rounded"), sem("operand_rest_ready")
    s_fd, s_fa = sem("half_free_dve"), sem("half_free_act")
    s_roped = sem("roped")
    s_v, s_y0, s_rs = sem("mean_square_ready"), sem("root_estimated"), sem("root_ready")
    s_id = sem("identity_landed")
    s_part = [sem(f"first_chunk_quarter{k}_landed") for k in range(3)]
    halves = [sem(f"chunk{QCH - 2 + n}_first_half_landed") for n in range(2)]
    quarters = [sem(f"expert_chunk{j}_quarters_landed") for j in LATE]
    s_mg, s_gtT = sem("mixer_gain_landed"), sem("mixer_gain_ready")
    s_gt, s_wr = sem("gain_turned"), sem("router_weights_ready")
    s_hsb, s_hda, s_hv = sem("head_sb_copied"), sem("head_da_copied"), sem("head_v_copied")
    s_tsb, s_tda = sem("sb_qk_turned"), sem("da_qk_turned")
    s_kd, s_ka = sem("qkT_by_dve"), sem("qkT_by_act")
    s_z, s_sc = sem("z_done"), sem("da_scores_done")
    s_l, s_L = sem("log_part_ready"), sem("softplus_ready")
    s_zc, s_c, s_a = sem("z_less_sum_ready"), sem("sums_done"), sem("a_ready")
    s_mx, s_p = sem("row_max_ready"), sem("probs_ready")
    s_at, s_att, s_atT = sem("attn_ready"), sem("attn_turned"), sem("attnT_ready")
    s_osb, s_oda = sem("sb_o_done"), sem("da_o_done")
    s_ost, s_oS, s_oN, s_oT, s_odt = (sem(n) for n in (
        "oT_sb_stored", "da_o_copied", "da_o_normed", "da_o_turned", "oT_da_stored"))
    s_ge, s_sig, s_gd = sem("gate_tile_copied"), sem("gates_squashed"), sem("gates_read")
    s_lam = sem("lambda_sums")
    s_lamE = sem("lambda_exps")
    s_At, s_Bt = sem("branch_a_read"), sem("branch_b_read")
    s_x2, s_sq2, s_h2 = sem("x2_ready"), sem("x2_squares"), sem("h2_ready")
    s_x2t, s_2d, s_2a = sem("x2_turned"), sem("x2T_by_dve"), sem("x2T_by_act")
    s_acc, s_accS = sem("logits_summed"), sem("logit_sums_copied")
    s_log, s_gm, s_gx = sem("logits_done"), sem("group_max_ready"), sem("group_exp_ready")
    s_ex = sem("pair_exp_ready")
    s_dd = sem("pair_gap_ready")
    s_took, s_rank, s_steps = sem("took_ready"), sem("ranks_done"), sem("steps_ready")
    s_shr = sem("shares_ready")
    s_sel, s_gath, s_xd, s_xa = sem("sel_ready"), sem("gathered"), sem("xgT_by_dve"), sem("xgT_by_act")
    s_swt, s_sw = sem("shares_turned"), sem("sharesT_ready")
    s_e, s_hS = sem("silu_ready"), sem("hidden_ready")
    s_ht, s_hT = sem("hidden_turned"), sem("hiddenT_ready")
    s_yn = sem("y_first_bank_done")
    s_yd, s_ya = sem("y_by_dve"), sem("y_by_act")
    s_comb, s_add = sem("combined"), sem("added")
    s_fss, s_xg = sem("final_squares"), sem("times_final_gain")
    s_out = [sem(f"out_half{k}_ready") for k in range(2)]
    extra_landed = sem("extra_chunk_landed")

    w_in_c = w_in[0].rearrange("(c k p) n -> c p k n", c=4, p=P)
    w_gt_c = w_in[0].rearrange("(c k p) n -> c p k n", c=2, p=P)
    w_br_c = [w[0].rearrange("(c k p) n -> c p k n", c=2, p=P) for w in (w_sb, w_da)]
    w_out_c = w_out[0].rearrange("(c k p) n -> c p k n", c=4, p=P)
    w_out_h = w_out[0].rearrange("(c k p) n -> c p k n", c=2, p=P)
    w_gate_q = w_gate[0].rearrange("(q e) (p c) f -> q p e c f", e=QUAD, c=KC)
    w_up_q = w_up[0].rearrange("(q e) (p c) f -> q p e c f", e=QUAD, c=KC)
    w_down_q = w_down[0].rearrange("(q e) (c p) n -> q p e c n", e=QUAD, p=P)
    x_rows = x[0].rearrange("(m p) d -> p m d", p=P)
    out_rows = out[0].rearrange("(m p) d -> p m d", p=P)

    def mslot(it, j):
        return MORDER[j if isinstance(it, int) and j < EXTRA else (j - 1) % MRING]

    def mlanded(eng, it, j):
        first = isinstance(it, int)
        if first and j == EXTRA:
            eng.wait_ge(extra_landed, 32)
        elif first and j in LATE:
            eng.wait_ge(quarters[j - LATE[0]], 64)
        else:
            s = mslot(it, j)
            base = 16 * (DENSE // DRING) if s < DRING else 0
            turn = 0 if first and j < EXTRA else (j - 1) // MRING
            if s in [MORDER[k] for k in LATE]:
                turn -= 1
            eng.wait_ge(landed[s], it * (16 * QCH // MRING) + base + 16 * (turn + 1))

    def expert_words(it, j, e):
        if isinstance(it, int) and j == EXTRA:
            return extra[e // 2][:, e % 2 * 1024:(e % 2 + 1) * 1024]
        return ring[mslot(it, j)][:, e * 1024:(e + 1) * 1024]

    def piece_of_ring(c):
        return ring[(c // 8) % DRING][:, (c % 8) * PIECE:(c % 8 + 1) * PIECE]

    block = ctx.enter_context(nc.Block())

    @block.sync
    def _(sp):
        def load_dense(c, n, src, k):
            if n is not None:
                sp.wait_ge(s_wl, n)
            sp.dma_start(ring[c].rearrange("p (k n) -> p k n", k=k), src).then_inc(landed[c], 16)

        sp.dma_start(cst[:, 0:P], consts[:, 0:P]).then_inc(s_id, 16)
        for c in range(4):
            cols = slice(c * PIECE, (c + 1) * PIECE)
            sp.dma_start(x0[:, :, cols], x_rows[:, :, cols]).then_inc(s_xk[c], 16)
            if c == 0:
                for k in range(4):
                    sp.dma_start(ring[0][:, k * 1024:(k + 1) * 1024], w_in_c[0, :, k, 0:1024]).then_inc(
                        s_part[k] if k < 3 else landed[0], 16)
            else:
                load_dense(c, None, w_in_c[c, :, :, 0:1024], 4)
        sp.dma_start(cst[:, P:], consts[:, P:]).then_inc(s_cst, 16)
        for c in range(4):
            load_dense(c, 8 * (c + 1), w_in_c[c, :, :, 3 * 1024:4 * 1024], 4)
        with sp.Fori(1, TILES_A // 2) as i:
            for par in range(2):
                for c in range(4):
                    load_dense(c, 64 * i + (32 * (par - 1) + 8 * (c + 1)),
                               w_in_c[c, :, :, bass.ds(i * 3072 + (1024 * par - 2048), 1024)], 4)
        with sp.Fori(0, H // 2) as i:
            for c in range(4):
                load_dense(c, 32 * i + (G_B - PT + 8 * (c + 1)),
                           w_gt_c[c % 2, :, :, bass.ds(i * 1024 + (6 * 1024 + 512 * (c // 2)), 512)], 8)
        for t in range(2):
            for c in range(4):
                load_dense(c, 32 * t + (G_C - PT + 8 * (c + 1)),
                           w_br_c[c // 2][c % 2, :, :, t * 1024:(t + 1) * 1024], 4)
        for c in range(4):
            load_dense(c, G_D - PT + 8 * (c + 1), w_out_c[c, :, :, 0:1024], 4)
        for c in range(4):
            cols = slice(1024 + 512 * (c // 2), 1536 + 512 * (c // 2))
            load_dense(c, G_D + 8 * (c + 1), w_out_h[c % 2, :, :, cols], 8)

        def load_quad(it):
            q, first = it % NQ, isinstance(it, int)
            for j in range(QCH):
                if not first or j > 2 * MRING:
                    sp.wait_ge(s_used, it * QCH + (j + 1))
                elif j > EXTRA:
                    sp.wait_ge(s_used, j)
                elif j < 2:
                    sp.wait_ge(s_gd, 1)
                elif j < LATE[0]:
                    sp.wait_ge(s_wl, G_D + PT + 8 * (j - 1))
                if j < 16:
                    w, kp = (w_gate_q, w_up_q)[j % 2], j // 2
                    src = w[bass.ds(q, 1), :, :, 2 * kp:2 * kp + 2, :].rearrange("q p e c f -> p (q e) (c f)")
                elif j < QCH - 2:
                    nh, c = (j - 16) // 4, (j - 16) % 4
                    src = w_down_q[bass.ds(q, 1), :, :, c, nh * 1024:nh * 1024 + 1024].rearrange(
                        "q p e n -> p (q e) n")
                else:
                    col = 1024 + 512 * (j - (QCH - 2))
                    src = [w_down_q[bass.ds(q, 1), :, :, c, col:col + 512].rearrange("q p e n -> p (q e) n")
                           for c in (2, 3)]
                if first and j in LATE:
                    for e in range(QUAD):
                        if j == 5:
                            sp.wait_ge(s_wl, G_D + 2 * PT - 8 + 2 * (e + 1))
                        elif j == 6:
                            sp.wait_ge(s_pu, G_D + 2 * PT + e + 1)
                        else:
                            sp.wait_ge(s_acc, 2 if e < 3 else 3)
                        sp.dma_start(ring[mslot(it, j)][:, e * 1024:(e + 1) * 1024].rearrange(
                            "p (o n) -> p o n", o=1), src[:, e:e + 1, :]).then_inc(quarters[j - LATE[0]], 16)
                elif first and j == EXTRA:
                    for k in range(2):
                        if k == 0:
                            sp.wait_ge(s_pu, G_D + 2 * PT + AHEAD)
                        else:
                            sp.wait_ge(s_h2, 4)
                        sp.dma_start(extra[k][:].rearrange("p (e n) -> p e n", e=2),
                                     src[:, 2 * k:2 * k + 2, :]).then_inc(extra_landed, 16)
                else:
                    s = mslot(it, j)
                    slot = ring[s].rearrange("p (e n) -> p e n", e=QUAD)
                    if j < QCH - 2:
                        sp.dma_start(slot, src).then_inc(landed[s], 16)
                    else:
                        sp.dma_start(slot[:, :, 0:512], src[0]).then_inc(halves[j - (QCH - 2)], 16)
                        sp.dma_start(slot[:, :, 512:1024], src[1]).then_inc(landed[s], 16)

        load_quad(0)
        sp.wait_ge(s_steps, 2)
        n_steps = sp.value_load(steps_i[0:1, 0:1], min_val=NQ, max_val=NQ * (T // SLOTS))
        with sp.Fori(1, n_steps) as it:
            load_quad(it)
        for m in range(TB):
            for k in range(2):
                sp.wait_ge(s_out[k], m + 1)
                cols = slice(k * 1024, (k + 1) * 1024)
                sp.dma_start(out_rows[:, m, cols], outS[:, m, cols]).then_inc(s_store, 16)
        sp.wait_ge(s_store, 16 * 2 * TB)

    @block.gpsimd
    def _(pool):
        pool.dma_start(g16[:, 0, :], mix_g[0].rearrange("(c p) -> c p", p=P)).then_inc(s_mg, 16)
        pool.wait_ge(s_xk[3], 16)
        for v, lv in enumerate((lq1, lk1, lq2, lk2)):
            pool.dma_start(lamv[:, v, :], lv[0:1, :].to_broadcast([P, HD])).then_inc(s_small, 16)
        pool.dma_start(gsub, sub_g[0:1, :].to_broadcast([P, P])).then_inc(s_small, 16)
        pool.dma_start(g16[:, 1, :], ffn_g[0].rearrange("(c p) -> c p", p=P)).then_inc(s_small, 16)
        pool.dma_start(wr[:, :, 0:G], w_gr[0].rearrange("(c p) g -> p c g", p=P)).then_inc(s_small, 16)
        pool.dma_start(wr[:, :, G:G + E], w_er[0].rearrange("(c p) g -> p c g", p=P)).then_inc(s_small, 16)
        pool.memset(wr[:, :, G + E:], 0.0).then_inc(s_set, 1)
        pool.dma_start(gain[:], ffn_g[0:1, :].to_broadcast([P, D])).then_inc(s_gain, 16)
        pool.wait_ge(s_id, 16)
        pool.wait_ge(s_cst, 16)
        pool.tensor_copy(ident16[:], ident)
        pool.tensor_copy(count16[:], cst[:, C_ONE:C_ONE + 2 * P].rearrange("p (a b) -> p a b", a=2))
        pool.tensor_copy(mask16[:], cst[:, C_MSB:C_MSB + 2 * P].rearrange("p (a b) -> p a b", a=2))
        pool.wait_ge(s_fd, 2 + TILES_A - 1)
        pool.wait_ge(s_fa, 2 + TILES_A - 1)
        pool.wait_ge(s_roped, 2)
        with pool.Fori(0, H) as h:
            pool.wait_ge(s_tsb, h + 1)
            for w, r in enumerate((R_QSB, R_KSB)):
                ins = pool.tensor_copy(qk_sb[:, w].rearrange("p m d -> p (m d)"),
                                       proj[:, r, bass.ds(h, 1), :, :].rearrange("p h m d -> p (h m d)"))
                ins.then_inc(s_hsb, 1)
            pool.wait_ge(s_tda, h + 1)
            for w, r in enumerate((R_QDA, R_KDA)):
                ins = pool.tensor_copy(qk_da[:, w].rearrange("p m d -> p (m d)"),
                                       proj[:, r, bass.ds(h, 1), :, :].rearrange("p h m d -> p (h m d)"))
                ins.then_inc(s_hda, 1)
            pool.wait_ge(s_osb, h + 1)
            pool.tensor_copy(v_sb.rearrange("p m d -> p (m d)"),
                             proj[:, R_VSB, bass.ds(h, 1), :, :].rearrange(
                                 "p h m d -> p (h m d)")).then_inc(s_hv, 1)
        pool.wait_ge(s_xl, 16)
        pool.dma_start(xr, x_rows).then_inc(s_xr, 16)
        pool.wait_ge(s_gain, 16)
        pool.wait_ge(s_pu, G_D + 2 * PT + AHEAD)
        for k in range(2):
            pool.wait_ge(s_x2, 4 * k + 4)
            for m in range(TB):
                cols = slice(k * 1024, (k + 1) * 1024)
                pool.tensor_tensor(h2[:, m, :, k * HD:(k + 1) * HD].rearrange("q c p -> q p c"),
                                   xr[:, m, cols].rearrange("q (p c) -> q p c", c=KC),
                                   gain[:, cols].rearrange("q (p c) -> q p c", c=KC), ALU.mult).then_inc(s_h2, 1)
        pool.wait_ge(s_used, MRING + EXTRA + 1)
        pool.dma_start(gain[:], fin_g.rearrange("(a d) -> a d", a=1).to_broadcast([P, D])).then_inc(s_gain, 16)

        n_steps = pool.value_load(steps_i[0:1, 0:1], min_val=NQ, max_val=NQ * (T // SLOTS))
        pool.wait_ge(s_gain, 32)
        pool.wait_ge(s_add, n_steps * 8)
        for m in range(TB):
            pool.tensor_tensor(outS[:, m, 0:1024], xr[:, m, 0:1024], gain[:, 0:1024], ALU.mult).then_inc(s_xg, 1)

    @block.tensor
    def _(pe):
        for s in (s_tsb, s_tda, s_osb):
            pe.sem_inc(s, 1)
        pe.sem_inc(s_pu, AHEAD)
        pe.sem_inc(s_used, MRING)

        def turn_rows(src, j, bank):
            for k in range(2):
                for m in range(TB):
                    c = 2 * j + k
                    mm = pe.transpose(ps[:, bank, (2 * k + m) * P:(2 * k + m + 1) * P],
                                      src[:, m, c * P:(c + 1) * P], ident)
            mm.then_inc(s_turned, 1)

        def piece(i, c, kc, banks, start, stop):
            pe.wait_ge(s_wl, i * PT + (c + 1))
            b = c % AHEAD
            for m in range(TB):
                o, cols = ps[:, banks[m], :], slice(m * P, (m + 1) * P)
                pe.matmul(o, xH[:, kc, cols], wH[b], start=start, stop=False)
                pe.matmul(o, xL[:, kc, cols], wH[b], start=False, stop=False)
                mm = pe.matmul(o, xH[:, kc, cols], wL[b], start=False, stop=stop)
            mm.then_inc(s_pu, 1)

        pe.wait_ge(s_id, 16)
        pe.wait_ge(s_mg, 16)
        pe.transpose(ps[:, 3, 0:KC], g16[:, 0, :], ident[0:KC, 0:KC]).then_inc(s_gt, 1)

        def turn_x(j):
            if j % 2 == 0:
                pe.wait_ge(s_xk[j // 2], 16)
            if j >= 4:
                pe.wait_ge(s_xl, j - 3)
            turn_rows(x0, j, 4 + j % 4)

        turn_x(0)
        turn_x(1)
        pe.wait_ge(s_gtT, 1)
        for c in range(PT):
            if c % 4 == 0:
                pe.wait_ge(s_xl, c // 4 + 1)
            if c % 8 in (4, 5) and c < 24:
                turn_x(2 * (c // 8) + c % 8 - 2)
            if c == 26:
                pe.wait_ge(s_small, 16 * 8)
                pe.wait_ge(s_xl, 8)
                pe.transpose(ps[:, 7, 0:KC], g16[:, 1, :], ident[0:KC, 0:KC]).then_inc(s_gt, 1)
            piece(0, c, c // 2, (c % 2, c % 2 + 2), c < 2, c >= PT - 2)
        pe.wait_ge(s_wr, 1)

        def a_tile(t, par):
            for c in range(PT):
                bank = 4 * par + c % 2
                piece(t, c, c // 2, (bank, bank + 2), c < 2, c >= PT - 2)

        a_tile(1, 1)
        with pe.Fori(1, TILES_A // 2) as i:
            for par in range(2):
                pe.wait_ge(s_fd, 2 * i + (par + 1))
                pe.wait_ge(s_fa, 2 * i + (par + 1))
                a_tile(2 * i + par, par)

        def turn_sb(h):
            pe.wait_ge(s_hsb, 2 * h + 2)
            pe.wait_ge(s_ost, h + 1)
            for w in range(2):
                for m in range(TB):
                    mm = pe.transpose(ps[:, 4, (2 * w + m) * P:(2 * w + m + 1) * P], qk_sb[:, w, m, :], ident)
            mm.then_inc(s_tsb, 1)

        def turn_da(h):
            pe.wait_ge(s_hda, 2 * h + 2)
            pe.wait_ge(s_oS, h + 1)
            for w in range(2):
                for m in range(TB):
                    mm = pe.transpose(ps[:, 7, (2 * w + m) * P:(2 * w + m + 1) * P], qk_da[:, w, m, :], ident)
            mm.then_inc(s_tda, 1)

        def head(i, par, last=False):
            h = 2 * i + par

            def gate_piece(p, par=par, i=i):
                piece(i + TILES_A, 16 * par + p, p % 16, (2 * (par % 2), 2 * (par % 2) + 1),
                      p == 0, p == KC - 1)

            gate_piece(2)
            pe.wait_ge(s_kd, h + 1)
            pe.matmul(ps[:, 4, 0:256], qkT_sb[:, 1, 0:P], qkT_sb[:, 0, :], start=True, stop=True)
            pe.matmul(ps[:, 4, 0:128], ident16[:], mask16[:, 0, :], start=False, stop=True,
                      skip_group_check=True)
            pe.matmul(ps[:, 4, 256:384], qkT_sb[:, 1, P:T], qkT_sb[:, 0, P:T], start=True, stop=True,
                      skip_group_check=True)
            pe.matmul(ps[:, 4, 256:384], ident16[:], mask16[:, 0, :], start=False, stop=True,
                      skip_group_check=True).then_inc(s_z, 1)
            gate_piece(3)
            pe.wait_ge(s_ka, h + 1)
            pe.wait_ge(s_odt, h + 1)
            for mp in range(2):
                r = slice(HD * mp, HD * mp + HD)
                pe.matmul(ps[:, 5 + mp, 0:128], qkT_da[r, 0, 0:P], qkT_da[r, 1, 0:P], start=True, stop=True)
                pe.matmul(ps[:, 5 + mp, 0:128], ident16[:], mask16[:, 1, :], start=False, stop=True,
                          skip_group_check=True)
                pe.matmul(ps[:, 5 + mp, 128:384], qkT_da[r, 0, P:T], qkT_da[r, 1, :], start=True, stop=True,
                          skip_group_check=True)
                mm = pe.matmul(ps[:, 5 + mp, 256:384], ident16[:], mask16[:, 1, :], start=False, stop=True,
                               skip_group_check=True)
            mm.then_inc(s_sc, 1)
            for p in range(4, 9):
                gate_piece(p)
            pe.wait_ge(s_L, h + 1)
            pe.matmul(ps[:, 4, 0:256], tri, eS[:, 0:256], start=True, stop=True)
            pe.matmul(ps[:, 4, 128:256], ones, eS[:, 256:384], start=False, stop=True, skip_group_check=True)
            pe.matmul(ps[:, 4, 256:384], tri, eS[:, 256:384], start=True, stop=True,
                      skip_group_check=True).then_inc(s_c, 1)
            for p in range(9, 11):
                gate_piece(p)
            pe.wait_ge(s_at, h + 1)
            for b in range(3):
                mm = pe.transpose(ps[:, 7, b * P:(b + 1) * P], attn[:, b * P:(b + 1) * P], ident)
            mm.then_inc(s_att, 1)
            gate_piece(11)
            pe.wait_ge(s_hv, h + 1)
            pe.wait_ge(s_a, h + 1)
            pe.matmul(ps[:, 4, 0:256], v_sb[:, 0, :], aT[:, 0:256], start=True, stop=True)
            pe.matmul(ps[:, 4, 128:256], v_sb[:, 1, :], aT[:, 256:384], start=False, stop=True,
                      skip_group_check=True).then_inc(s_osb, 1)
            gate_piece(12)
            gate_piece(13)
            pe.wait_ge(s_atT, h + 1)

            def v_da(m):
                return proj[:, R_VDA, bass.ds(h, 1), m, :].rearrange("p h d -> p (h d)")

            pe.matmul(ps[:, 7, 0:128], attnT[:, 0:P], v_da(0), start=True, stop=True)
            pe.matmul(ps[:, 7, 128:256], attnT[:, P:2 * P], v_da(0), start=True, stop=True,
                      skip_group_check=True)
            pe.matmul(ps[:, 7, 128:256], attnT[:, 2 * P:3 * P], v_da(1), start=False, stop=True,
                      skip_group_check=True).then_inc(s_oda, 1)
            for p in range(14, 16):
                gate_piece(p)
            if not last:
                turn_sb(h + 1)
                pe.wait_ge(s_ge, h + 2)
                gate_piece(0, (par + 1) % 2, i + (par + 1) // 2)
                turn_da(h + 1)
                gate_piece(1, (par + 1) % 2, i + (par + 1) // 2)
                turn_o(h)

        def turn_o(h):
            pe.wait_ge(s_oN, h + 1)
            for m in range(TB):
                mm = pe.transpose(ps[:, 5, m * P:(m + 1) * P], oN[:, m, :], ident)
            mm.then_inc(s_oT, 1)

        pe.wait_ge(s_fd, 2 + TILES_A - 1)
        pe.wait_ge(s_fa, 2 + TILES_A - 1)
        piece(TILES_A, 0, 0, (0, 1), True, False)
        piece(TILES_A, 1, 1, (0, 1), False, False)
        pe.wait_ge(s_fd, 2 + TILES_A)
        pe.wait_ge(s_fa, 2 + TILES_A)
        pe.wait_ge(s_set, 2)
        turn_sb(0)
        turn_da(0)
        with pe.Fori(0, H // 2 - 1) as i:
            head(i, 0)
            head(i, 1)
        head(H // 2 - 1, 0)
        head(H // 2 - 1, 1, last=True)

        pe.wait_ge(s_ge, H + 2)
        for t in range(2):
            for c in range(PT):
                if t == 0 and c % 4 == 0:
                    pe.wait_ge(s_xl, 8 + c // 4 + 1)
                if t == 0 and c == 4:
                    turn_o(H - 1)
                if t == 0 and c == 16:
                    pe.wait_ge(s_odt, H + 1)
                if t == 1 and c == 0:
                    pe.wait_ge(s_At, 1)
                if t == 1 and c == 16:
                    pe.wait_ge(s_Bt, 1)
                bank = 4 * (c // 16) + c % 2
                piece(10 + t, c, c // 2, (bank, bank + 2), c % 16 < 2, c % 16 >= 14)
                if t == 1 and c == 20:
                    pe.wait_ge(s_At, 2)
                if t == 1 and 20 <= c < 28 and c % 2 == 0:
                    turn_rows(merged, (c - 20) // 2, (c - 20) // 2)
        def turn_x2(j, bank):
            for k in range(2):
                for m in range(TB):
                    c = 2 * j + k
                    mm = pe.transpose(ps[:, bank, (2 * k + m) * P:(2 * k + m + 1) * P],
                                      xr[:, m, c * P:(c + 1) * P], ident)
            mm.then_inc(s_x2t, 1)

        def logits(c0, c1):
            for c in range(c0, c1):
                g = c % 2
                mm = pe.matmul(ps[RC * g:RC * g + RC, 3, 0:T], wr[:, c, :], x2T[:, c, :],
                               start=(c < 2), stop=(c >= KC - 2), skip_group_check=True)
            mm.then_inc(s_acc, 1)

        for t in range(2):
            for c in range(PT):
                if t == 0 and c % 4 == 0:
                    pe.wait_ge(s_xl, 16 + max(c // 4 + 1, 4))
                if t == 0 and c in (8, 10, 12, 14):
                    j = 4 + (c - 8) // 2
                    if j == 4:
                        pe.wait_ge(s_Bt, 2)
                    turn_rows(merged, j, j)
                if t == 1 and c == 6:
                    pe.wait_ge(s_x2, 4)
                    for j in range(4):
                        turn_x2(j, j)
                if t == 1 and c == 14:
                    pe.wait_ge(s_2d, 2)
                    pe.wait_ge(s_2a, 2)
                    logits(0, 8)
                if t == 1 and c == 22:
                    pe.wait_ge(s_x2, 6)
                    turn_x2(4, 0)
                    turn_x2(5, 1)
                if t == 1 and c == 30:
                    pe.wait_ge(s_2d, 3)
                    pe.wait_ge(s_2a, 3)
                    logits(8, 12)
                if t == 0:
                    bank = c % 2
                    piece(12, c, c // 2, (bank, bank + 2), c < 2, c >= PT - 2)
                else:
                    bank = 4 + c // KC
                    piece(13, c, c % KC, (bank, bank + 2), c % KC == 0, c % KC == KC - 1)
        for m in range(TB):
            pe.wait_ge(s_x2, 7 + m)
            for j, bank in ((6, 2), (7, 4)):
                for k in range(2):
                    c = 2 * j + k
                    mm = pe.transpose(ps[:, bank, (2 * k + m) * P:(2 * k + m + 1) * P],
                                      xr[:, m, c * P:(c + 1) * P], ident)
                if m == 1:
                    mm.then_inc(s_x2t, 1)
        pe.wait_ge(s_2d, 4)
        pe.wait_ge(s_2a, 4)
        logits(12, 16)
        pe.wait_ge(s_accS, 1)
        for m in range(TB):
            mm = pe.matmul(ps[:, m, 0:G + E], accS[:, m * P:(m + 1) * P], cst[:, C_ST:], start=True, stop=True)
        mm.then_inc(s_log, 1)
        def keep_busy(times):
            for _ in range(times):
                pe.matmul(ps[:, 7, 0:2 * P], ident16[:], mask16[:].rearrange("p a b -> p (a b)"), start=True,
                          stop=True)

        keep_busy(KEEP_BUSY)
        pe.wait_ge(s_took, 1)
        both = took16[:].rearrange("p m e -> p (m e)")
        pe.matmul(ps[:, 2, 0:2 * E], prev16, both, start=True, stop=True)
        pe.matmul(ps[:, 2, E:2 * E], ones16, took16[:, 0, :], start=False, stop=True, skip_group_check=True)
        pe.matmul(ps[:, 2, 2 * E:3 * E], ones16, took16[:, 0, :], start=True, stop=True, skip_group_check=True)
        pe.matmul(ps[:, 2, 2 * E:3 * E], ones16, took16[:, 1, :], start=False, stop=True,
                  skip_group_check=True).then_inc(s_rank, 1)
        keep_busy(KEEP_BUSY // 2)
        pe.wait_ge(s_h2, 4)

        def step(it):
            def gather(b, ks=range(4)):
                for k in ks:
                    bank = 3 if b == 0 and k < 2 else 4 + b
                    for m in range(TB):
                        mm = pe.matmul(ps[:, bank, k * P:(k + 1) * P], h2[:, m, 4 * b + k, :], selG[:, m, :],
                                       start=(m == 0), stop=(m == 1), skip_group_check=True)
                mm.then_inc(s_gath, 1)

            def combine(k):
                if k % 2 == 0:
                    pe.wait_ge((s_yd, s_ya)[k // 2 % 2], 2 * it + (k // 4 + 2))
                if k >= 2:
                    pe.wait_ge(s_add, 8 * it + (k + 3))
                m, n = k % 2, k // 2
                pe.matmul(ps[:, 2 + m, :], selWT[:, m * P:(m + 1) * P], yS[:, n * 512:(n + 1) * 512],
                          start=True, stop=True).then_inc(s_comb, 1)

            pe.wait_ge(s_sel, it + 1)
            pe.wait_ge(s_yd, 2 * it + 1)
            pe.wait_ge(s_ya, 2 * it + 1)
            pe.wait_ge(s_add, 8 * it + 4)
            gather(0, range(0, 2))
            for j in range(16):
                if j in (0, 2, 8):
                    pe.wait_ge(s_xd, 3 * it + (1, 2, 0, 0, 3)[j // 2])
                elif j in (4, 12):
                    pe.wait_ge(s_xa, 2 * it + (j // 8 + 1))
                mlanded(pe, it, j)
                for c in range(2):
                    kc = 2 * (j // 2) + c
                    for e in range(QUAD):
                        mm = pe.matmul(ps[SLOTS * e:SLOTS * e + SLOTS, j % 2, :],
                                       xgT[:, kc, SLOTS * e:SLOTS * e + SLOTS],
                                       expert_words(it, j, e)[:, c * 512:(c + 1) * 512],
                                       start=(kc == 0), stop=(kc == KC - 1))
                mm.then_inc(s_used, 1)
                if j == 0:
                    gather(0, range(2, 4))
                if j in (1, 4, 8):
                    gather(j // 4 + 1)
            pe.wait_ge(s_shr, it + 1)
            for m in range(TB):
                mm = pe.transpose(ps[:, 2, m * P:(m + 1) * P], selW[:, m, :, :].rearrange("p e s -> p (e s)"),
                                  ident)
            mm.then_inc(s_swt, 1)
            pe.wait_ge(s_hS, it + 1)
            for f in range(4):
                mm = pe.transpose(ps[:, 0, f * P:(f + 1) * P], hidden[:, f * P:(f + 1) * P], ident)
            mm.then_inc(s_ht, 1)
            pe.wait_ge(s_hT, it + 1)
            pe.wait_ge(s_sw, it + 1)

            def down(j, c, bank, word, start, stop):
                for e in range(QUAD):
                    mm = pe.matmul(ps[SLOTS * e:SLOTS * e + SLOTS, bank, :],
                                   hT4[:, c * P + SLOTS * e:c * P + SLOTS * e + SLOTS],
                                   expert_words(it, j, e)[:, word:word + 512], start=start, stop=stop)
                return mm

            for c in range(4):
                mlanded(pe, it, 16 + c)
                for n in range(2):
                    mm = down(16 + c, c, 4 + n, n * 512, c == 0, c == 3)
                    if c == 3 and n == 0:
                        mm.then_inc(s_yn, 1)
                mm.then_inc(s_used, 1)
            for c in range(2):
                mlanded(pe, it, 20 + c)
                for n in range(2):
                    mm = down(20 + c, c, 6 + n, n * 512, c == 0, False)
                mm.then_inc(s_used, 1)
                combine(2 * c)
                combine(2 * c + 1)
            for n in range(2):
                for c in (2, 3):
                    if c == 2:
                        pe.wait_ge(halves[n], 16 * it + 16)
                    else:
                        mlanded(pe, it, 22 + n)
                    mm = down(22 + n, c, 6 + n, (c - 2) * 512, False, c == 3)
                mm.then_inc(s_used, 1)
                combine(4 + 2 * n)
                combine(5 + 2 * n)

        step(0)
        pe.wait_ge(s_steps, 2)
        n_steps = pe.value_load(steps_i[0:1, 0:1], min_val=NQ, max_val=NQ * (T // SLOTS))
        with pe.Fori(1, n_steps) as it:
            step(it)

    def rsqrt_dve(dve, link, dst, src, scale, n):
        dve.tensor_scalar(rv, src, scale, EPS, ALU.mult, ALU.add).then_inc(s_v, 1)
        dve.wait_ge(s_v, n)
        dve.wait_ge(s_y0, n)
        link(dve.tensor_tensor(rq, rv, ry, ALU.mult))
        link(dve.tensor_tensor(rq, rq, ry, ALU.mult))
        link(dve.tensor_scalar(rq, rq, -0.5, 1.5, ALU.mult, ALU.add))
        dve.tensor_tensor(dst, rq, ry, ALU.mult).then_inc(s_rs, 1)
        dve.wait_ge(s_rs, n)

    def rsqrt_act(act, link, n):
        act.wait_ge(s_v, n)
        link(act.activation(ry, rv, ACT.Ln))
        act.activation(ry, ry, ACT.Exp, scale=-0.5).then_inc(s_y0, 1)

    @block.vector
    def _(dve):
        ch = Chain(dve, s_dve)
        link = ch.link
        for s in (s_ost, s_yd):
            dve.sem_inc(s, 1)
        dve.sem_inc(s_add, 4)
        dve.memset(one_c, 1.0).then_inc(s_set, 1)

        def rest(i, c):
            dve.wait_ge(s_wh, i * PT + (c + 1))
            b = c % AHEAD
            dve.tensor_tensor(wL[b], piece_of_ring(c), wH[b].bitcast(F32), ALU.subtract).then_inc(s_wl, 1)

        def x_rest(n, src, j):
            dve.wait_ge(s_xh, n + 1)
            cols = slice(j * PIECE, (j + 1) * PIECE)
            return dve.tensor_tensor(split[:, SLOT + j * PIECE:SLOT + (j + 1) * PIECE], src,
                                     split[:, cols].bitcast(F32), ALU.subtract).then_inc(s_xl, 1)

        dve.wait_ge(s_gt, 1)
        dve.tensor_copy(gT[:, 0, :], ps[:, 3, 0:KC]).then_inc(s_gtT, 1)

        def h_rest(j):
            dve.wait_ge(s_gtT, 1)
            dve.wait_ge(s_xh, j + 1)
            for k in range(2):
                cols = slice(j * PIECE + k * T, j * PIECE + (k + 1) * T)
                ins = dve.scalar_tensor_tensor(split[:, SLOT + cols.start:SLOT + cols.stop],
                                               ps[:, 4 + j % 4, k * T:(k + 1) * T],
                                               gT[:, 0, 2 * j + k:2 * j + k + 1], split[:, cols].bitcast(F32),
                                               ALU.mult, ALU.subtract)
            ins.then_inc(s_xl, 1)

        def take_tile(t):
            dve.wait_ge(s_pu, t * PT + (PT + AHEAD))
            dve.tensor_scalar(proj[:, bass.ds(t, 1), :, 0, :].rearrange("p r h d -> p (r h) d"),
                              ps[:, bass.ds((t % 2) * 4, 2), :].rearrange("p b (h d) -> p (b h) d", d=P),
                              rs[:, 0:1], None, ALU.mult).then_inc(s_fd, 1)

        h_rest(0)
        h_rest(1)
        for c in range(PT + AHEAD):
            if 8 <= c < PT and c % 8 in (0, 2):
                h_rest(2 * (c // 8) + c % 8 // 2)
            rest(0, c)
            if c in (14, 28):
                k = (c - 14) // 14
                cols = slice(k * 1024, (k + 1) * 1024)
                dve.wait_ge(s_xk[2 * k], 16)
                dve.wait_ge(s_xk[2 * k + 1], 16)
                link(dve.tensor_tensor_reduce(squares[:, 1, cols], x0[:, 1, cols], x0[:, 1, cols], 1.0, 0.0,
                                              ALU.mult, ALU.add, (ssA, ssB)[k][:, 1:2]))
            if c == 31:
                dve.wait_ge(s_gt, 2)
                link(dve.tensor_copy(gT[:, 1, :], ps[:, 7, 0:KC]))
                dve.tensor_tensor(wr[:, :, 0:G + E], wr[:, :, 0:G + E],
                                  gT[:, 1, :].unsqueeze(2).to_broadcast([P, KC, G + E]), ALU.mult).then_inc(s_wr, 1)
        dve.wait_ge(s_ssq, 2)
        link(dve.tensor_tensor(ss, ssA, ssB, ALU.add))
        rsqrt_dve(dve, link, rs, ss, 1.0 / D, 1)
        dve.sem_inc(s_fd, 2)
        take_tile(0)
        with dve.Fori(1, TILES_A - 1) as t:
            for c in range(AHEAD, PT + AHEAD):
                rest(t, c)
            take_tile(t)
        cosB = cosH.unsqueeze(1).to_broadcast([P, H, 4, HD // 2])
        sinB = sinH.unsqueeze(1).to_broadcast([P, H, 4, HD // 2])

        def rope_steps(r):
            qk = at(B_P + r * 2048, 2048).rearrange("p (b s a f) -> p b s a f", b=H, s=4, a=2)
            lo, hi = qk[:, :, :, 0, :], qk[:, :, :, 1, :]
            return [(rope_u, hi, sinB, ALU.mult), (rope_v, lo, sinB, ALU.mult), (lo, lo, cosB, ALU.mult),
                    (hi, hi, cosB, ALU.mult), (lo, lo, rope_u, ALU.subtract), (hi, hi, rope_v, ALU.add)]

        dve.wait_ge(s_small, 16 * 8)
        for v in range(2):
            link(dve.tensor_tensor_reduce(lamv[:, 2 * v, :], lamv[:, 2 * v, :], lamv[:, 2 * v + 1, :], 1.0, 0.0,
                                          ALU.mult, ALU.add, lam4[:, v:v + 1]))
        dve.tensor_copy(lamE, lam4).then_inc(s_lam, 1)
        dve.wait_ge(s_lamE, 1)
        link(dve.tensor_tensor(neglam, lam4[:, 1:2], lam4[:, 0:1], ALU.subtract))
        link(dve.tensor_scalar(neglam, neglam, -LAM_INIT, None, ALU.add))
        dve.wait_ge(s_fa, 2 + TILES_A - 1)
        dve.wait_ge(s_fd, 2 + TILES_A - 1)
        rope = rope_steps(R_QDA) + rope_steps(R_KDA)
        for c in range(AHEAD, PT + AHEAD):
            rest(TILES_A - 1, c)
            if c % 2 == 1 and rope:
                step = rope.pop(0)
                ins = dve.tensor_tensor(*step)
                if len(rope) in (0, 6):
                    ins.then_inc(s_roped, 1)
                else:
                    link(ins)
        take_tile(TILES_A - 1)

        def head(i, par, last=0):
            h = 2 * i + par
            dve.wait_ge(s_tsb, h + 2)
            link(dve.tensor_scalar(qkT_sb[:, 0, :], ps[:, 4, 0:256], float(P) ** -0.5, None, ALU.mult))
            dve.tensor_copy(qkT_sb[:, 1, :], ps[:, 4, 256:512]).then_inc(s_kd, 1)
            for p in range(4, 20 - last):
                rest(i + TILES_A, 16 * par + p)
                if p == 8:
                    dve.wait_ge(s_sc, h + 1)
                    link(dve.tensor_reduce(mx[:, 0:2], ps[:, 5:7, 0:128], AX.X, ALU.max))
                    link(dve.tensor_reduce(mx[:, 2:4], ps[:, 5:7, 128:384], AX.X, ALU.max))
                    dve.tensor_scalar(nmx, mx, -1.0, None, ALU.mult).then_inc(s_mx, 1)
                if p == 9:
                    dve.wait_ge(s_l, h + 1)
                    dve.scalar_tensor_tensor(eS, zS, 0.0, lS, ALU.max, ALU.add).then_inc(s_L, 1)
                if p == 11:
                    dve.wait_ge(s_p, h + 1)
                    link(dve.reciprocal(rsm, sm))
                    rsm2 = rsm.rearrange("p (q a) -> p q a", a=2)
                    link(dve.tensor_scalar(rsn.rearrange("p (q a) -> p q a", a=1), rsm2[:, :, 1:2], neglam, None,
                                           ALU.mult))
                    for q, cols in enumerate((slice(0, 128), slice(128, 384))):
                        link(dve.tensor_scalar(attn[:, cols], pS[:, 0, cols], rsm[:, 2 * q:2 * q + 1], None,
                                               ALU.mult))
                    link(dve.scalar_tensor_tensor(attn[:, 0:128], pS[:, 1, 0:128], rsn[:, 0:1], attn[:, 0:128],
                                                  ALU.mult, ALU.add))
                    dve.scalar_tensor_tensor(attn[:, 128:384], pS[:, 1, 128:384], rsn[:, 1:2],
                                             attn[:, 128:384], ALU.mult, ALU.add).then_inc(s_at, 1)
                if p == 12:
                    dve.wait_ge(s_c, h + 1)
                    dve.tensor_tensor(zS, zS, ps[:, 4, 0:384], ALU.subtract).then_inc(s_zc, 1)
                if p == 15:
                    dve.wait_ge(s_att, h + 1)
                    dve.tensor_copy(attnT, ps[:, 7, 0:384]).then_inc(s_atT, 1)
                if p == 16:
                    dve.wait_ge(s_osb, h + 2)
                    dve.tensor_copy(oT[:, bass.ds(h, 1), :].rearrange("p h t -> p (h t)"),
                                    ps[:, 4, 0:256]).then_inc(s_ost, 1)
                if p == 18:
                    dve.wait_ge(s_oS, h + 2)
                    for m in range(TB):
                        link(dve.tensor_tensor_reduce(sq, oS[:, m, :], oS[:, m, :], 1.0, 0.0, ALU.mult,
                                                      ALU.add, oss[:, m:m + 1]))
                    dve.tensor_scalar(rv, oss, 1.0 / P, EPS, ALU.mult, ALU.add).then_inc(s_v, 1)

        def norm_o(h):
            root(h + 2, ors)
            link(dve.tensor_scalar(ors, ors, 1.0 - LAM_INIT, None, ALU.mult))
            link(dve.scalar_tensor_tensor(oN[:, 0, :], oS[:, 0, :], ors[:, 0:1], gsub, ALU.mult, ALU.mult))
            dve.scalar_tensor_tensor(oN[:, 1, :], oS[:, 1, :], ors[:, 1:2], gsub, ALU.mult,
                                     ALU.mult).then_inc(s_oN, 1)

        def root(n, dst):
            dve.wait_ge(s_v, n)
            dve.wait_ge(s_y0, n)
            link(dve.tensor_tensor(rq, rv, ry, ALU.mult))
            link(dve.tensor_tensor(rq, rq, ry, ALU.mult))
            link(dve.tensor_scalar(rq, rq, -0.5, 1.5, ALU.mult, ALU.add))
            dve.tensor_tensor(dst, rq, ry, ALU.mult).then_inc(s_rs, 1)
            dve.wait_ge(s_rs, n)

        n0, per = ch.n, 2 * 15
        with dve.Fori(0, H // 2 - 1) as i:
            ch.off = i * per
            for par in range(2):
                head(i, par)
                norm_o(2 * i + par)
        assert ch.n - n0 == per, ch.n - n0
        ch.n, ch.off = n0 + per * (H // 2 - 1), 0
        head(H // 2 - 1, 0)
        norm_o(H - 2)
        head(H // 2 - 1, 1, last=1)

        def gate(t, br, m):
            g = gates[:, :, 4 * br + 2 * t:4 * br + 2 * t + 2, m, :]
            return g.rearrange("p r h d -> p h r d")

        def branch(ap):
            return ap.rearrange("p (h r d) -> p h r d", h=2, r=4)

        def take_a(t, m):
            dve.wait_ge(s_pu, G_C + t * PT + 16 + AHEAD)
            dve.wait_ge(s_sig, 2 * t + 1)
            src = ps[:, 2 * m:2 * m + 2, :].rearrange("p b (r d) -> p b r d", r=4)
            ins = dve.tensor_tensor(branch(merged[:, m, t * 1024:(t + 1) * 1024]), src, gate(t, 0, m), ALU.mult)
            if m == 0:
                link(ins)
            else:
                ins.then_inc(s_At, 1)

        def take_b(t, m, step):
            if step == 0:
                dve.wait_ge(s_pu, G_C + (t + 1) * PT + AHEAD)
                dve.wait_ge(s_sig, 2 * t + 2)
                src = ps[:, 4 + 2 * m:6 + 2 * m, :].rearrange("p b (r d) -> p b r d", r=4)
                link(dve.tensor_tensor(branch(part), src, gate(t, 1, m), ALU.mult))
            else:
                mg = merged[:, m, t * 1024:(t + 1) * 1024]
                ins = dve.tensor_tensor(mg, mg, part, ALU.add)
                if m == 0:
                    link(ins)
                else:
                    ins.then_inc(s_Bt, 1)

        for j in range(2):
            x_rest(8 + j, oT[:, 2 * j:2 * j + 2, :].rearrange("p c t -> p (c t)"), j)
            if j == 0:
                rest(H // 2 - 1 + TILES_A, PT + AHEAD - 1)
        norm_o(H - 1)
        for t in range(2):
            for c in range(AHEAD, PT + AHEAD):
                rest(10 + t, c)
                if t == 0 and c % 2 == 0 and 2 <= c // 2 < 8:
                    j = c // 2
                    x_rest(8 + j, oT[:, 2 * j:2 * j + 2, :].rearrange("p c t -> p (c t)"), j)
                if c in (19, 21):
                    take_a(t, (c - 19) // 2)
                if t == 1 and 4 <= c < 12 and c % 2 == 0:
                    take_b(0, (c - 4) // 4, (c - 4) // 2 % 2)
                if t == 1 and 25 <= c < 33 and c % 2 == 1:
                    j = (c - 25) // 2
                    x_rest(16 + j, ps[:, j, :], j)
        def add_out(t, n, m):
            xs = xr[:, m, t * 1024 + n * 512:t * 1024 + (n + 1) * 512]
            dve.tensor_tensor(xs, xs, ps[:, 4 * t + 2 * m + n, :], ALU.add).then_inc(s_x2, 1)

        for t in range(2):
            for c in range(AHEAD, PT + (AHEAD if t == 0 else 0)):
                rest(12 + t, c)
                if t == 0 and 4 <= c < 8:
                    take_b(1, (c - 4) // 2, c % 2)
                if t == 0 and c == 8:
                    dve.wait_ge(s_Bt, 2)
                    dve.memset(cell[:, 40:41], 0.0).then_inc(s_gd, 1)
                if t == 0 and c in (12, 14, 16, 18):
                    j = 4 + (c - 12) // 2
                    x_rest(16 + j, ps[:, j, :], j)
                if t == 1 and 4 <= c < 8:
                    dve.wait_ge(s_xr, 16)
                    dve.wait_ge(s_pu, G_D + PT + AHEAD)
                    add_out(0, (c - 4) // 2, c % 2)
                if t == 1 and c in (20, 21):
                    dve.wait_ge(s_pu, G_D + PT + KC + AHEAD)
                    add_out(1, 0, c - 20)
                if t == 1 and c in (11, 13, 27):
                    j = {11: 0, 13: 2, 27: 4}[c]
                    bank = j % 4
                    dve.wait_ge(s_x2t, j + 1)
                    dve.tensor_copy(x2T[:, 2 * j:2 * j + 2, :].rearrange("p c t -> p (c t)"),
                                    ps[:, bank, :]).then_inc(s_2d, 1)
        dve.wait_ge(s_pu, G_D + 2 * PT + AHEAD)
        for m in range(TB):
            add_out(1, 1, m)
        dve.wait_ge(s_x2t, 7)
        dve.tensor_copy(x2T[:, 12:14, :].rearrange("p c t -> p (c t)"), ps[:, 2, :]).then_inc(s_2d, 1)
        dve.wait_ge(s_acc, 3)
        dve.tensor_copy(accS, ps[:, 3, 0:T]).then_inc(s_accS, 1)
        dve.wait_ge(s_sq2, 1)
        link(dve.tensor_tensor(ss, ssA, ssB, ALU.add))
        link(dve.tensor_tensor(ss, ss, ssC, ALU.add))
        dve.tensor_scalar(rv, ss, 1.0 / D, EPS, ALU.mult, ALU.add).then_inc(s_v, 1)
        link(dve.memset(lg[:, :, G:8], -3.0e38))
        def issue(ins):
            ch.n += 1
            ins.then_inc(s_dve, 1)

        def join():
            dve.wait_ge(s_dve, ch.n)

        rt4 = rt.rearrange("p (a m) -> p a m", m=TB)
        neg_gm, gsum, pg = rt4[:, 0, :], rt4[:, 1, :], rt4[:, 2, :]
        gap, dexp, base, w1, w2, e1, e2 = (rt4[:, 3 + i, :] for i in range(7))
        iota_g = cst[:, C_IOTA:C_IOTA + G]
        iota_e = cst[:, C_IOTA:C_IOTA + E]

        def col(a):
            return a.unsqueeze(2)

        def over(a, n):
            return a.unsqueeze(2).to_broadcast([P, TB, n])

        def both(a, n):
            return a.unsqueeze(1).to_broadcast([P, TB, n])

        dve.wait_ge(s_log, 1)
        issue(dve.tensor_copy(lg[:, :, 0:G], ps[:, 0:TB, 0:G]))
        issue(dve.tensor_copy(lg[:, :, 8:8 + E], ps[:, 0:TB, G:G + E]))
        join()
        for m in range(TB):
            issue(dve.max(gm8[:, m, :], lg[:, m, 0:8]))
        dve.wait_ge(s_v, H + 2)
        dve.wait_ge(s_y0, H + 2)
        issue(dve.tensor_tensor(rq, rv, ry, ALU.mult))
        join()
        for m in range(TB):
            issue(dve.max_index(gi8[:, m, :], gm8[:, m, :], lg[:, m, 0:8]))
        issue(dve.tensor_tensor(rq, rq, ry, ALU.mult))
        join()
        issue(dve.tensor_copy(gi8f, gi8))
        issue(dve.tensor_scalar(rq, rq, -0.5, 1.5, ALU.mult, ALU.add))
        join()
        dve.tensor_tensor(rs, rq, ry, ALU.mult).then_inc(s_rs, 1)
        issue(dve.tensor_tensor(goh, both(iota_g, G), gi8f[:, :, 0:1].to_broadcast([P, TB, G]), ALU.is_equal))
        issue(dve.tensor_scalar(col(base), gi8f[:, :, 0:1], float(EPG), None, ALU.mult))
        join()
        for m in range(TB):
            issue(dve.tensor_tensor(picked[:, m, :].rearrange("p (g j) -> p g j", g=G),
                                    lg[:, m, 8:8 + E].rearrange("p (g j) -> p g j", g=G),
                                    goh[:, m, :].unsqueeze(2).to_broadcast([P, G, EPG]), ALU.mult))
        join()
        link(dve.tensor_reduce(esel, picked.rearrange("p m (g j) -> p m j g", g=G), AX.X, ALU.add))
        for m in range(TB):
            issue(dve.max(ev8[:, m, :], esel[:, m, :]))
        join()
        for m in range(TB):
            issue(dve.max_index(ei8[:, m, :], ev8[:, m, :], esel[:, m, :]))
        issue(dve.tensor_tensor(col(gap), ev8[:, :, 1:2], ev8[:, :, 0:1], ALU.subtract))
        join()
        link(dve.tensor_copy(ei8f, ei8))
        issue(dve.tensor_tensor(col(e1), col(base), ei8f[:, :, 0:1], ALU.add))
        issue(dve.tensor_tensor(col(e2), col(base), ei8f[:, :, 1:2], ALU.add))
        join()
        issue(dve.tensor_tensor(oh1, both(iota_e, E), over(e1, E), ALU.is_equal))
        issue(dve.tensor_tensor(oh2, both(iota_e, E), over(e2, E), ALU.is_equal))
        join()
        dve.tensor_tensor(took16[:], oh1, oh2, ALU.add).then_inc(s_took, 1)
        dve.wait_ge(s_rank, 1)
        link(dve.tensor_scalar(rank, ps[:, 2, 0:2 * E].rearrange("p (m e) -> p m e", m=TB), 4096.0, None, ALU.add))
        dve.wait_ge(s_took, 1)
        link(dve.tensor_tensor(rank, rank, took16[:], ALU.mult))
        link(dve.tensor_scalar(rank, rank, -4096.0, None, ALU.add))

        def exp_arguments():
            dve.wait_ge(s_rs, H + 2)
            issue(dve.scalar_tensor_tensor(col(neg_gm), gm8[:, :, 0:1], -1.0, col(rs), ALU.mult, ALU.mult))
            dve.tensor_tensor(gap, gap, rs, ALU.mult).then_inc(s_dd, 1)
            for m in range(TB):
                ins = dve.tensor_scalar(lg[:, m, 0:G], lg[:, m, 0:G], rs[:, m:m + 1], None, ALU.mult)
                issue(ins) if m == 0 else ins.then_inc(s_gm, 1)

        def shares():
            dve.wait_ge(s_gx, 1)
            issue(dve.reciprocal(pg, gsum))
            dve.wait_ge(s_ex, 1)
            link(dve.tensor_scalar(w1, dexp, 1.0, None, ALU.add))
            link(dve.reciprocal(w1, w1))
            link(dve.tensor_tensor(w1, w1, pg, ALU.mult))
            link(dve.tensor_tensor(w2, w1, dexp, ALU.mult))
            issue(dve.tensor_tensor(oh1, oh1, over(w1, E), ALU.mult))
            issue(dve.tensor_tensor(oh2, oh2, over(w2, E), ALU.mult))
            join()
            link(dve.tensor_tensor(share, oh1, oh2, ALU.add))

        def steps():
            link(dve.tensor_reduce(w1[:, 0:1], ps[:, 2, 2 * E:3 * E], AX.X, ALU.max))
            link(dve.tensor_scalar(count8, cst[:, C_THR:C_THR + 8], w1[:, 0:1], None, ALU.is_lt))
            link(dve.tensor_reduce(w1[:, 1:2], count8, AX.X, ALU.add))
            for k in range(2):
                dve.tensor_scalar(steps_i[:, k:k + 1], w1[:, 1:2], float(NQ), float(NQ - k), ALU.mult,
                                  ALU.add).then_inc(s_steps, 1)
            dve.wait_ge(s_steps, 2)

        def squares_1(cols, sums):
            link(dve.tensor_tensor_reduce(outS[:, 1, 1024:1024 + cols.stop - cols.start], xr[:, 1, cols],
                                          xr[:, 1, cols], 1.0, 0.0, ALU.mult, ALU.add, sums[:, 1:2]))

        def step(it, final=False):
            q = it % NQ
            rk = rank[:, :, bass.ds(q * QUAD, QUAD)]
            for m in range(TB):
                ins = dve.tensor_tensor(selE[:, m], iota_e.unsqueeze(1).to_broadcast([P, QUAD, SLOTS]),
                                        rk[:, m, :].unsqueeze(2).to_broadcast([P, QUAD, SLOTS]), ALU.is_equal)
                if m == 1:
                    link(ins)
            dve.wait_ge(s_rs, H + 2)
            for m in range(TB):
                ins = dve.tensor_scalar(selG[:, m, :], selE[:, m].rearrange("p e s -> p (e s)"), rs[:, m:m + 1],
                                        None, ALU.mult)
            ins.then_inc(s_sel, 1)

            def take_gathered(n, c0, c1, bank):
                dve.wait_ge(s_gath, 5 * it + n)
                dve.tensor_copy(xgT[:, c0:c1, :].rearrange("p c s -> p (c s)"),
                                ps[:, bank, c0 % 4 * P:(c0 % 4 + c1 - c0) * P]).then_inc(s_xd, 1)

            if isinstance(it, int):
                exp_arguments()
            take_gathered(1, 0, 2, 3)
            if isinstance(it, int):
                steps()
            take_gathered(2, 2, 4, 4)
            if isinstance(it, int):
                shares()
            for m in range(TB):
                ins = dve.tensor_tensor(selW[:, m], selE[:, m],
                                        share[:, m, bass.ds(q * QUAD, QUAD)].unsqueeze(2).to_broadcast(
                                            [P, QUAD, SLOTS]), ALU.mult)
            ins.then_inc(s_shr, 1)
            link(dve.tensor_scalar(rk, rk, -float(SLOTS), None, ALU.add))
            take_gathered(4, 8, 12, 6)
            dve.wait_ge(s_swt, it + 1)
            dve.tensor_copy(selWT, ps[:, 2, 0:T]).then_inc(s_sw, 1)
            dve.wait_ge(s_e, it + 1)
            dve.tensor_tensor(hidden, hidden, ps[:, 1, :], ALU.mult).then_inc(s_hS, 1)
            for nh in range(2):
                if nh == 0:
                    dve.wait_ge(s_yn, it + 1)
                else:
                    dve.wait_ge(s_used, it * QCH + (MRING + 23))
                dve.tensor_copy(yS[:, nh * 1024:nh * 1024 + 512], ps[:, 4 + 2 * nh, :]).then_inc(s_yd, 1)
                for n in range(2):
                    for m in range(TB):
                        k = 4 * nh + 2 * n + m
                        dve.wait_ge(s_comb, it * 8 + (k + 1))
                        cols = slice((2 * nh + n) * 512, (2 * nh + n + 1) * 512)
                        dve.tensor_tensor(xr[:, m, cols], xr[:, m, cols], ps[:, 2 + m, :],
                                          ALU.add).then_inc(s_add, 1)
                    if final and (nh, n) != (0, 0):
                        dve.wait_ge(s_add, 8 * it + (4 + 4 * nh + 2 * n + 2))
                        squares_1(*((slice(0, 1024), ssA), (slice(1024, 1536), ssC),
                                    (slice(1536, 2048), ssB))[2 * nh + n - 1])

        step(0)
        last = dve.value_load(steps_i[0:1, 1:2], min_val=NQ - 1, max_val=NQ * (T // SLOTS) - 1)
        n0 = ch.n
        per_step = 2
        with dve.Fori(1, last) as it:
            ch.off = (it - 1) * per_step
            step(it)
        assert ch.n - n0 == per_step, ch.n - n0
        ch.n, ch.off = n0, last * per_step - per_step
        step(last, final=True)
        dve.wait_ge(s_fss, 1)
        link(dve.tensor_tensor(ss, ssA, ssC, ALU.add))
        link(dve.tensor_tensor(ss, ss, ssB, ALU.add))
        rsqrt_dve(dve, link, rs, ss, 1.0 / D, H + 3)
        dve.wait_ge(s_gain, 32)
        for m in range(TB):
            dve.scalar_tensor_tensor(outS[:, m, 1024:], xr[:, m, 1024:], rs[:, m:m + 1], gain[:, 1024:], ALU.mult,
                                     ALU.mult).then_inc(s_out[1], 1)

    @block.scalar
    def _(act):
        ch = Chain(act, s_act)
        link = ch.link
        for s in (s_odt, s_oS, s_ya):
            act.sem_inc(s, 1)
        for s in (s_ge, s_fa):
            act.sem_inc(s, 2)

        def rounded(i, c):
            if isinstance(i, int) and i == 0 and c < 8:
                if c % 2 == 0:
                    act.wait_ge(s_part[c // 2] if c < 6 else landed[0], 16)
            elif c % 8 == 0:
                act.wait_ge(landed[(c // 8) % DRING], i * 16 + 16 * (c // PT + 1))
            act.wait_ge(s_pu, i * PT + (c + 1))
            act.copy(wH[c % AHEAD], piece_of_ring(c)).then_inc(s_wh, 1)

        def x_rounded(src, j):
            act.copy(split[:, j * PIECE:(j + 1) * PIECE], src).then_inc(s_xh, 1)

        act.preload_act_table_set(LN_EXP)

        def h_rounded(j):
            act.wait_ge(s_turned, j + 1)
            for k in range(2):
                ins = act.activation(split[:, j * PIECE + k * T:j * PIECE + (k + 1) * T],
                                     ps[:, 4 + j % 4, k * T:(k + 1) * T], ACT.Copy,
                                     scale=gT[:, 0, 2 * j + k:2 * j + k + 1])
            ins.then_inc(s_xh, 1)

        def take_tile(t):
            act.wait_ge(s_pu, t * PT + (PT + AHEAD))
            act.activation(proj[:, bass.ds(t, 1), :, 1, :].rearrange("p r h d -> p (r h) d"),
                           ps[:, bass.ds((t % 2) * 4 + 2, 2), :].rearrange("p b (h d) -> p (b h) d", d=P),
                           ACT.Copy, scale=rs[:, 1:2]).then_inc(s_fa, 1)

        act.wait_ge(s_gtT, 1)
        h_rounded(0)
        h_rounded(1)
        for c in range(PT + AHEAD):
            if 8 <= c < PT and c % 8 in (0, 2):
                h_rounded(2 * (c // 8) + c % 8 // 2)
            rounded(0, c)
            if c in (14, 28):
                k = (c - 14) // 14
                cols = slice(k * 1024, (k + 1) * 1024)
                act.wait_ge(s_xk[2 * k], 16)
                act.wait_ge(s_xk[2 * k + 1], 16)
                act.activation(squares[:, 0, cols], x0[:, 0, cols], ACT.Square,
                               accum_out=(ssA, ssB)[k][:, 0:1]).then_inc(s_ssq, 1)
        rsqrt_act(act, link, 1)
        act.wait_ge(s_rs, 1)
        take_tile(0)
        with act.Fori(1, TILES_A - 1) as t:
            for c in range(AHEAD, PT + AHEAD):
                rounded(t, c)
            take_tile(t)
        act.wait_ge(s_lam, 1)
        act.activation(lam4, lamE, ACT.Exp).then_inc(s_lamE, 1)
        for c in range(AHEAD, PT + AHEAD):
            rounded(TILES_A - 1, c)
        take_tile(TILES_A - 1)
        act.wait_ge(s_set, 2)

        act.preload_act_table_set(LN_EXP)
        def head(i, par, last=0):
            h = 2 * i + par
            act.wait_ge(s_tda, h + 2)
            link(act.activation(qkT_da[:, 0, :], ps[:, 7, 0:256], ACT.Copy, scale=float(HD) ** -0.5))
            act.copy(qkT_da[:, 1, :], ps[:, 7, 256:512]).then_inc(s_ka, 1)
            for p in range(4, 20 - last):
                rounded(i + TILES_A, 16 * par + p)
                if p == 7:
                    act.wait_ge(s_z, h + 1)
                    link(act.copy(zS, ps[:, 4, 0:384]))
                    link(act.activation(lS, ps[:, 4, 0:384], ACT.Abs))
                    link(act.activation(lS, lS, ACT.Exp, scale=-1.0))
                    act.activation(lS, lS, ACT.Ln, bias=one_c).then_inc(s_l, 1)
                if p == 9:
                    act.wait_ge(s_mx, h + 1)
                    for q, cols in enumerate((slice(0, 128), slice(128, 384))):
                        for mp in range(2):
                            k = 2 * q + mp
                            ins = act.activation(pS[:, mp, cols], ps[:, 5 + mp, cols], ACT.Exp,
                                                 bias=nmx[:, k:k + 1], accum_out=sm[:, k:k + 1])
                    ins.then_inc(s_p, 1)
                if p == 13:
                    act.wait_ge(s_zc, h + 1)
                    act.activation(aT, zS, ACT.Exp).then_inc(s_a, 1)
                if p == 17:
                    act.wait_ge(s_oda, h + 1)
                    act.copy(oS.rearrange("p m d -> p (m d)"), ps[:, 7, 0:256]).then_inc(s_oS, 1)

        def take_gate(i, par):
            h = 2 * i + par
            act.wait_ge(s_pu, h * KC + (G_B + KC + AHEAD))
            for m in range(TB):
                ins = act.activation(gates[:, :, bass.ds(h, 1), m, :].rearrange("p r h d -> p (r h) d"),
                                     ps[:, 2 * par + m, :].rearrange("p (r d) -> p r d", r=4), ACT.Copy,
                                     scale=rs[:, m:m + 1])
            ins.then_inc(s_ge, 1)

        def take_o(h):
            act.wait_ge(s_oT, h + 1)
            act.copy(oT[:, bass.ds(h + H, 1), :].rearrange("p h t -> p (h t)"),
                     ps[:, 5, 0:256]).then_inc(s_odt, 1)

        n0, per = ch.n, 2 * 5
        with act.Fori(0, H // 2 - 1) as i:
            ch.off = i * per
            for par in range(2):
                head(i, par)
                rsqrt_act(act, link, 2 * i + par + 2)
                take_gate(i, par)
                take_o(2 * i + par)
        assert ch.n - n0 == per, ch.n - n0
        ch.n, ch.off = n0 + per * (H // 2 - 1), 0
        head(H // 2 - 1, 0)
        rsqrt_act(act, link, H)
        take_gate(H // 2 - 1, 0)
        take_o(H - 2)
        head(H // 2 - 1, 1, last=1)


        def o_part(j):
            return oT[:, 2 * j:2 * j + 2, :].rearrange("p c t -> p (c t)")

        act.wait_ge(s_ost, H + 1)
        act.wait_ge(s_pu, G_C + AHEAD)
        x_rounded(o_part(0), 0)
        take_gate(H // 2 - 1, 1)
        rounded(H // 2 - 1 + TILES_A, PT + AHEAD - 1)
        x_rounded(o_part(1), 1)
        rsqrt_act(act, link, H + 1)
        act.preload_act_table(ACT.Sigmoid)
        for t in range(2):
            for c in range(AHEAD, PT + AHEAD):
                rounded(10 + t, c)
                if t == 0 and c == 11:
                    take_o(H - 1)
                    act.wait_ge(s_odt, H + 1)
                    act.wait_ge(s_ge, H + 2)
                if t == 0 and c % 2 == 0 and 2 <= c // 2 < 8:
                    x_rounded(o_part(c // 2), c // 2)
                if (t, c) in ((0, 12), (0, 24), (1, 8), (1, 20)):
                    n = ((0, 12), (0, 24), (1, 8), (1, 20)).index((t, c))
                    tt, br = n // 2, n % 2
                    gt = gates[:, :, 4 * br + 2 * tt:4 * br + 2 * tt + 2, :, :].rearrange("p r h m d -> p r (h m d)")
                    act.activation(gt, gt, ACT.Sigmoid).then_inc(s_sig, 1)
                if t == 1 and 25 <= c < 33 and c % 2 == 1:
                    j = (c - 25) // 2
                    act.wait_ge(s_turned, 8 + j + 1)
                    act.wait_ge(s_pu, G_C + PT + 16 + AHEAD)
                    x_rounded(ps[:, j, :], j)
        def squares_of(cols, sums):
            for m in range(TB):
                ins = act.activation(outJ[:, m, 0:cols.stop - cols.start], xr[:, m, cols], ACT.Square,
                                     accum_out=sums[:, m:m + 1])
            return ins

        for t in range(2):
            for c in range(AHEAD, PT + (AHEAD if t == 0 else 0)):
                rounded(12 + t, c)
                if t == 0 and c == 24:
                    act.preload_act_table_set(LN_EXP)
                if t == 0 and c in (12, 14, 16, 18):
                    j = 4 + (c - 12) // 2
                    act.wait_ge(s_turned, 8 + j + 1)
                    x_rounded(ps[:, j, :], j)
                if t == 1 and c in (12, 14, 28):
                    j = {12: 1, 14: 3, 28: 5}[c]
                    bank = j % 4
                    act.wait_ge(s_x2t, j + 1)
                    act.copy(x2T[:, 2 * j:2 * j + 2, :].rearrange("p c t -> p (c t)"),
                             ps[:, bank, :]).then_inc(s_2a, 1)
                if t == 1 and c == 18:
                    squares_of(slice(0, 1024), ssA)
                if t == 1 and c == 30:
                    squares_of(slice(1024, 1536), ssB)
        act.wait_ge(s_x2t, 8)
        act.copy(x2T[:, 14:16, :].rearrange("p c t -> p (c t)"), ps[:, 4, :]).then_inc(s_2a, 1)
        squares_of(slice(1536, 2048), ssC).then_inc(s_sq2, 1)
        rsqrt_act(act, link, H + 2)
        rt4 = rt.rearrange("p (a m) -> p a m", m=TB)
        act.wait_ge(s_dd, 1)
        act.activation(rt4[:, 4, :], rt4[:, 3, :], ACT.Exp).then_inc(s_ex, 1)
        act.wait_ge(s_gm, 1)
        for m in range(TB):
            ins = act.activation(gexp[:, m, :], lg[:, m, 0:G], ACT.Exp, bias=rt4[:, 0, m:m + 1],
                                 accum_out=rt4[:, 1, m:m + 1])
        ins.then_inc(s_gx, 1)
        act.preload_act_table(ACT.Silu)

        def step(it, final=False):
            for b in (1, 3):
                act.wait_ge(s_gath, 5 * it + (b + 2))
                act.copy(xgT[:, 4 * b:4 * b + 4, :].rearrange("p c s -> p (c s)"),
                         ps[:, 4 + b, :]).then_inc(s_xa, 1)
            act.wait_ge(s_used, it * QCH + (MRING + 16))
            act.activation(hidden, ps[:, 0, :], ACT.Silu).then_inc(s_e, 1)
            act.wait_ge(s_ht, it + 1)
            act.copy(hT4, ps[:, 0, :]).then_inc(s_hT, 1)
            for nh in range(2):
                act.wait_ge(s_used, it * QCH + (MRING + 20 + 4 * nh))
                act.copy(yS[:, nh * 1024 + 512:nh * 1024 + 1024], ps[:, 5 + 2 * nh, :]).then_inc(s_ya, 1)
                if final and nh == 0:
                    act.preload_act_table_set(LN_EXP)
                    act.wait_ge(s_add, 8 * it + 8)
                    act.activation(outS[:, 0, 1024:], xr[:, 0, 0:1024], ACT.Square, accum_out=ssA[:, 0:1])
                    act.wait_ge(s_add, 8 * it + 10)
                    act.activation(xgJ[:, 0, 0:512], xr[:, 0, 1024:1536], ACT.Square, accum_out=ssC[:, 0:1])

        step(0)
        act.wait_ge(s_steps, 2)
        last = act.value_load(steps_i[0:1, 1:2], min_val=NQ - 1, max_val=NQ * (T // SLOTS) - 1)
        with act.Fori(1, last) as it:
            step(it)
        step(last, final=True)
        act.wait_ge(s_add, last * 8 + 12)
        act.activation(xgJ[:, 1, 0:512], xr[:, 0, 1536:], ACT.Square, accum_out=ssB[:, 0:1]).then_inc(s_fss, 1)
        rsqrt_act(act, link, H + 3)
        act.wait_ge(s_rs, H + 3)
        act.wait_ge(s_xg, 2)
        for m in range(TB):
            act.activation(outS[:, m, 0:1024], outS[:, m, 0:1024], ACT.Copy, scale=rs[:, m:m + 1]).then_inc(
                s_out[0], 1)

    ctx.close()


_INS = ["x", "mix_norm_g", "w_in", "lambda_q1", "lambda_k1", "lambda_q2", "lambda_k2", "diff_subnorm_g",
        "w_branch_sb", "w_branch_diff", "w_out", "ffn_norm_g", "w_group_router", "w_expert_router",
        "w_gate", "w_up", "w_down", "final_norm_g"]


def kernel(**inputs):
    import concourse.bacc as bacc
    from concourse.bass_utils import run_bass_kernel_spmd

    nc = bacc.Bacc("TRN2", target_bir_lowering=False, num_devices=1)
    arrays, args = {}, []
    for name in _INS:
        a = np.ascontiguousarray(inputs[name])
        arrays[f"in_{name}"] = a
        args.append(nc.dram_tensor(f"in_{name}", a.shape, mybir.dt.from_np(a.dtype), kind="ExternalInput").ap())
    c = shape_constants()
    arrays["shape_constants"] = c
    args.append(nc.dram_tensor("shape_constants", c.shape, F32, kind="ExternalInput").ap())
    out = nc.dram_tensor("out", inputs["x"].shape, F32, kind="ExternalOutput").ap()
    build(nc, *args, out)
    r = run_bass_kernel_spmd(nc, [arrays], core_ids=[0])
    return r.results[0]["out"]
```
